# Optimizing a Trainium2 kernel written in Bass

```python
import jax, jax.numpy as jnp
from jax import lax
import numpy as np

D_MODEL = 1024
BATCH = 1
SEQ = 1024
DEPTH = 2
DEC_BATCH = 8
DEC_SEQ = 8
PAST_LEN = 512
PAGE_SIZE = 128

N_EVEN = (DEPTH + 1) // 2
N_ODD = DEPTH // 2
N_HEADS = 8
HEAD_DIM = 64
N_KV_HEADS = 2
KV_GROUP = N_HEADS // N_KV_HEADS
D_ATTN = N_HEADS * HEAD_DIM
D_KV = N_KV_HEADS * HEAD_DIM
N_IDX_HEADS = 8
D_IDX = 64
TOPK_MAX = 256
Q_BLOCK = 128
ROPE_THETA = 10000.0
POOL_WINDOWS = (2, 4, 8, 16)
N_POOL_GROUPS = 4
D_POOL = D_MODEL // 2
D_POOL_GROUP = D_POOL // N_POOL_GROUPS
POOL_BUF = 15
D_IN_EVEN = D_ATTN + 2 * D_KV + N_IDX_HEADS * D_IDX + D_IDX + N_IDX_HEADS + D_POOL
D_OUT_EVEN = D_ATTN + D_POOL
D_SGU = D_MODEL
N_SGU_HEADS = 8
D_SGU_HEAD = D_SGU // N_SGU_HEADS
CHUNK = 128
D_FF = -(-8 * D_MODEL // (3 * 256)) * 256
EPS = 1e-6

kernel_name = 'hybrid_dsa_pool_gmlp_decode_step'

def _rmsnorm(x, g):
    x32 = x.astype(jnp.float32)
    y = x32 * lax.rsqrt(jnp.mean(x32 * x32, axis=-1, keepdims=True) + EPS)
    return (y * g.astype(jnp.float32)).astype(x.dtype)

def _layernorm(x, g, b):
    x32 = x.astype(jnp.float32)
    mu = jnp.mean(x32, axis=-1, keepdims=True)
    xc = x32 - mu
    y = xc * lax.rsqrt(jnp.mean(xc * xc, axis=-1, keepdims=True) + EPS)
    return (y * g.astype(jnp.float32) + b.astype(jnp.float32)).astype(x.dtype)

def _rope(x, pos):
    half = x.shape[-1] // 2
    inv = ROPE_THETA ** (-jnp.arange(half, dtype=jnp.float32) / half)
    ang = pos.astype(jnp.float32)[:, None] * inv[None, :]
    cos = jnp.cos(ang)[None, :, None, :]
    sin = jnp.sin(ang)[None, :, None, :]
    x32 = x.astype(jnp.float32)
    x1, x2 = x32[..., :half], x32[..., half:]
    return jnp.concatenate([x1 * cos - x2 * sin, x2 * cos + x1 * sin], axis=-1).astype(x.dtype)

def _dsa_block(q, iq, iw, qpos, k_all, v_all, ik_all, topk):
    b, n = q.shape[:2]
    L = k_all.shape[1]
    rel = jax.nn.relu(jnp.einsum('bnhd,bsd->bnhs', iq.astype(jnp.float32), ik_all.astype(jnp.float32)) * D_IDX ** -0.5)
    score = jnp.einsum('bnh,bnhs->bns', iw.astype(jnp.float32) * N_IDX_HEADS ** -0.5, rel)
    kpos = jnp.arange(L, dtype=jnp.int32)
    score = jnp.where((kpos[None, :] <= qpos[:, None])[None], score, -jnp.inf)
    _, sel = lax.top_k(score, topk)
    take = jax.vmap(lambda a, i: a[i])
    k_sel = take(k_all, sel)
    v_sel = take(v_all, sel)
    valid = sel <= qpos[None, :, None]
    qg = q.reshape(b, n, N_KV_HEADS, KV_GROUP, HEAD_DIM).astype(jnp.float32)
    logits = jnp.einsum('bnhgd,bnshd->bnhgs', qg, k_sel.astype(jnp.float32)) * HEAD_DIM ** -0.5
    logits = jnp.where(valid[:, :, None, None, :], logits, -jnp.inf)
    p = jax.nn.softmax(logits, axis=-1)
    o = jnp.einsum('bnhgs,bnshd->bnhgd', p, v_sel.astype(jnp.float32))
    return o.reshape(b, n, D_ATTN).astype(q.dtype)

def _dsa_attend(q, iq, iw, qpos, k_all, v_all, ik_all, topk):
    b, T = q.shape[:2]
    blk = min(Q_BLOCK, T)
    nb = T // blk

    def to_blocks(a):
        return jnp.moveaxis(a.reshape((b, nb, blk) + a.shape[2:]), 1, 0)

    out = lax.map(lambda args: _dsa_block(*args, k_all, v_all, ik_all, topk),
                  (to_blocks(q), to_blocks(iq), to_blocks(iw), qpos.reshape(nb, blk)))
    return jnp.moveaxis(out, 0, 1).reshape(b, T, D_ATTN)

def _pool_mix(xp, prefix, pos, w_pg, pool_scale):
    b, T, _ = xp.shape
    ext = jnp.concatenate([prefix.astype(xp.dtype), xp], axis=1).astype(jnp.float32)
    cs = jnp.concatenate([jnp.zeros((b, 1, D_POOL), jnp.float32), jnp.cumsum(ext, axis=1)], axis=1)
    groups = []
    for g, w in enumerate(POOL_WINDOWS):
        sl = slice(g * D_POOL_GROUP, (g + 1) * D_POOL_GROUP)
        win_sum = cs[:, POOL_BUF + 1:POOL_BUF + 1 + T, sl] - cs[:, POOL_BUF + 1 - w:POOL_BUF + 1 - w + T, sl]
        count = jnp.minimum(w, pos + 1).astype(jnp.float32)[None, :, None]
        groups.append(win_sum / count - ext[:, POOL_BUF:, sl])
    d = jnp.stack(groups, axis=2).astype(xp.dtype)
    y = jnp.einsum('btgc,gce->btge', d, w_pg).reshape(b, T, D_POOL) * pool_scale
    return y, ext[:, T:].astype(xp.dtype)

def _even_mixer(h, pos, topk, past, w_in, w_out, w_pg, pool_scale):
    b, T, _ = h.shape
    widths = [D_ATTN, D_KV, D_KV, N_IDX_HEADS * D_IDX, D_IDX, N_IDX_HEADS]
    cuts, acc = [], 0
    for wd in widths:
        acc += wd
        cuts.append(acc)
    q, k, v, iq, ik, iw, xp = jnp.split(h @ w_in, cuts, axis=-1)
    q = _rope(q.reshape(b, T, N_HEADS, HEAD_DIM), pos)
    k = _rope(k.reshape(b, T, N_KV_HEADS, HEAD_DIM), pos)
    v = v.reshape(b, T, N_KV_HEADS, HEAD_DIM)
    iq = _rope(iq.reshape(b, T, N_IDX_HEADS, D_IDX), pos)
    ik = _rope(ik.reshape(b, T, 1, D_IDX), pos)[:, :, 0]
    if past is None:
        k_all, v_all, ik_all = k, v, ik
        prefix = jnp.zeros((b, POOL_BUF, D_POOL), h.dtype)
    else:
        k_past, v_past, ik_past, prefix = past
        k_all = jnp.concatenate([k_past.astype(k.dtype), k], axis=1)
        v_all = jnp.concatenate([v_past.astype(v.dtype), v], axis=1)
        ik_all = jnp.concatenate([ik_past.astype(ik.dtype), ik], axis=1)
    attn = _dsa_attend(q, iq, iw, pos, k_all, v_all, ik_all, topk)
    pool, new_prefix = _pool_mix(xp, prefix, pos, w_pg, pool_scale)
    out = jnp.concatenate([attn, pool], axis=-1) @ w_out
    return out, k, v, ik, new_prefix

def _odd_mixer(h, w_in, ln_g, ln_b, w_s, b_s, w_out):
    b, T, _ = h.shape
    u, v = jnp.split(jax.nn.gelu(h @ w_in, approximate=False), 2, axis=-1)
    z = _layernorm(v, ln_g, ln_b)
    c = min(CHUNK, T)
    nc = T // c
    mask = jnp.tril(jnp.ones((c, c), dtype=bool))
    w_m = jnp.where(mask[None], w_s[:, :c, :c], 0.0)
    zc = z.reshape(b, nc, c, N_SGU_HEADS, D_SGU_HEAD)
    s = jnp.einsum('gts,bnsgd->bntgd', w_m, zc) + jnp.swapaxes(b_s[:, :c], 0, 1)[None, None, :, :, None]
    y = u * s.reshape(b, T, D_SGU)
    return y @ w_out, z

def _swiglu(h, w_gu, w_down):
    gate, up = jnp.split(h @ w_gu, 2, axis=-1)
    return (jax.nn.silu(gate) * up) @ w_down

def _gather_pages(pool, page_table):
    g = pool[page_table]
    return g.reshape((g.shape[0], g.shape[1] * g.shape[2]) + g.shape[3:])

def setup_inputs(seed: int = 0) -> dict:
    key = jax.random.key(seed)
    ks = jax.random.split(key, 32)
    f32 = jnp.float32
    n_pages = PAST_LEN // PAGE_SIZE
    n_pool = (DEC_BATCH * n_pages * 5) // 4

    def nrm(k, shape, scale=1.0):
        return scale * jax.random.normal(k, shape, f32)

    def gain(k, shape):
        return 1.0 + 0.05 * jax.random.normal(k, shape, f32)

    page_table = jax.random.permutation(ks[6], n_pool)[:DEC_BATCH * n_pages].reshape(DEC_BATCH, n_pages).astype(jnp.int32)
    return {
        'x_prompt': nrm(ks[0], (BATCH, SEQ, D_MODEL)),
        'x_sample': nrm(ks[1], (DEC_BATCH, DEC_SEQ, D_MODEL)),
        'cache_k': nrm(ks[2], (N_EVEN, n_pool, PAGE_SIZE, N_KV_HEADS, HEAD_DIM)),
        'cache_v': nrm(ks[3], (N_EVEN, n_pool, PAGE_SIZE, N_KV_HEADS, HEAD_DIM)),
        'cache_idx_k': nrm(ks[4], (N_EVEN, n_pool, PAGE_SIZE, D_IDX)),
        'state_pool': nrm(ks[5], (N_EVEN, DEC_BATCH, POOL_BUF, D_POOL)),
        'page_table': page_table,
        'norm_mix_pre': gain(ks[7], (DEPTH, D_MODEL)),
        'norm_mix_post': gain(ks[8], (DEPTH, D_MODEL)),
        'norm_ffn_pre': gain(ks[9], (DEPTH, D_MODEL)),
        'norm_ffn_post': gain(ks[10], (DEPTH, D_MODEL)),
        'w_in_even': nrm(ks[11], (N_EVEN, D_MODEL, D_IN_EVEN), D_MODEL ** -0.5),
        'w_out_even': nrm(ks[12], (N_EVEN, D_OUT_EVEN, D_MODEL), D_OUT_EVEN ** -0.5),
        'w_pool_group': nrm(ks[13], (N_EVEN, N_POOL_GROUPS, D_POOL_GROUP, D_POOL_GROUP), D_POOL_GROUP ** -0.5),
        'pool_scale': gain(ks[14], (N_EVEN, D_POOL)),
        'w_in_odd': nrm(ks[15], (N_ODD, D_MODEL, 2 * D_SGU), D_MODEL ** -0.5),
        'sgu_norm_g': gain(ks[16], (N_ODD, D_SGU)),
        'sgu_norm_b': nrm(ks[17], (N_ODD, D_SGU), 0.02),
        'w_spatial': nrm(ks[18], (N_ODD, N_SGU_HEADS, CHUNK, CHUNK), CHUNK ** -0.5),
        'b_spatial': gain(ks[19], (N_ODD, N_SGU_HEADS, CHUNK)),
        'w_out_odd': nrm(ks[20], (N_ODD, D_SGU, D_MODEL), D_SGU ** -0.5),
        'w_ffn_gate_up': nrm(ks[21], (DEPTH, D_MODEL, 2 * D_FF), D_MODEL ** -0.5),
        'w_ffn_down': nrm(ks[22], (DEPTH, D_FF, D_MODEL), D_FF ** -0.5),
    }

def reference(x_prompt, x_sample, cache_k, cache_v, cache_idx_k, state_pool, page_table,
              norm_mix_pre, norm_mix_post, norm_ffn_pre, norm_ffn_post,
              w_in_even, w_out_even, w_pool_group, pool_scale,
              w_in_odd, sgu_norm_g, sgu_norm_b, w_spatial, b_spatial, w_out_odd,
              w_ffn_gate_up, w_ffn_down):
    t_prompt = x_prompt.shape[1]
    t_sample = x_sample.shape[1]
    past_len = page_table.shape[1] * PAGE_SIZE
    pos_p = jnp.arange(t_prompt, dtype=jnp.int32)
    pos_s = past_len + jnp.arange(t_sample, dtype=jnp.int32)
    topk_p = min(TOPK_MAX, t_prompt // 4)
    topk_s = min(TOPK_MAX, (past_len + t_sample) // 4)

    hp, hs = x_prompt, x_sample
    nk_p, nv_p, nik_p, npool_p = [], [], [], []
    nk_s, nv_s, nik_s, npool_s, nsgu_s = [], [], [], [], []
    for layer in range(DEPTH):
        li = layer // 2
        ap = _rmsnorm(hp, norm_mix_pre[layer])
        as_ = _rmsnorm(hs, norm_mix_pre[layer])
        if layer % 2 == 0:
            mp, kp, vp, ikp, poolp = _even_mixer(ap, pos_p, topk_p, None,
                                                 w_in_even[li], w_out_even[li], w_pool_group[li], pool_scale[li])
            past = (_gather_pages(cache_k[li], page_table), _gather_pages(cache_v[li], page_table),
                    _gather_pages(cache_idx_k[li], page_table), state_pool[li])
            ms, ks_, vs, iks, pools = _even_mixer(as_, pos_s, topk_s, past,
                                                  w_in_even[li], w_out_even[li], w_pool_group[li], pool_scale[li])
            nk_p.append(kp); nv_p.append(vp); nik_p.append(ikp); npool_p.append(poolp)
            nk_s.append(ks_); nv_s.append(vs); nik_s.append(iks); npool_s.append(pools)
        else:
            mp, _ = _odd_mixer(ap, w_in_odd[li], sgu_norm_g[li], sgu_norm_b[li], w_spatial[li], b_spatial[li], w_out_odd[li])
            ms, zs = _odd_mixer(as_, w_in_odd[li], sgu_norm_g[li], sgu_norm_b[li], w_spatial[li], b_spatial[li], w_out_odd[li])
            nsgu_s.append(zs)
        hp = hp + _rmsnorm(mp, norm_mix_post[layer])
        hs = hs + _rmsnorm(ms, norm_mix_post[layer])
        hp = hp + _rmsnorm(_swiglu(_rmsnorm(hp, norm_ffn_pre[layer]), w_ffn_gate_up[layer], w_ffn_down[layer]), norm_ffn_post[layer])
        hs = hs + _rmsnorm(_swiglu(_rmsnorm(hs, norm_ffn_pre[layer]), w_ffn_gate_up[layer], w_ffn_down[layer]), norm_ffn_post[layer])

    return (hp, hs,
            jnp.stack(nk_p), jnp.stack(nv_p), jnp.stack(nik_p), jnp.stack(npool_p),
            jnp.stack(nk_s), jnp.stack(nv_s), jnp.stack(nik_s), jnp.stack(npool_s),
            jnp.stack(nsgu_s))


_drawn_inputs = setup_inputs


def setup_inputs(seed=0):
    import zlib

    import numpy as np

    out = dict(_drawn_inputs(seed))
    spreads = {}
    factors = {'sgu_norm_b': 2.881}
    for name, (base, spread) in spreads.items():
        noise = np.random.default_rng([zlib.crc32(name.encode()), seed]).standard_normal(out[name].shape)
        drawn = base * np.exp(spread * noise) if base else spread * noise
        out[name] = __import__('jax').numpy.asarray(drawn.astype(out[name].dtype))
    for name, factor in factors.items():
        out[name] = (out[name] * factor).astype(out[name].dtype)
    return out
```

```python
from contextlib import ExitStack

import numpy as np

import concourse.bass as bass
from concourse import mybir

F32 = mybir.dt.float32
F32R = mybir.dt.float32r
BF16 = mybir.dt.bfloat16
I32 = mybir.dt.int32
ALU = mybir.AluOpType
ACT = mybir.ActivationFunctionType
AX = mybir.AxisListType
ds = bass.ds

P = 128
D = 1024
NB = D // P
SEQ = 1024
DB, DT = 8, 8
NS = DB * DT
PAST = 512
PAGE = 128
NPG = PAST // PAGE
HEADS, HD = 8, 64
FF = 2816
FH = FF // P // 2
POOLW = (2, 4, 8, 16)
BUF = 15
TOPK_P, TOPK_S = 256, 130
EPS = 1e-6
T = (512, 512 + NS)
HALF = ((1, 512), (2, 288))
NT = (4, 5)
EXT = BUF + 512 + DB * (BUF + DT)
KCOL = PAST + NS
CHOSEN, INVALID, DUMMY, SPLITTER = -3.0e38, -1.0e38, -2.9e38, -2.0e38
MASK = -1.0e30
RING = 6
assert TOPK_P % 8 == 0 and TOPK_S % 8 == 2

CN = {}
_at = 0
for _name, _w in (("ident", P), ("ones", P), ("perm", P), ("tril", P), ("neg", P), ("inv", 64),
                  ("m01s", NS), ("negs", NS), ("sel", NS), ("dm", DB * NS), ("em", DB * NS)):
    CN[_name] = (_at, _at + _w)
    _at += _w
NKEEP = CN["em"][0]
NCONST = _at


def constants():
    c = np.zeros((P, NCONST), np.float32)

    def put(name, a):
        c[:a.shape[0], CN[name][0]:CN[name][0] + a.shape[1]] = a

    i = np.arange(P)
    put("ident", np.eye(P))
    put("ones", np.ones((P, P)))
    perm = np.zeros((P, P))
    for m in range(P):
        if m % HD < HD // 2:
            perm[m + HD // 2, m] = -1.0
        else:
            perm[m - HD // 2, m] = 1.0
    put("perm", perm)
    tril = (i[None, :] <= i[:, None]).astype(np.float64)
    put("tril", tril)
    put("neg", (1.0 - tril) * INVALID)
    inv = np.zeros((P, 64))
    for g, w in enumerate(POOLW):
        inv[:, 16 * g:16 * g + 16] = 1.0 / np.minimum(w, np.arange(16) + 1)
    put("inv", inv)
    r = np.arange(NS)
    same = (r[:, None] // DT == r[None, :] // DT) & (r[None, :] <= r[:, None])
    put("m01s", same.astype(np.float64))
    put("negs", (1.0 - same) * INVALID)
    put("sel", (np.arange(8)[:, None] == r[None, :] // DT).astype(np.float64))
    b = np.arange(DB)
    row, col = r[:, None, None], r[None, None, :]
    put("dm", ((row % DT == col % DT) & (col // DT == b[None, :, None])).reshape(NS, -1).astype(np.float64))
    put("em", ((row % DT == col % DT) & (row // DT == b[None, :, None])).reshape(NS, -1).astype(np.float64))
    half = HD // 2
    freq = np.float32(10000.0) ** (-np.arange(half, dtype=np.float32) / np.float32(half))
    pos = np.concatenate([np.arange(SEQ), PAST + r % DT]).astype(np.float32)
    ang = (pos[None, :] * freq.astype(np.float32)[np.arange(P) % half, None]).astype(np.float32)
    rope = np.stack([np.cos(ang), np.sin(ang)], axis=1).astype(np.float32)
    return c, rope


class Phase:

    def __init__(self, name, g, kt, iters, nd, free, layer=0, half=0):
        self.name, self.g, self.kt, self.iters, self.nd, self.free = name, g, kt, iters, nd, free
        self.layer, self.half = layer, half


def phases():
    out = [Phase("in", 0, 8, 8, 2, "aa"), Phase("in", 1, 8, 8, 2, "aa")]
    for g in range(2):
        def mixer(layer):
            for h in range(2):
                out.append(Phase("gu", g, 8, FH, 2, "ad", layer, h))
                out.append(Phase("dn", g, FH, 4, 2, "aa" if h == 0 else "dd", layer, h))
        out.append(Phase("out", g, 8, 4, 3, "aa"))
        mixer(0)
        out += [Phase("v", g, 8, 4, 2, "aa"), Phase("u", g, 8, 4, 2, "aa"), Phase("oo", g, 8, 4, 2, "aa")]
        mixer(1)
    chunk, win, freed, gus = 0, [0, 0], {("a", 0): 0, ("a", 1): 0, ("d", 0): 1, ("d", 1): 1}, 0
    prev = None
    for ph in out:
        ph.c0, ph.win = chunk, list(win)
        ph.base = {k: v for k, v in freed.items()}
        ph.prev = [(prev.free[p], freed[prev.free[p], p]) if prev else None for p in (0, 1)]
        ph.hb = FH * gus + 1
        gus += ph.name == "gu"
        chunk += 2 * ph.iters
        for p in (0, 1):
            win[p] += 16 * ph.nd * ph.iters
            freed[ph.free[p], p] += ph.iters
        ph.end = {k: v for k, v in freed.items()}
        prev = ph
    for a, b in zip(out, out[1:]):
        a.next = b
    out[-1].next = None
    return out


def wait(eng, sem, value):
    if isinstance(value, int):
        if value > 0:
            eng.wait_ge(sem, value)
        return
    eng.wait_ge(sem, value)
    eng.nop(nofuse=True)


def build_kernel(nc, ins, outs):
    ph_list = phases()
    by = {(q.name, q.g, q.layer, q.half): q for q in ph_list}

    def phase(name, g, layer=0, half=0):
        return by[name, g, layer, half]

    with ExitStack() as ctx:
        start = (nc.sbuf_base + 63) // 64 * 64
        cursor = [start]

        def place(name, shape, dt, at=None):
            size = 2 if dt == BF16 else 4
            n = size * int(np.prod(shape[1:]))
            if at is None:
                at = cursor[0]
                cursor[0] = (at + n + 31) // 32 * 32
                assert cursor[0] <= nc.sbuf_usable_end, (name, cursor[0], nc.sbuf_usable_end)
            return nc.alloc_sbuf_tensor_at(name, shape, dt, offset=at), at

        X, _ = place("resid", [P, NB, T[1]], F32)
        AR, a_at = place("act_split", [P, 2, NB, T[1]], F32R)
        HR, h_at = place("hidden_split", [P, 2, FH, T[1]], F32R)
        Y, y_at = place("mixed", [P, NB, T[1]], F32)
        WR, _ = place("w_raw", [P, 2, FH * P], F32)
        WH, _ = place("w_hi", [P, 2, FH * P], F32R)
        WL, _ = place("w_lo", [P, 2, FH * P], F32R)
        KT, _ = place("keys_t", [P, SEQ + NS], F32)
        IKT, _ = place("idx_keys_t", [P, SEQ + NS], F32)
        VN, _ = place("values", [P, 9, P], F32)
        IW, _ = place("idx_weights", [P, 9, 8], F32)
        SB, sb_at = place("scores1", [P, 3328 + KCOL + 8], F32)
        SA, _ = place("scores0", [P, 896], F32)
        SQ, sq_at = place("squares", [P, 2, T[1]], F32)
        TT, tt_at = place("temps", [P, 2, T[1]], F32)
        SS, _ = place("square_sums", [P, 5 * P], F32)
        RT, _ = place("root_rstd", [P, 2, 5], F32)
        CT, _ = place("constants", [P, NKEEP], F32)
        GC, _ = place("gains", [P, 84], F32)
        IDB, _ = place("ident_bf16", [P, P], BF16)
        MCB, _ = place("causal_bf16", [P, P], BF16)
        EB, _ = place("spread_bf16", [NS, DB, NS], BF16)
        IWT, _ = place("idx_weights_t", [8, NS], F32)
        M8, _ = place("top8", [P, 5, 8], F32)
        MX, _ = place("row_stats", [P, 4, 16], F32)
        PGT, _ = place("pages", [1, DB * NPG], I32)
        T16, _ = place("first_windows", [P, 16], F32)

        def over(name, shape, dt, base, words):
            return place(name, shape, dt, base + 4 * words)[0]

        DG = over("diag_rstd", [P, 5, P], F32, tt_at, 0)

        IQ = over("idx_queries_t", [P, 4, T[1]], F32, h_at, 0)
        XPE = over("pool_in", [P, 4, EXT], F32, h_at, 2304)
        RP = over("rope", [P, 2, T[1]], F32, h_at, 5152)
        KN = over("keys_rows", [P, 5, P], F32, h_at, 6304)
        IKN = over("idx_keys_rows", [P, 5, HD], F32, h_at, 6944)
        XN = over("x_rows", [P, 5, D], F32, h_at, 7552)
        GN = over("gain_rows", [84, P], F32, h_at, 0)
        EM = over("spread_f32", [P, DB * NS], F32, h_at, 128)
        SPN = over("state_rows", [DB * BUF, 512], F32, h_at, 640)
        XNS = over("xp_rows", [P, 2, 512], F32, h_at, 7552)
        WPG = over("w_pool", [P, 4, P], F32, sb_at, 0)
        QT = over("queries_t", [P, 2, T[1]], F32, sb_at, 512)
        PD = over("pooled", [P, 2, T[1]], F32, sb_at, 512)
        PHL = over("pool_split", [P, 2, T[1]], F32R, sb_at, 1664)
        GXS = over("xp_sample", [P, 4, NS], F32, sb_at, 2816)
        PA = over("window_a", [P, 2 * T[1]], F32, sq_at, 0)
        PB = over("window_b", [P, 2 * T[1]], F32, tt_at, 0)
        IKS = over("idx_keys_split", [P, 2, SEQ], F32R, a_at, 0)
        IQS = over("idx_queries_split", [P, 2, 8, P], F32R, a_at, 2048)
        IKP = over("idx_key_pages", [P, DB * NPG, P], F32, a_at, 4096)
        IQZ = over("idx_queries_sample", [P, DB, NS], F32, a_at, 8192)
        IKTB = [over("idx_page_keys0", [P, PAST], F32, a_at, 8704), over("idx_page_keys1", [P, PAST], F32, y_at, 3712)]
        R = over("relu", [P, 2, SEQ], F32, y_at, 0)
        MS = over("head_mix", [NS, DB, NS], F32, y_at, 2048)
        RS = over("relu_sample", [NS, 2, KCOL], F32, y_at, 2560)
        PR = over("probs", [P, RING, SEQ], F32, h_at, 0)
        VS = over("values_split", [P, 2, 8, P], F32R, h_at, 6144)
        QST = over("queries_split", [P, 8, P], F32R, h_at, 8192)
        PT = over("probs_t", [P, 2, 2, 512], F32R, h_at, 9216)
        MK = over("mask", [P, 2, SEQ], BF16, h_at, 11264)
        KS = over("keys_split", [P, 2, 2, SEQ], F32R, y_at, 0)
        QR = over("queries_tile", [P, 4, P], F32, y_at, 4096)
        KP = over("key_pages", [P, DB * NPG, P], F32, h_at, 0)
        VP = over("value_pages", [P, DB * NPG, P], F32, h_at, 4096)
        QZ = over("queries_sample", [P, DB, NS], F32, h_at, 8192)
        KTB = over("page_keys_t", [P, 2, PAST], F32, h_at, 9216)
        PRS = over("probs_sample", [NS, 2, KCOL], F32, h_at, 10240)
        PTS = over("probs_sample_t", [P, 2, 5 * NS], F32, h_at, 11392)
        MKS = over("mask_sample", [NS, KCOL], BF16, h_at, 12032)
        ZN = over("z_rows", [P, 5, D], F32, h_at, 0)
        WS = over("w_spatial_rows", [P, 8, P], F32, h_at, 0)
        WS8 = over("w_spatial_sample_rows", [NS, 8, NS], F32, h_at, 1024)
        U = over("u_t", [P, NB, T[1]], F32, h_at, 5120)
        WMT = over("w_spatial_t", [P, 8, P], F32, h_at, 9728)
        WM8T = over("w_spatial_sample_t", [NS, 8, NS], F32, h_at, 10752)
        BS = over("b_spatial_all", [P, 8, P], F32, h_at, 11264)
        ON = over("y_rows", [P, 5, D], F32, h_at, 0)

        PS = ctx.enter_context(nc.psum_tensor("psum", [P, 8, 512], F32))
        PSF = PS[:].rearrange("p b n -> p (b n)")

        q_dram = nc.dram_tensor("queries_spill", [2, P, 4, T[1]], F32, kind="Internal").ap()
        c_dram = nc.dram_tensor("pool_spill", [2, P, 2, 4, T[1]], F32, kind="Internal").ap()
        x_dram = nc.dram_tensor("resid_spill", [P, NB, T[1]], F32, kind="Internal").ap()

        def const(name, rows=P):
            a, b = CN[name]
            return CT[0:rows, a:b]

        IDENT, ONES, TRIL = const("ident"), const("ones"), const("tril")
        sems = {}

        def S(name):
            if name not in sems:
                sems[name] = ctx.enter_context(nc.semaphore(name))
            return sems[name]

        G_MIX_PRE, G_MIX_POST, G_FFN_PRE, G_FFN_POST, G_LN, B_LN, G_POOL = 0, 16, 32, 48, 64, 72, 80

        def gain(base, layer, n):
            return GC[:, base + 8 * layer + n:base + 8 * layer + n + 1]

        def lin(p, g):
            h, w = HALF[g]
            return PS[:, 2 * p:2 * p + h, 0:w]

        def aux(x, g):
            h, w = HALF[g]
            return PS[:, 4 + 2 * x:4 + 2 * x + h, 0:w]

        def hv(ap, g):
            return ap.rearrange("p (h w) -> p h w", h=HALF[g][0])

        def halves(g):
            h, w = HALF[g]
            return [(b, b * w, (b + 1) * w) for b in range(h)]

        def tiles(g):
            return [(k, P * k, min(P, T[g] - P * k)) for k in range(NT[g])]

        def flat(ap):
            return ap.rearrange("p a n -> p (a n)")

        def norm_at(kind, g, s):
            if kind == "load":
                return g
            return 2 + 4 * g + s

        def r_at(g, s):
            return 2 + 8 * g + s

        def a_at_(g, s):
            return 2 + 4 * g + s

        def z_at(g, s):
            return 2 + 5 * g + s

        SPOST = (0, 2, 5, 7)
        SPRE = (1, 3, 6)
        SA_ = (0, 1, 3)
        SZ = (0, 1, 3, 4)

        IDX_T = ((2, 3), (4, 5, 6, 7))
        IDX_U = ((0, 1), (2, 3, 4, 5))
        SB_AT = {4: 0, 5: 640, 6: 1408, 7: 2304}
        SS_AT = 3328

        def score(t):
            n = P * (t + 1)
            return SA[:, 384 * (t - 2):384 * (t - 2) + n] if t < 4 else SB[:, SB_AT[t]:SB_AT[t] + n]

        SCS = SB[0:NS, SS_AT:SS_AT + KCOL + 8]

        def kbase(t, kv):
            return sum(2 * (u + 1) for u in range(t)) + kv * (t + 1)

        def items(g):
            out = []
            last = 4 * g + 3
            for t in range(4 * g, 4 * g + 4):
                out += [("qk", t, h) for h in (range(6) if t == 4 * g else range(2, 6))]
                out.append(("pv", t, 0))
                out += [("qk", t, 6), ("qk", t, 7)]
                if t < last:
                    out += [("qk", t + 1, 0), ("qk", t + 1, 1)]
                out.append(("pv", t, 1))
            return out

        def logits(x, t, rows=P):
            n = P * (t + 1)
            k = 1 if n <= 512 else 2
            return PS[0:rows, 2 * x:2 * x + k, 0:n // k]

        def cut(ap, t):
            k = 1 if t < 4 else 2
            return ap.rearrange("p (c n) -> p c n", c=k)

        block = ctx.enter_context(nc.Block())

        @block.sync
        def _(sp):
            w_ge, w_oe = ins["w_in_even"][0], ins["w_out_even"][0]
            w_io, w_oo = ins["w_in_odd"][0], ins["w_out_odd"][0]

            def cols(w, first, k0, k1, n=P):
                return w[P * k0:P * k1, :].rearrange("(k p) c -> p k c", p=P)[:, :, ds(first, n)]

            def load_chunk(ph, i, p):
                c = ph.c0 + 2 * i + p
                if not (isinstance(c, int) and c < 2):
                    sp.wait_ge(S("w_lo"), c - 1)
                slot = WR[:, p, :].rearrange("p (k c) -> p k c", c=P)
                sem = S(f"w_in{p}")

                def put(dst, src):
                    sp.dma_start(dst, src).then_inc(sem, 16)

                if ph.name == "in":
                    local = 2 * i + p
                    if local < 8:
                        first = 64 * i + (768 if p else 0)
                        parts = [(first, 0), (first + 256, 64)]
                    elif local == 8:
                        parts = [(512, 0), (576, 64)]
                    elif local == 9:
                        parts = [(1280, 0), (1280, 64)]
                    elif local == 10:
                        parts = [(640, 0), (704, 64)]
                    elif local == 11:
                        parts = [(1344, 0), (1408, 64)]
                    else:
                        parts = [(1352 + P * (local - 12), 0), (1352 + P * (local - 12) + 64, 64)]
                    for first, at in parts:
                        put(slot[:, 0:8, at:at + 64], cols(w_ge, first, 0, 8, 64))
                elif ph.name == "out":
                    first = P * (2 * i + p)
                    for r in range(2):
                        put(slot[64 * r:64 * r + 64, 0:4, :],
                            w_oe[256 * r:256 * r + 256, :].rearrange("(k p) c -> p k c", p=64)[:, :, ds(first, P)])
                    put(slot[:, 4:8, :], cols(w_oe, first, 4, 8))
                else:
                    if ph.name == "gu":
                        w, first, row = ins["w_ffn_gate_up"][ph.layer], FF * p + P * (FH * ph.half + i), 0
                    elif ph.name == "dn":
                        w, first, row = ins["w_ffn_down"][ph.layer], P * (2 * i + p), FH * ph.half
                    elif ph.name == "v":
                        w, first, row = w_io, D + P * (2 * i + p), 0
                    elif ph.name == "u":
                        w, first, row = w_io, P * (2 * i + p), 0
                    else:
                        w, first, row = w_oo, P * (2 * i + p), 0
                    mid = (ph.kt + 1) // 2
                    put(slot[:, 0:mid, :], cols(w, first, row, row + mid))
                    put(slot[:, mid:ph.kt, :], cols(w, first, row + mid, row + ph.kt))

            def head(ph):
                load_chunk(ph, 0, 0)
                load_chunk(ph, 0, 1)

            def rest(ph):
                with sp.Fori(1, ph.iters) as i:
                    load_chunk(ph, i, 0)
                    load_chunk(ph, i, 1)

            def load_x(g):
                for k in range(4):
                    sp.dma_start(XN[:, k, :], ins["x_prompt"][0, 512 * g + P * k:512 * g + P * k + P, :]).then_inc(S("x_in"), 16)
                if g:
                    sp.dma_start(XN[0:NS, 4, :], ins["x_sample"].rearrange("b t d -> (b t) d")).then_inc(S("x_in"), 16)

            def in_stage(g):
                ph = phase("in", g)

                def after(local):
                    if 0 <= local < 8 and local % 2 == 0:
                        j = local // 2
                        sp.wait_ge(S("rope_out"), 10 * g + local + 1)
                        sp.dma_start(q_dram[g, :, j, 0:T[g]], QT[:, j % 2, 0:T[g]]).then_inc(S(f"q_out{j % 2}"), 16)

                for local in range(2, 16):
                    load_chunk(ph, local // 2, local % 2)
                    after(local - 6)
                nxt = phase("in", 1) if g == 0 else phase("out", 0)
                head(nxt)
                rows = slice(512 * g, 512 * g + 512)
                kn = [outs["new_k_prompt"], outs["new_v_prompt"]]
                sp.wait_ge(S("nat_a"), 3 * g + 2)
                for k in range(4):
                    r0 = 512 * g + P * k
                    sp.dma_start(kn[0][0, 0, r0:r0 + P].rearrange("t h d -> t (h d)"), KN[:, k, :]).then_inc(S("kv_out"), 16)
                    sp.dma_start(outs["new_idx_k_prompt"][0, 0, r0:r0 + P], IKN[:, k, :]).then_inc(S("kv_out"), 16)
                if g:
                    sp.dma_start(outs["new_k_sample"][0].rearrange("b t h d -> (b t) (h d)"), KN[0:NS, 4, :]).then_inc(S("kv_out"), 16)
                    sp.dma_start(outs["new_idx_k_sample"][0].rearrange("b t d -> (b t) d"), IKN[0:NS, 4, :]).then_inc(S("kv_out"), 16)
                sp.wait_ge(S("nat_a"), 3 * g + 3)
                for k in range(4):
                    r0 = 512 * g + P * k
                    sp.dma_start(kn[1][0, 0, r0:r0 + P].rearrange("t h d -> t (h d)"), VN[:, 4 * g + k, :]).then_inc(S("kv_out"), 16)
                if g:
                    sp.dma_start(outs["new_v_sample"][0].rearrange("b t h d -> (b t) (h d)"), VN[0:NS, 8, :]).then_inc(S("kv_out"), 16)
                for pg in range(4):
                    sp.wait_ge(S("pool_lo"), 4 * g + pg + 1)
                    sp.dma_start(c_dram[g, :, :, pg, 0:T[g]], PHL[:, :, 0:T[g]].bitcast(F32)).then_inc(S("pool_out"), 16)
                if g:
                    sp.wait_ge(S("xp_rows"), 1)
                    sp.dma_start(outs["new_pool_prompt"][0, 0], XNS[0:BUF, 0, :]).then_inc(S("st_out"), 16)
                    for b in range(DB):
                        sp.dma_start(outs["new_pool_sample"][0, b, BUF - DT:BUF], XNS[DT * b:DT * b + DT, 1, :]).then_inc(S("st_out"), 16)

            def pages(dst, cache, sem, width, copies):
                with sp.Fori(0, DB * NPG) as i:
                    page = sp.value_load(PGT[0:1, ds(i, 1)], min_val=0, max_val=DB * NPG * 5 // 4 - 1)
                    for c in range(copies):
                        src = cache[ds(page, 1)].rearrange("a s d -> (a s) d")
                        sp.dma_start(dst[:, ds(i, 1), width * c:width * c + width].rearrange("p a d -> p (a d)"), src).then_inc(sem, 16)

            def attend(g):
                if g == 0:
                    sp.wait_ge(S("mix_mm"), DB)
                sp.dma_start(AR[:, 0, 4:8, 0:T[g]].bitcast(F32), c_dram[g, :, 0, :, 0:T[g]]).then_inc(S("pool_in"), 16)
                sp.dma_start(AR[:, 1, 4:8, 0:T[g]].bitcast(F32), c_dram[g, :, 1, :, 0:T[g]]).then_inc(S("pool_in"), 16)
                for k in range(4):
                    t = 4 * g + k
                    wait(sp, S("qst_lo"), 2 * t)
                    sp.dma_start(QR[:], q_dram[g, :, :, P * k:P * k + P]).then_inc(S("q_in"), 16)
                if g:
                    sp.wait_ge(S("qst_lo"), 16)
                    sp.dma_start(QR[:, :, 0:NS], q_dram[1, :, :, 512:T[1]]).then_inc(S("q_in"), 16)
                    sp.wait_ge(S("pv_mm"), kbase(8, 0))
                    sp.wait_ge(S("o_hi"), 16)
                    pages(KP, ins["cache_k"][0].rearrange("n s h d -> n s (h d)"), S("kp_in"), P, 1)
                    pages(VP, ins["cache_v"][0].rearrange("n s h d -> n s (h d)"), S("vp_in"), P, 1)

            def spatial_weights(g):
                sp.wait_ge(S("w_used"), phase("dn", g, 0, 1).c0 + 8)
                sp.dma_start(WS[:], ins["w_spatial"][0].rearrange("g t s -> t g s")).then_inc(S("ws_in"), 16)
                sp.dma_start(BS[:], ins["b_spatial"][0].unsqueeze(0).to_broadcast([P, 8, P])).then_inc(S("ws_in"), 16)
                sp.wait_ge(S("ws8_zero"), g + 1)
                for b in range(DB):
                    sp.dma_start(WS8[DT * b:DT * b + DT, :, DT * b:DT * b + DT],
                                 ins["w_spatial"][0, :, 0:DT, 0:DT].rearrange("g t s -> t g s")).then_inc(S("ws_in"), 16)

            sp.dma_start(CT[:], ins["constants"][:, 0:NKEEP]).then_inc(S("c_in"), 16)
            row = 0
            for name in ("norm_mix_pre", "norm_mix_post", "norm_ffn_pre", "norm_ffn_post", "sgu_norm_g", "sgu_norm_b", "pool_scale"):
                src = ins[name].rearrange("l (n p) -> (l n) p", p=P)
                sp.dma_start(GN[row:row + src.shape[0], :], src).then_inc(S("g_in"), 16)
                row += src.shape[0]
            load_x(0)
            head(phase("in", 0))
            sp.dma_start(EM[:], ins["constants"][:, NKEEP:NCONST]).then_inc(S("g_in"), 16)
            sp.dma_start(SPN[:], ins["state_pool"][0].rearrange("b r d -> (b r) d")).then_inc(S("g_in"), 16)
            sp.dma_start(PGT[:], ins["page_table"].rearrange("b n -> (b n)").unsqueeze(0)).then_inc(S("pt_in"), 16)
            sp.dma_start(WPG[:], ins["w_pool_group"][0].rearrange("g c e -> c g e")).then_inc(S("wp_in"), 16)
            sp.dma_start(outs["new_pool_sample"][0, :, 0:BUF - DT], ins["state_pool"][0, :, DT:BUF]).then_inc(S("st_out"), 16)
            sp.wait_ge(S("setup_a"), 5)
            sp.dma_start(RP[:, :, 0:T[0]], ins["rope"][:, :, 0:T[0]]).then_inc(S("rope_in"), 16)
            in_stage(0)
            load_x(1)
            sp.wait_ge(S("rope_out"), 10)
            sp.dma_start(RP[:], ins["rope"][:, :, 512:SEQ + NS]).then_inc(S("rope_in"), 16)
            sp.wait_ge(S("a_t"), 16)
            sp.dma_start(x_dram, Y[:]).then_inc(S("x_out"), 16)
            in_stage(1)
            sp.wait_ge(S("pt_in"), 16)
            sp.wait_ge(S("w_used"), phase("in", 1).c0 + 16)
            pages(IKP, ins["cache_idx_k"][0], S("ikp_in"), HD, 2)
            for g in range(2):
                attend(g)
                rest(phase("out", g))
                for layer in range(2):
                    for half in range(2):
                        for name in ("gu", "dn"):
                            q = phase(name, g, layer, half)
                            head(q)
                            rest(q)
                    if layer == 0:
                        head(phase("v", g))
                        spatial_weights(g)
                        rest(phase("v", g))
                        for name in ("u", "oo"):
                            head(phase(name, g))
                            if g and name == "oo":
                                sp.wait_ge(S("zc_d"), 8)
                                sp.wait_ge(S("zc_a"), 8)
                                sp.dma_start(outs["new_sgu_v_sample"][0].rearrange("b t d -> (b t) d"), ZN[0:NS, 4, :]).then_inc(S("z_out"), 16)
                            rest(phase(name, g))
                if g == 0:
                    head(phase("out", 1))
                    sp.wait_ge(S("y_ps"), 4)
                    sp.dma_start(X[:], x_dram).then_inc(S("xb_in"), 16)
                for k, _, w in tiles(g):
                    sp.wait_ge(S("y_cp"), 5 * g + k + 1 - g)
                    dst = outs["y_prompt"][0, 512 * g + P * k:512 * g + P * k + P] if k < 4 else \
                        outs["y_sample"].rearrange("b t d -> (b t) d")
                    sp.dma_start(dst, ON[0:w, k, :]).then_inc(S("y_out"), 16)
            sp.wait_ge(S("y_out"), 16 * 9)
            sp.wait_ge(S("kv_out"), 16 * 27)
            sp.wait_ge(S("st_out"), 16 * 10)
            for b in range(2):
                sp.wait_ge(S(f"q_out{b}"), 64)
            sp.wait_ge(S("pool_out"), 128)
            sp.wait_ge(S("x_out"), 16)
            sp.wait_ge(S("z_out"), 16)

        @block.tensor
        def _(pe):
            def chunk(ph, i, p, x_hi, x_lo, ready=None):
                c = ph.c0 + 2 * i + p
                g = ph.g
                pe.wait_ge(S("w_lo"), c + 1)
                e, n = ph.free[p], ph.base[ph.free[p], p]
                if ph.prev[p] and ph.prev[p][0] != e:
                    wait(pe, S(f"free_{ph.prev[p][0]}{p}"), ph.prev[p][1])
                if isinstance(n + i, int):
                    wait(pe, S(f"free_{e}{p}"), n + i)
                else:
                    pe.wait_ge(S(f"free_{e}{p}"), n + i)
                for k in range(ph.kt):
                    if ready:
                        ready(k)
                    at = slice(P * k, P * k + P)
                    for w, x in ((WH, x_hi), (WH, x_lo), (WL, x_hi)):
                        for b, lo, hi in halves(g):
                            mm = pe.matmul(PS[:, 2 * p + b, 0:hi - lo], w[:, p, at], x(k)[:, lo:hi],
                                           start=(k == 0 and w is WH and x is x_hi),
                                           stop=(k == ph.kt - 1 and w is WL))
                mm.then_inc(S("w_used"), 1)

            def a_hi(k):
                return AR[:, 0, k, :]

            def a_lo(k):
                return AR[:, 1, k, :]

            def h_hi(k):
                return HR[:, 0, k, :]

            def h_lo(k):
                return HR[:, 1, k, :]

            def linear(ph, split=None):
                def ready(k):
                    if split is not None:
                        pe.wait_ge(S("a_lo"), 8 * split + k + 1)
                chunk(ph, 0, 0, a_hi, a_lo, ready)
                chunk(ph, 0, 1, a_hi, a_lo)
                with pe.Fori(1, ph.iters) as i:
                    chunk(ph, i, 0, a_hi, a_lo)
                    chunk(ph, i, 1, a_hi, a_lo)

            def down(ph):
                def ready(k):
                    if k == 0:
                        pe.wait_ge(S("h_lo"), ph.hb - 1)
                    if k == FH - 1:
                        pe.wait_ge(S("h_lo"), ph.hb)
                with pe.Fori(0, ph.iters) as i:
                    chunk(ph, i, 0, h_hi, h_lo, ready)
                    chunk(ph, i, 1, h_hi, h_lo)

            def token_sums(g, sem, value):
                pe.wait_ge(S(sem), value)
                for k, lo, w in tiles(g):
                    mm = pe.matmul(PS[0:w, 6, 2 * k:2 * k + 1], SS[:, lo:lo + w], ONES[:, 0:1], start=True, stop=True)
                mm.then_inc(S("n_sum"), 1)

            def block_sum(n, g, ready, done, m):
                pe.wait_ge(S(ready), 8 * m + n + 1)
                order = tiles(g) if n == 0 else tiles(g)[::-1]
                for k, lo, w in order:
                    mm = pe.matmul(PS[0:w, 6, 2 * k:2 * k + 1], SQ[:, n % 2, lo:lo + w], ONES[:, 0:1],
                                   start=n == 0 and k == 0, stop=n == NB - 1 and k == 0)
                mm.then_inc(S(done if n < NB - 1 else "n_sum"), 1)

            def spread(r, g):
                pe.wait_ge(S("n_dg"), r + 1)
                for k, lo, w in tiles(g):
                    mm = pe.matmul(PSF[:, 4 * 512 + lo:4 * 512 + lo + w], ONES, DG[:, k, 0:w], start=True, stop=True)
                mm.then_inc(S("n_b"), 1)

            def load_x(g):
                pe.wait_ge(S("x_in"), 64 if g == 0 else 144)
                if g:
                    for p in (0, 1):
                        pe.wait_ge(S(f"free_a{p}"), phase("in", 0).end["a", p])
                for n in range(NB):
                    wait(pe, S("xt_cp"), 8 * g + n - 1)
                    for k, lo, w in tiles(g):
                        mm = pe.transpose(PSF[:, 1024 * (n % 2) + lo:1024 * (n % 2) + lo + w],
                                          XN[0:w, k, P * n:P * n + P], IDENT[0:w, 0:w])
                    mm.then_inc(S("xt_ps"), 1)
                if g:
                    pe.wait_ge(S("idx_r"), 16)
                token_sums(g, "ss_p", 8 * g + 8)
                spread(g, g)
                pe.wait_ge(S("xt_cp"), 8 * g + 8)

            def rows_of(src, rows, x, g, idn):
                for k, lo, w in tiles(g):
                    mm = pe.transpose(PSF[0:w, (4 + 2 * x) * 512 + P * k:(4 + 2 * x) * 512 + P * k + rows],
                                      src[:, lo:lo + w], idn)
                mm.then_inc(S("nat"), 1)

            def in_stage(g):
                ph = phase("in", g)

                def rotate(local):
                    r = 10 * g + local
                    p = local % 2
                    pe.wait_ge(S(f"free_a{p}"), ph.base["a", p] + local // 2 + 1)
                    wait(pe, S("rope_t1"), r - 1)
                    for b, lo, hi in halves(g):
                        mm = pe.matmul(PS[:, 4 + 2 * p + b, 0:hi - lo], const("perm"), SQ[:, p, lo:hi], start=True, stop=True)
                    mm.then_inc(S("rope_sw"), 1)

                def pooled(pg):
                    pe.wait_ge(S("pool_d"), 4 * g + pg + 1)
                    if pg == 0:
                        pe.wait_ge(S("nat_a"), 3 * g + 3)
                    elif pg == 1:
                        pe.wait_ge(S("iw_rows"), g + 1)
                    else:
                        pe.wait_ge(S("pool_lo"), 4 * g + pg - 1)
                    for b, lo, hi in halves(g):
                        mm = pe.matmul(PS[:, 4 + 2 * (pg % 2) + b, 0:hi - lo], WPG[:, pg, :], PD[:, pg % 2, lo:hi], start=True, stop=True)
                    mm.then_inc(S("pool_mm"), 1)

                for local in range(16):
                    def ready(k):
                        if local == 0:
                            pe.wait_ge(S("a_lo"), 8 * g + k + 1)
                    chunk(ph, local // 2, local % 2, a_hi, a_lo, ready)
                    if 1 <= local <= 10:
                        rotate(local - 1)
                    if local == 11:
                        c0 = 512 * g
                        pe.wait_ge(S("rope_t1"), 10 * g + 10)
                        pe.wait_ge(S("rope_out"), 10 * g + 10)
                        rows_of(KT[:, c0:c0 + T[g]], P, 0, g, IDENT)
                        rows_of(IKT[0:HD, c0:c0 + T[g]], HD, 1, g, IDENT[0:HD, 0:HD])
                    if local == 12:
                        pe.wait_ge(S("nat_a"), 3 * g + 1)
                        pe.wait_ge(S("free_a0"), ph.base["a", 0] + 6)
                        rows_of(SQ[:, 0, 0:T[g]], P, 0, g, IDENT)
                    if local == 13:
                        pe.wait_ge(S("nat_a"), 3 * g + 2)
                        pe.wait_ge(S("free_a1"), ph.base["a", 1] + 6)
                        rows_of(SQ[:, 1, 0:T[g]], P, 1, g, IDENT)
                    if local == 14:
                        pe.wait_ge(S("wp_in"), 16)
                        pooled(0)
                    if local == 15:
                        pooled(1)
                pooled(2)
                pooled(3)
                if g:
                    for p in (0, 1):
                        pe.wait_ge(S(f"free_a{p}"), ph.end["a", p])
                    for pg in range(4):
                        pe.transpose(PS[0:BUF, 0, P * pg:P * pg + P], XPE[:, pg, 512:512 + BUF], IDENT)
                    pe.wait_ge(S("xs_cp"), 1)
                    for pg in range(4):
                        mm = pe.transpose(PS[0:NS, 1, P * pg:P * pg + P], GXS[:, pg, :], IDENT)
                    mm.then_inc(S("xp_ps"), 1)

            def index(g):
                pe.wait_ge(S("ik_lo"), g + 1)
                pe.wait_ge(S("pool_lo"), 4 * g + 4)
                for u, t in zip(IDX_U[g], IDX_T[g]):
                    n = P * (t + 1)
                    k = 1 if n <= 512 else 2
                    pe.wait_ge(S("iq_lo"), 2 * u + 2)
                    for h in range(8):
                        wait(pe, S("idx_r"), 8 * u + h - 1)
                        x = h % 2
                        for part in range(2):
                            for b in range(k):
                                w = n // k
                                mm = pe.matmul(PS[:, 4 + 2 * x + b, 0:w], IQS[:, u % 2, h, :], IKS[:, part, b * w:b * w + w],
                                               start=part == 0, stop=part == 1)
                        mm.then_inc(S("idx_mm"), 1)

            def index_sample():
                pe.wait_ge(S("idx_r"), 48)
                pe.wait_ge(S("iw_rows"), 2)
                pe.wait_ge(S("c_in"), 16)
                pe.matmul(PS[0:NS, 6, 0:NS], const("sel", 8), IWT[:, :], start=True, stop=True).then_inc(S("spread_mm"), 1)
                pe.wait_ge(S("ikp_in"), 16 * 2 * DB * NPG)
                pe.wait_ge(S("xp_rows"), 1)

                def turn(b):
                    wait(pe, S("ikt_cp"), b - 1)
                    for j in range(NPG):
                        mm = pe.transpose(PS[:, b % 2, P * j:P * j + P], IKP[:, NPG * b + j, :], IDENT)
                    mm.then_inc(S("ikt_ps"), 1)

                def mix(b):
                    pe.wait_ge(S("rs"), b + 1)
                    if b == 0:
                        pe.wait_ge(S("ms"), 1)
                    for bank, lo, hi in ((4, 0, PAST), (5, PAST, KCOL)):
                        mm = pe.matmul(PS[0:NS, bank, 0:hi - lo], MS[:, b, :], RS[:, b % 2, lo:hi], start=b == 0, stop=b == DB - 1)
                    mm.then_inc(S("mix_mm"), 1)

                turn(0)
                for b in range(DB):
                    if b + 1 < DB:
                        turn(b + 1)
                    pe.wait_ge(S("ikt_cp"), b + 1)
                    pe.wait_ge(S("iqz"), 1)
                    wait(pe, S("rs"), b)
                    pe.matmul(PS[0:NS, 2, 0:PAST], IQZ[:, b, :], IKTB[b % 2][:], start=True, stop=True)
                    pe.matmul(PS[0:NS, 3, 0:NS], IQZ[:, b, :], IKT[:, SEQ:SEQ + NS], start=True, stop=True).then_inc(S("rel_mm"), 1)
                    if b:
                        mix(b - 1)
                mix(DB - 1)

            def attend(g):
                pe.wait_ge(S("ks_lo"), g + 1)
                if g:
                    pe.wait_ge(S("y_cp"), 4)
                for kind, t, z in items(g):
                    if kind == "qk":
                        h, hh, x = z, 8 * t + z, z % 2
                        n = P * (t + 1)
                        k = 1 if n <= 512 else 2
                        w = n // k
                        pe.wait_ge(S("qst_lo"), 2 * t + h // 4 + 1)
                        wait(pe, S("exp"), hh - 1)
                        if t >= 2:
                            pe.wait_ge(S("mk"), t - 1)
                            for b in range(k):
                                pe.matmul(PS[:, 2 * x + b, 0:w], IDB[:], MK[:, t % 2, b * w:b * w + w], start=True, stop=False)
                        for part in range(2):
                            for b in range(k):
                                mm = pe.matmul(PS[:, 2 * x + b, 0:w], QST[:, h, :], KS[:, h // 4, part, b * w:b * w + w],
                                               start=t < 2 and part == 0, stop=t >= 2 and part == 1)
                        if t < 2:
                            mm = pe.matmul(PS[:, 2 * x, P * t:P * t + P], IDB[:], MCB[:], start=False, stop=True)
                        mm.then_inc(S("qk_mm"), 1)
                        continue
                    kv, k0 = z, kbase(t, z)
                    pe.wait_ge(S("p_norm"), 8 * t + 4 * kv + 4)
                    wait(pe, S("o_lo"), 2 * t + kv - 1)

                    def turn(kk):
                        wait(pe, S("pt_lo"), k0 + kk - 1)
                        for j in range(4):
                            slot = (8 * t + 4 * kv + j) % RING
                            mm = pe.transpose(PS[:, 4 + (k0 + kk) % 2, P * j:P * j + P], PR[:, slot, P * kk:P * kk + P], IDENT)
                        mm.then_inc(S("p_tr"), 1)

                    turn(0)
                    for kk in range(t + 1):
                        if kk < t:
                            turn(kk + 1)
                        pe.wait_ge(S("pt_lo"), k0 + kk + 1)
                        b = (k0 + kk) % 2
                        for v, q in ((0, 0), (0, 1), (1, 0)):
                            mm = pe.matmul(PS[:, 6 + kv, :], VS[:, v, kk, :], PT[:, b, q, :],
                                           start=kk == 0 and v == 0 and q == 0, stop=kk == t and v == 1)
                        mm.then_inc(S("pv_mm"), 1)

            def attend_sample():
                pe.wait_ge(S("kp_in"), 16 * DB * NPG)
                pe.wait_ge(S("pt_lo"), kbase(8, 0))
                pe.wait_ge(S("o_lo"), 16)
                pe.wait_ge(S("exp"), 64)

                def turn(b):
                    wait(pe, S("ktb"), b - 1)
                    for j in range(NPG):
                        mm = pe.transpose(PS[:, 4 + b % 2, P * j:P * j + P], KP[:, NPG * b + j, :], IDENT)
                    mm.then_inc(S("kt_ps"), 1)

                def values(b):
                    pe.wait_ge(S("ps_norm"), b + 1)
                    wait(pe, S("pts"), b)
                    for j in range(NPG):
                        pe.transpose(PS[:, 6, NS * j:NS * j + NS], PRS[:, b % 2, P * j:P * j + P], IDENT[0:NS, 0:NS])
                    pe.transpose(PS[0:NS, 6, NS * NPG:NS * NPG + NS], PRS[:, b % 2, PAST:KCOL], IDENT[0:NS, 0:NS]).then_inc(S("ps_tr"), 1)
                    pe.wait_ge(S("pts"), b + 1)
                    for j in range(NPG):
                        pe.matmul(PS[:, 7, NS * b:NS * b + NS], VP[:, NPG * b + j, :], PTS[:, b % 2, NS * j:NS * j + NS],
                                  start=j == 0, stop=False)
                    pe.matmul(PS[:, 7, NS * b:NS * b + NS], VN[0:NS, 8, :], PTS[0:NS, b % 2, NS * NPG:NS * NPG + NS],
                              start=False, stop=True).then_inc(S("pvs_mm"), 1)

                turn(0)
                for b in range(DB):
                    if b + 1 < DB:
                        turn(b + 1)
                    x = b % 2
                    pe.wait_ge(S("ktb"), b + 1)
                    pe.wait_ge(S("qz"), 1)
                    pe.wait_ge(S("mks"), 1)
                    wait(pe, S("exps"), b - 1)
                    for bank, lo, hi, keys in ((2 * x, 0, PAST, KTB[:, x, :]), (2 * x + 1, PAST, KCOL, KT[:, SEQ:SEQ + NS])):
                        pe.matmul(PS[0:NS, bank, 0:hi - lo], EB[:, b, :], MKS[:, lo:hi], start=True, stop=False)
                        mm = pe.matmul(PS[0:NS, bank, 0:hi - lo], QZ[:, b, :], keys, start=False, stop=True)
                    mm.then_inc(S("qks_mm"), 1)
                    if b == 0:
                        pe.wait_ge(S("vp_in"), 16 * DB * NPG)
                    else:
                        values(b - 1)
                values(DB - 1)

            def post(g, s):
                mp = norm_at("post", g, s)
                token_sums(g, "ss_p", 8 * mp + 8)
                spread(r_at(g, SPOST[s]), g)
                if s < 3:
                    for n in range(NB):
                        block_sum(n, g, "sq_m", "ss_m", 3 * g + s)
                    spread(r_at(g, SPRE[s]), g)

            def gate(g):
                ph = phase("u", g)
                pe.wait_ge(S("ws_m"), 2 * g + 2)
                for q in range(8):
                    pe.transpose(PS[:, 4 + q // 4, P * (q % 4):P * (q % 4) + P], WS[:, q, :], IDENT)
                for q in range(8):
                    mm = pe.transpose(PS[0:NS, 6, NS * q:NS * q + NS], WS8[:, q, :], IDENT[0:NS, 0:NS])
                mm.then_inc(S("ws_t"), 1)
                for local in range(8):
                    chunk(ph, local // 2, local % 2, a_hi, a_lo)
                    if local == 0:
                        pe.wait_ge(S("wmt"), g + 1)
                        pe.wait_ge(S("lv"), 8 * g + 9)
                        for b, lo, hi in halves(g):
                            mm = pe.matmul(PS[:, 4 + b, 0:hi - lo], ONES, SS[:, lo:hi], start=True, stop=True)
                        mm.then_inc(S("mean"), 1)
                    if 2 <= local <= 4:
                        for n in range(3 * local - 6, min(3 * local - 3, NB)):
                            block_sum(n, g, "ln_sq", "ln_ss", g)
                    if local == 5:
                        spread(r_at(g, 4), g)

                def turn(n):
                    x = 1 - n % 2
                    pe.wait_ge(S("ln_z"), 8 * g + n + 1)
                    if n == 1:
                        pe.wait_ge(S("ln_t"), 8 * g + 8)
                    if n >= 2:
                        pe.wait_ge(S("zc_d" if n % 2 == 0 else "zc_a"), 4 * g + n // 2)
                    for k, lo, w in tiles(g):
                        mm = pe.transpose(PSF[0:w, (4 + 2 * x) * 512 + lo:(4 + 2 * x) * 512 + lo + P], Y[:, n, lo:lo + w], IDENT)
                    mm.then_inc(S("z_ps"), 1)

                for p in (0, 1):
                    pe.wait_ge(S(f"free_a{p}"), ph.end["a", p])
                turn(0)
                turn(1)
                for n in range(NB):
                    if n + 2 < NB:
                        turn(n + 2)
                    pe.wait_ge(S("zc_d" if n % 2 == 0 else "zc_a"), 4 * g + n // 2 + 1)
                    wait(pe, S("s_b"), 8 * g + n - 1)
                    for k in range(4):
                        mm = pe.matmul(PS[:, 2 * (n % 2), P * k:P * k + P], ZN[:, k, P * n:P * n + P], WMT[:, n, :], start=True, stop=True)
                    if g:
                        mm = pe.matmul(PS[:, 2 * (n % 2) + 1, 0:NS], ZN[0:NS, 4, P * n:P * n + P], WM8T[:, n, :], start=True, stop=True)
                    mm.then_inc(S("s_mm"), 1)
                pe.wait_ge(S("s_b"), 8 * g + 8)

            def result(g):
                for k, lo, w in tiles(g):
                    if k == 0:
                        for p in (0, 1):
                            pe.wait_ge(S(f"free_d{p}"), phase("dn", g, 1, 1).end["d", p])
                    if k >= 2:
                        pe.wait_ge(S("y_cp"), 4 * g + k - 1)
                    for n in range(NB):
                        if k == 0:
                            pe.wait_ge(S("x_new"), 8 * (4 * g + 3) + n + 1)
                        mm = pe.transpose(PS[0:w, 2 * (k % 2) + n // 4, P * (n % 4):P * (n % 4) + P], X[:, n, lo:lo + w], IDENT)
                    mm.then_inc(S("y_ps"), 1)

            pe.wait_ge(S("c_in"), 16)
            pe.wait_ge(S("g_in"), 16 * 9)
            pe.transpose(PS[:, 6, 0:84], GN[:], IDENT[0:84, 0:84]).then_inc(S("setup_pe"), 1)
            for pg in range(4):
                pe.transpose(PS[:, 7, P * pg:P * pg + DB * BUF], SPN[:, P * pg:P * pg + P],
                             IDENT[0:DB * BUF, 0:DB * BUF]).then_inc(S("setup_pe"), 1)
            pe.wait_ge(S("setup_a"), 5)
            load_x(0)
            in_stage(0)
            index(0)
            load_x(1)
            in_stage(1)
            index(1)
            index_sample()
            for g in range(2):
                attend(g)
                if g:
                    attend_sample()
                    pe.wait_ge(S("osc"), 1)
                    pe.wait_ge(S("exps"), 8)
                pe.wait_ge(S("exp"), 32 * g + 32)
                pe.wait_ge(S("o_lo"), 8 * g + 8)
                pe.wait_ge(S("pool_in"), 32 * g + 32)
                linear(phase("out", g))
                post(g, 0)
                for layer in range(2):
                    for half in range(2):
                        if half == 0:
                            linear(phase("gu", g, layer, 0), a_at_(g, 0 if layer == 0 else 3))
                        else:
                            linear(phase("gu", g, layer, 1))
                        down_ph = phase("dn", g, layer, half)
                        down(down_ph)
                    if layer == 0:
                        post(g, 1)
                        linear(phase("v", g), a_at_(g, 1))
                        gate(g)
                        linear(phase("oo", g), a_at_(g, 2))
                        post(g, 2)
                    else:
                        post(g, 3)
                result(g)

        @block.scalar
        def _(act):
            def hi_part(ph, i, p):
                wait(act, S(f"w_in{p}"), ph.win[p] + 16 * ph.nd * (i + 1))
                n = ph.kt * P
                act.activation(WH[:, p, 0:n], WR[:, p, 0:n], ACT.Copy).then_inc(S("w_hi"), 1)

            def loop(ph, take):
                def body(i, last):
                    for p in (0, 1):
                        wait(act, S("w_used"), ph.c0 + 2 * i + p + 1)
                        if not last:
                            hi_part(ph, i + 1, p)
                        elif ph.next:
                            hi_part(ph.next, 0, p)
                        take(i, p)
                with act.Fori(0, ph.iters - 1) as i:
                    body(i, False)
                body(ph.iters - 1, True)

            def warm(func):
                act.activation(MX[0:1, 3, 0:1], const("ident")[0:1, 0:1], func).then_inc(S("warm"), 1)

            def root(r, g):
                act.wait_ge(S("n_sum"), r + 1)
                for lo, hi, w in ((0, 4, P), (4, 5, NS)):
                    if lo < NT[g]:
                        ins_ = act.activation(RT[0:w, 0, lo:hi], PS[0:w, 6, 2 * lo:2 * hi].rearrange("p (k a) -> p k a", a=2)[:, :, 0],
                                              ACT.Sqrt, scale=1.0 / D, bias=EPS)
                ins_.then_inc(S("n_rt"), 1)

            def split(a, n, g):
                act.wait_ge(S("a_t"), 8 * a + n + 1)
                act.activation(AR[:, 0, n, 0:T[g]], TT[:, n % 2, 0:T[g]], ACT.Copy).then_inc(S("a_hi"), 1)

            def load_x(g):
                dst = Y if g else X
                if g:
                    act.wait_ge(S("s_acc"), 16)
                for n in range(NB):
                    act.wait_ge(S("xt_ps"), 8 * g + n + 1)
                    wait(act, S("ss_p"), 8 * g + n - 1)
                    src = PSF[:, 1024 * (n % 2):1024 * (n % 2) + T[g]]
                    act.activation(SQ[:, n % 2, 0:T[g]], src, ACT.Square).then_inc(S("sq_p"), 1)
                    act.activation(dst[:, n, 0:T[g]], src, ACT.Copy).then_inc(S("xt_cp"), 1)
                if g == 0:
                    for p in (0, 1):
                        hi_part(phase("in", 0), 0, p)
                root(g, g)
                for n in range(NB):
                    split(g, n, g)

            def in_stage(g):
                ph = phase("in", g)
                for local in range(16):
                    p = local % 2
                    act.wait_ge(S("w_used"), ph.c0 + local + 1)
                    if local < 14:
                        hi_part(ph, (local + 2) // 2, p)
                    else:
                        hi_part(ph.next, 0, p)
                    free = S(f"free_a{p}")
                    if local < 12:
                        if local >= 2:
                            r = 10 * g + local - 2
                            act.wait_ge(S("rope_sw"), r + 1)
                            act.wait_ge(S("rope_t2"), r + 1)
                        act.activation(hv(SQ[:, p, 0:T[g]], g), lin(p, g), ACT.Copy).then_inc(free, 1)
                    else:
                        pg = local - 12
                        act.wait_ge(S("halo"), g + 1)
                        if g == 0:
                            act.activation(XPE[:, pg, BUF:BUF + 512], PS[:, 2 * p, :], ACT.Copy).then_inc(free, 1)
                        else:
                            act.activation(XPE[:, pg, BUF:BUF + 288], PS[:, 2 * p, 0:288], ACT.Copy)
                            act.activation(XPE[:, pg, BUF + 288:BUF + 512], PS[:, 2 * p + 1, 0:224], ACT.Copy)
                            dst = XPE[:, pg, BUF + 512:EXT].rearrange("p (b r) -> p b r", b=DB)[:, :, BUF:]
                            act.activation(dst, PS[:, 2 * p + 1, 224:288].rearrange("p (b t) -> p b t", b=DB), ACT.Copy).then_inc(free, 1)
                    if local == 12:
                        if g:
                            act.wait_ge(S("kv_out"), 16 * 12)
                        act.wait_ge(S("nat"), 4 * g + 1)
                        for lo, hi, w in ((0, 4, P), (4, 5, NS)):
                            if lo < NT[g]:
                                ins_ = act.activation(KN[0:w, lo:hi, :], PSF[0:w, 2048 + P * lo:2048 + P * hi].rearrange("p (k d) -> p k d", d=P), ACT.Copy)
                        ins_.then_inc(S("nat_a"), 1)
                        act.wait_ge(S("nat"), 4 * g + 2)
                        for lo, hi, w in ((0, 4, P), (4, 5, NS)):
                            if lo < NT[g]:
                                ins_ = act.activation(IKN[0:w, lo:hi, :], PSF[0:w, 3072 + P * lo:3072 + P * hi].rearrange("p (k d) -> p k d", d=P)[:, :, 0:HD], ACT.Copy)
                        ins_.then_inc(S("nat_a"), 1)
                    if local == 13:
                        act.wait_ge(S("nat"), 4 * g + 3)
                        for lo, hi, w in ((0, 4, P), (4, 5, NS)):
                            if lo < NT[g]:
                                ins_ = act.activation(VN[0:w, 4 * g + lo:4 * g + hi, :], PSF[0:w, 2048 + P * lo:2048 + P * hi].rearrange("p (k d) -> p k d", d=P), ACT.Copy)
                        ins_.then_inc(S("nat_a"), 1)
                for pg in range(4):
                    act.wait_ge(S("pool_mm"), 4 * g + pg + 1)
                    wait(act, S("pool_out"), 16 * (4 * g + pg))
                    act.activation(hv(PHL[:, 0, 0:T[g]], g), aux(pg % 2, g), ACT.Identity,
                                   scale=GC[:, G_POOL + pg:G_POOL + pg + 1]).then_inc(S("pool_hi"), 1)
                if g:
                    act.wait_ge(S("xp_ps"), 1)
                    act.activation(XNS[0:BUF, 0, :], PS[0:BUF, 0, :], ACT.Copy)
                    act.activation(XNS[0:NS, 1, :], PS[0:NS, 1, :], ACT.Copy).then_inc(S("xp_rows"), 1)

            def index(g):
                ph = phase("in", g)
                n = 512 * (g + 1)
                if g:
                    act.wait_ge(S("x_out"), 16)
                act.wait_ge(S("w_used"), ph.c0 + 16)
                act.activation(IKS[:, 0, 0:n], IKT[:, 0:n], ACT.Copy).then_inc(S("ik_hi"), 1)
                for u, t in zip(IDX_U[g], IDX_T[g]):
                    at = slice(P * (t - 4 * g), P * (t - 4 * g) + P)
                    wait(act, S("idx_mm"), 8 * (u - 1))
                    act.activation(IQS[0:64, u % 2, 0:4, :], IQ[0:64, :, at], ACT.Copy)
                    act.activation(IQS[64:128, u % 2, 4:8, :], IQ[64:128, :, at], ACT.Copy).then_inc(S("iq_hi"), 1)
                    m = P * (t + 1)
                    k = 1 if m <= 512 else 2
                    for h in range(8):
                        act.wait_ge(S("idx_mm"), 8 * u + h + 1)
                        wait(act, S("s_acc"), 8 * u + h - 1)
                        act.activation(R[:, h % 2, 0:m].rearrange("p (c n) -> p c n", c=k),
                                       PS[:, 4 + 2 * (h % 2):4 + 2 * (h % 2) + k, 0:m // k],
                                       ACT.Relu, scale=HD ** -0.5).then_inc(S("idx_r"), 1)

            def index_sample():
                act.wait_ge(S("iqz0"), 1)
                src = IQ[:, :, 512:T[1]].rearrange("p j (b t) -> p j b t", b=DB)
                dst = IQZ[:].rearrange("p b (a j t) -> p a j b t", a=2, j=4)
                for j in range(4):
                    act.activation(dst[0:64, 0, j], src[0:64, j], ACT.Copy)
                    ins_ = act.activation(dst[64:128, 1, j], src[64:128, j], ACT.Copy)
                ins_.then_inc(S("iqz"), 1)
                act.wait_ge(S("s_acc"), 48)
                for b in range(DB + 1):
                    if b < DB:
                        act.wait_ge(S("ikt_ps"), b + 1)
                        wait(act, S("rel_mm"), b - 1)
                        act.activation(IKTB[b % 2][:], PS[:, b % 2, :], ACT.Copy).then_inc(S("ikt_cp"), 1)
                    if b:
                        act.wait_ge(S("rel_mm"), b)
                        wait(act, S("mix_mm"), b - 2)
                        act.activation(RS[:, (b - 1) % 2, :], PSF[0:NS, 1024:1024 + KCOL], ACT.Relu, scale=HD ** -0.5).then_inc(S("rs"), 1)

            def attend(g):
                n = 512 * (g + 1)
                if g == 0:
                    act.wait_ge(S("mix_mm"), DB)
                    act.wait_ge(S("kv_out"), 16 * 27)
                    act.wait_ge(S("st_out"), 16 * 10)
                else:
                    act.wait_ge(S("y_out"), 64)
                for kv in range(2):
                    for r in range(2):
                        act.activation(KS[64 * r:64 * r + 64, kv, 0, 0:n], KT[64 * kv:64 * kv + 64, 0:n], ACT.Copy)
                act.activation(VS[:, 0, 0:4 * (g + 1), :], VN[:, 0:4 * (g + 1), :], ACT.Copy).then_inc(S("ks_hi"), 1)

                def queries(t, half):
                    r = slice(64 * half, 64 * half + 64)
                    act.wait_ge(S("q_in"), 16 * (t + 1))
                    if t:
                        act.wait_ge(S("qk_mm"), 8 * (t - 1) + 4 * half + 4)
                    act.activation(QST[r, 4 * half:4 * half + 4, :], QR[r, :, :], ACT.Copy).then_inc(S("qst_hi"), 1)

                queries(4 * g, 0)
                queries(4 * g, 1)
                for kind, t, z in items(g):
                    if kind == "qk":
                        hh = 8 * t + z
                        if z == 6 and t % 4 < 3:
                            queries(t + 1, 0)
                        if z == 0 and t % 4 > 0:
                            queries(t, 1)
                        act.wait_ge(S("nm"), hh + 1)
                        if hh - RING >= 0:
                            ot, oh = divmod(hh - RING, 8)
                            act.wait_ge(S("p_tr"), kbase(ot, oh // 4) + ot + 1)
                        act.activation(cut(PR[:, hh % RING, 0:P * (t + 1)], t), logits(z % 2, t), ACT.Exp,
                                       bias=MX[:, 1, hh % 16:hh % 16 + 1], scale=HD ** -0.5,
                                       accum_out=MX[:, 2, hh % 16:hh % 16 + 1]).then_inc(S("exp"), 1)
                        continue
                    kv, k0 = z, kbase(t, z)
                    for kk in range(t + 1):
                        kc = k0 + kk
                        act.wait_ge(S("p_tr"), kc + 1)
                        wait(act, S("pv_mm"), kc - 1)
                        act.activation(PT[:, kc % 2, 0, :], PS[:, 4 + kc % 2, :], ACT.Copy).then_inc(S("pt_hi"), 1)
                    act.wait_ge(S("pv_mm"), k0 + t + 1)
                    if t == 4 * g and kv == 0 and g == 0:
                        act.wait_ge(S("mix_mm"), DB)
                    at = slice(P * (t - 4 * g), P * (t - 4 * g) + P)
                    act.activation(AR[64 * kv:64 * kv + 64, 0, 0:4, at],
                                   PS[64 * kv:64 * kv + 64, 6 + kv, :].rearrange("p (j q) -> p j q", j=4), ACT.Copy).then_inc(S("o_hi"), 1)

            def attend_sample():
                act.wait_ge(S("q_in"), 16 * 9)
                act.wait_ge(S("qz0"), 1)
                src = QR[:, :, 0:NS].rearrange("p j (b t) -> p j b t", b=DB)
                dst = QZ[:].rearrange("p b (a j t) -> p a j b t", a=2, j=4)
                for j in range(4):
                    act.activation(dst[0:64, 0, j], src[0:64, j], ACT.Copy)
                    ins_ = act.activation(dst[64:128, 1, j], src[64:128, j], ACT.Copy)
                ins_.then_inc(S("qz"), 1)

                def page_keys(b):
                    act.wait_ge(S("kt_ps"), b + 1)
                    wait(act, S("qks_mm"), b - 1)
                    act.activation(KTB[:, b % 2, :], PS[:, 4 + b % 2, :], ACT.Copy).then_inc(S("ktb"), 1)

                def turned(b):
                    act.wait_ge(S("ps_tr"), b + 1)
                    wait(act, S("pvs_mm"), b - 1)
                    act.activation(PTS[:, b % 2, 0:NS * NPG], PS[:, 6, 0:NS * NPG], ACT.Copy)
                    act.activation(PTS[0:NS, b % 2, NS * NPG:NS * NPG + NS], PS[0:NS, 6, NS * NPG:NS * NPG + NS], ACT.Copy).then_inc(S("pts"), 1)

                page_keys(0)
                for b in range(DB):
                    if b + 1 < DB:
                        page_keys(b + 1)
                    act.wait_ge(S("nms"), b + 1)
                    wait(act, S("ps_tr"), b - 1)
                    act.activation(PRS[:, b % 2, :], PSF[0:NS, 1024 * (b % 2):1024 * (b % 2) + KCOL], ACT.Exp,
                                   bias=MX[0:NS, 1, b:b + 1], scale=HD ** -0.5, accum_out=MX[0:NS, 2, b:b + 1]).then_inc(S("exps"), 1)
                    if b:
                        turned(b - 1)
                turned(DB - 1)
                act.wait_ge(S("pvs_mm"), DB)
                for half in range(2):
                    r = slice(64 * half, 64 * half + 64)
                    for j in range(4):
                        ins_ = act.activation(AR[r, 0, j, 512:T[1]].rearrange("p (b t) -> p b t", b=DB),
                                              PS[r, 7, :].rearrange("p (b h t) -> p h b t", b=DB, h=8)[:, 4 * half + j], ACT.Copy)
                ins_.then_inc(S("osc_hi"), 1)

            def out_like(ph, mp):
                g = ph.g

                def take(i, p):
                    n = 2 * i + p
                    wait(act, S("ss_p"), 8 * mp + n - 1)
                    act.activation(hv(SQ[:, p, 0:T[g]], g), lin(p, g), ACT.Square).then_inc(S("sq_p"), 1)
                    act.activation(hv(flat(Y[:, ds(n, 1), 0:T[g]]), g), lin(p, g), ACT.Copy).then_inc(S(f"free_a{p}"), 1)
                loop(ph, take)

            def gate_up(ph):
                g = ph.g
                if g and ph.layer:
                    act.wait_ge(S("z_out"), 16)

                def take(i, p):
                    if p == 0:
                        wait(act, S("free_d1"), ph.base["d", 1] + i)
                        act.activation(hv(TT[:, 0, 0:T[g]], g), lin(0, g), ACT.Silu).then_inc(S("free_a0"), 1)
                    else:
                        wait(act, S("free_d1"), ph.base["d", 1] + i + 1)
                        act.activation(flat(HR[:, 0, ds(i, 1), 0:T[g]]), TT[:, 1, 0:T[g]], ACT.Copy).then_inc(S("h_hi"), 1)
                warm(ACT.Silu)
                loop(ph, take)

            def down(ph, mp):
                g = ph.g

                def first(i, p):
                    act.activation(hv(flat(Y[:, ds(2 * i + p, 1), 0:T[g]]), g), lin(p, g), ACT.Copy).then_inc(S(f"free_a{p}"), 1)

                def second(i, p):
                    n = 2 * i + p
                    wait(act, S(f"free_d{p}"), ph.base["d", p] + i + 1)
                    wait(act, S("ss_p"), 8 * mp + n - 1)
                    act.activation(SQ[:, p, 0:T[g]], flat(Y[:, ds(n, 1), 0:T[g]]), ACT.Square).then_inc(S("sq_p"), 1)
                loop(ph, second if ph.half else first)

            def post(g, s):
                root(r_at(g, SPOST[s]), g)
                if s == 3:
                    return
                m = 3 * g + s
                for n in range(NB):
                    act.wait_ge(S("x_new"), 8 * (4 * g + s) + n + 1)
                    if n >= 2:
                        act.wait_ge(S("ss_m"), 7 * m + n - 1)
                    act.activation(SQ[:, n % 2, 0:T[g]], X[:, n, 0:T[g]], ACT.Square).then_inc(S("sq_m"), 1)
                root(r_at(g, SPRE[s]), g)
                for n in range(NB):
                    split(a_at_(g, SA_[s]), n, g)

            def gate(g):
                ph = phase("v", g)
                warm(ACT.Gelu)

                def take(i, p):
                    act.activation(hv(flat(Y[:, ds(2 * i + p, 1), 0:T[g]]), g), lin(p, g), ACT.Gelu).then_inc(S(f"free_a{p}"), 1)
                loop(ph, take)
                act.wait_ge(S("ws_t"), g + 1)
                act.activation(WMT[:].rearrange("p g s -> p (g s)"), PSF[:, 2048:3072], ACT.Copy)
                act.activation(WM8T[:].rearrange("p g s -> p (g s)"), PS[0:NS, 6, :], ACT.Copy).then_inc(S("wmt"), 1)
                ph = phase("u", g)

                def centred(n):
                    act.wait_ge(S("ln_c"), 8 * g + n + 1)
                    if n >= 2:
                        act.wait_ge(S("ln_ss"), 7 * g + n - 1)
                    act.activation(SQ[:, n % 2, 0:T[g]], Y[:, n, 0:T[g]], ACT.Square).then_inc(S("ln_sq"), 1)

                def scaled(n):
                    act.wait_ge(S("ln_t"), 8 * g + n + 1)
                    act.activation(Y[:, n, 0:T[g]], TT[:, n % 2, 0:T[g]], ACT.Identity, scale=gain(G_LN, 0, n),
                                   bias=gain(B_LN, 0, n)).then_inc(S("ln_z"), 1)

                for local in range(8):
                    p = local % 2
                    act.wait_ge(S("w_used"), ph.c0 + local + 1)
                    if local < 6:
                        hi_part(ph, (local + 2) // 2, p)
                    else:
                        hi_part(ph.next, 0, p)
                    act.activation(hv(U[:, local, 0:T[g]], g), lin(p, g), ACT.Gelu).then_inc(S(f"free_a{p}"), 1)
                    if 1 <= local <= 3:
                        for n in range(3 * local - 3, min(3 * local, NB)):
                            centred(n)
                    if local == 4:
                        root(r_at(g, 4), g)
                    if local >= 6:
                        for n in range(4 * local - 24, 4 * local - 20):
                            scaled(n)
                a = a_at_(g, 2)
                for n in range(NB):
                    if n % 2:
                        act.wait_ge(S("z_ps"), 8 * g + n + 1)
                        z_rows(act, g, n).then_inc(S("zc_a"), 1)
                    if n >= 2:
                        split(a, n - 2, g)
                split(a, 6, g)
                split(a, 7, g)

            def z_rows(eng, g, n):
                x = 1 - n % 2
                base = (4 + 2 * x) * 512
                ins_ = eng.activation(ZN[:, 0:4, P * n:P * n + P], PSF[:, base:base + 512].rearrange("p (k d) -> p k d", d=P), ACT.Copy)
                if g:
                    ins_ = eng.activation(ZN[0:NS, 4, P * n:P * n + P], PSF[0:NS, base + 512:base + 512 + P], ACT.Copy)
                return ins_

            def result(g):
                for k, lo, w in tiles(g):
                    act.wait_ge(S("y_ps"), 4 * g + k + 1)
                    act.activation(ON[0:w, k, :], PSF[0:w, 1024 * (k % 2):1024 * (k % 2) + D], ACT.Copy).then_inc(S("y_cp"), 1)

            act.wait_ge(S("setup_pe"), 1)
            act.activation(GC[:], PS[:, 6, 0:84], ACT.Copy).then_inc(S("setup_a"), 1)
            act.wait_ge(S("setup_d"), 4)
            act.wait_ge(S("setup_pe"), 5)
            for pg in range(4):
                act.activation(XPE[:, pg, BUF + 512:EXT].rearrange("p (b r) -> p b r", b=DB)[:, :, 0:BUF],
                               PS[:, 7, P * pg:P * pg + DB * BUF].rearrange("p (b r) -> p b r", b=DB), ACT.Copy).then_inc(S("setup_a"), 1)
            load_x(0)
            in_stage(0)
            index(0)
            load_x(1)
            in_stage(1)
            index(1)
            index_sample()
            for g in range(2):
                attend(g)
                if g:
                    attend_sample()
                out_like(phase("out", g), norm_at("post", g, 0))
                post(g, 0)
                for layer in range(2):
                    for half in range(2):
                        gate_up(phase("gu", g, layer, half))
                        down(phase("dn", g, layer, half), norm_at("post", g, 1 + 2 * layer))
                    if layer == 0:
                        post(g, 1)
                        gate(g)
                        out_like(phase("oo", g), norm_at("post", g, 2))
                        post(g, 2)
                    else:
                        post(g, 3)
                result(g)

        @block.gpsimd
        def _(pool):
            def lo_part(ph, i, p):
                wait(pool, S("w_hi"), ph.c0 + 2 * i + p + 1)
                n = ph.kt * P
                pool.tensor_tensor(WL[:, p, 0:n], WR[:, p, 0:n], WH[:, p, 0:n].bitcast(F32), ALU.subtract).then_inc(S("w_lo"), 1)

            def loop(ph):
                with pool.Fori(0, ph.iters - 1) as i:
                    lo_part(ph, i + 1, 0)
                    lo_part(ph, i + 1, 1)
                if ph.next:
                    lo_part(ph.next, 0, 0)
                    lo_part(ph.next, 0, 1)

            def split(a, n, g):
                pool.wait_ge(S("a_hi"), 8 * a + n + 1)
                pool.tensor_tensor(AR[:, 1, n, 0:T[g]], TT[:, n % 2, 0:T[g]], AR[:, 0, n, 0:T[g]].bitcast(F32), ALU.subtract).then_inc(S("a_lo"), 1)

            def in_stage(g):
                ph = phase("in", g)
                pool.wait_ge(S("rope_in"), 16 * (g + 1))
                for local in range(16):
                    p = local % 2
                    if local < 14:
                        lo_part(ph, (local + 2) // 2, p)
                    else:
                        lo_part(ph.next, 0, p)
                    if local < 10:
                        r = 10 * g + local
                        pool.wait_ge(S(f"free_a{p}"), ph.base["a", p] + local // 2 + 1)
                        wait(pool, S("rope_out"), r)
                        pool.tensor_tensor(TT[:, 1, 0:T[g]], SQ[:, p, 0:T[g]], RP[:, 0, 0:T[g]], ALU.mult).then_inc(S("rope_t2"), 1)

            def index(g):
                pool.wait_ge(S("w_lo"), phase("in", g).c0 + 18)
                for u, t in zip(IDX_U[g], IDX_T[g]):
                    at = slice(P * (t - 4 * g), P * (t - 4 * g) + P)
                    pool.wait_ge(S("iq_hi"), u + 1)
                    for half in range(2):
                        r, o = slice(64 * half, 64 * half + 64), slice(64 - 64 * half, 128 - 64 * half)
                        pool.tensor_tensor(IQS[o, u % 2, 4 * half:4 * half + 4, :], IQ[r, :, at],
                                           IQS[r, u % 2, 4 * half:4 * half + 4, :].bitcast(F32), ALU.subtract).then_inc(S("iq_lo"), 1)
                        pool.wait_ge(S("iq_lo"), 2 * u + half + 1)

            def attend(g):
                pool.wait_ge(S("w_lo"), phase("out", g).c0 + 2)
                for t in range(4 * g, 4 * g + 4):
                    for half in range(2):
                        r, o = slice(64 * half, 64 * half + 64), slice(64 - 64 * half, 128 - 64 * half)
                        pool.wait_ge(S("qst_hi"), 2 * t + half + 1)
                        pool.tensor_tensor(QST[o, 4 * half:4 * half + 4, :], QR[r, :, :],
                                           QST[r, 4 * half:4 * half + 4, :].bitcast(F32), ALU.subtract).then_inc(S("qst_lo"), 1)
                        pool.wait_ge(S("qst_lo"), 2 * t + half + 1)

            def post(g, s):
                if s == 3:
                    return
                for n in range(NB):
                    split(a_at_(g, SA_[s]), n, g)

            for p in (0, 1):
                lo_part(phase("in", 0), 0, p)
            for n in range(NB):
                split(0, n, 0)
            in_stage(0)
            index(0)
            for n in range(NB):
                split(1, n, 1)
            in_stage(1)
            index(1)
            for g in range(2):
                attend(g)
                loop(phase("out", g))
                post(g, 0)
                for layer in range(2):
                    for half in range(2):
                        loop(phase("gu", g, layer, half))
                        loop(phase("dn", g, layer, half))
                    if layer == 0:
                        post(g, 1)
                        loop(phase("v", g))
                        ph = phase("u", g)
                        for local in range(8):
                            if local < 6:
                                lo_part(ph, (local + 2) // 2, local % 2)
                            else:
                                lo_part(ph.next, 0, local % 2)
                        for n in range(NB):
                            split(a_at_(g, 2), n, g)
                        loop(phase("oo", g))
                        post(g, 2)

        @block.vector
        def _(dve):
            def sum_zero(z):
                dve.memset(SS[:], 0.0).then_inc(S("ss_zero"), 1)

            def add_square(mp, n, p, g, z):
                wait(dve, S("sq_p"), 8 * mp + n + 1)
                wait(dve, S("ss_p"), 8 * mp + n)
                dve.wait_ge(S("ss_zero"), z + 1)
                dve.tensor_tensor(SS[:, 0:T[g]], SS[:, 0:T[g]], SQ[:, p, 0:T[g]], ALU.add).then_inc(S("ss_p"), 1)

            def diagonals(r, g):
                dve.wait_ge(S("n_rt"), r + 1)
                dve.reciprocal(RT[:, 1, 0:NT[g]], RT[:, 0, 0:NT[g]]).then_inc(S("n_rc"), 1)
                dve.wait_ge(S("n_rc"), r + 1)
                for k in range(NT[g]):
                    ins_ = dve.tensor_scalar(DG[:, k, :], IDENT, RT[:, 1, k:k + 1], None, ALU.mult)
                ins_.then_inc(S("n_dg"), 1)

            def spread(g):
                return PSF[:, 2048:2048 + T[g]]

            def split(a, g, src, base, layer):
                for n in range(NB):
                    wait(dve, S("a_lo"), 8 * a + n - 1)
                    dve.scalar_tensor_tensor(out=TT[:, n % 2, 0:T[g]], in0=src[:, n, 0:T[g]], scalar=gain(base, layer, n),
                                             in1=spread(g), op0=ALU.mult, op1=ALU.mult).then_inc(S("a_t"), 1)

            def load_x(g):
                sum_zero(g)
                for n in range(NB):
                    add_square(g, n, n % 2, g, g)
                diagonals(g, g)
                dve.wait_ge(S("n_b"), g + 1)
                dve.wait_ge(S("xt_cp"), 8 * g + 8)
                split(g, g, Y if g else X, G_MIX_PRE, 0)

            rounds = [0]

            def top_round(spans, r):
                wait(dve, S("top"), 2 * r)
                for m, s in spans:
                    ins_ = dve.max(M8[0:s.shape[0], m, :], s)
                ins_.then_inc(S("top"), 1)
                wait(dve, S("top"), 2 * r + 1)
                for m, s in spans:
                    ins_ = dve.match_replace(out=s, in_to_replace=M8[0:s.shape[0], m, :], in_values=s, imm_value=CHOSEN)
                ins_.then_inc(S("top"), 1)

            def in_stage(g):
                ph = phase("in", g)
                if g:
                    dve.tensor_copy(XPE[:, :, 0:BUF], XPE[:, :, 512:512 + BUF]).then_inc(S("halo"), 1)

                def pool_windows(pg):
                    w = POOLW[pg]
                    n = EXT if g else BUF + 512
                    p = pg % 2
                    dve.wait_ge(S(f"free_a{p}"), ph.base["a", p] + 7 + pg // 2)
                    dve.wait_ge(S("nat"), 4 * g + 4)
                    src = XPE[:, pg, 0:n]
                    base = sum((q + 2 + (1 if g == 0 else 0)) for q in range(pg)) + (0 if g == 0 else 18)
                    step = 1
                    count = base
                    for q in range(pg + 1):
                        dst = (PA, PB)[q % 2]
                        n -= step
                        if q:
                            dve.wait_ge(S("win"), count)
                        dve.tensor_tensor(dst[:, 0:n], src[:, 0:n], src[:, step:step + n], ALU.add).then_inc(S("win"), 1)
                        count += 1
                        src = dst
                        step *= 2
                    dve.wait_ge(S("win"), count)
                    if pg >= 2:
                        dve.wait_ge(S("pool_mm"), 4 * g + pg - 1)
                    else:
                        dve.wait_ge(S(f"q_out{pg}"), 16 * (2 * g + 2))
                    first = 16 - w
                    ins_ = dve.scalar_tensor_tensor(out=PD[:, p, 0:512], in0=src[:, first:first + 512], scalar=1.0 / w,
                                                    in1=XPE[:, pg, BUF:BUF + 512], op0=ALU.mult, op1=ALU.subtract)
                    if g == 0:
                        a = CN["inv"][0] + 16 * pg
                        ins_.then_inc(S("win"), 1)
                        dve.tensor_tensor(T16[:], src[:, first:first + 16], CT[:, a:a + 16], ALU.mult).then_inc(S("win"), 1)
                        dve.wait_ge(S("win"), count + 2)
                        ins_ = dve.tensor_tensor(PD[:, p, 0:16], T16[:], XPE[:, pg, BUF:BUF + 16], ALU.subtract)
                    else:
                        ins_.then_inc(S("win"), 1)
                        ins_ = dve.scalar_tensor_tensor(out=PD[:, p, 512:T[1]].rearrange("p (b t) -> p b t", b=DB), in0=sample_windows(src, first),
                                                        scalar=1.0 / w,
                                                        in1=XPE[:, pg, BUF + 512:EXT].rearrange("p (b r) -> p b r", b=DB)[:, :, BUF:],
                                                        op0=ALU.mult, op1=ALU.subtract)
                    ins_.then_inc(S("pool_d"), 1)

                def sample_windows(src, first):
                    a = BUF + 512
                    return src[:, a:a + DB * (BUF + DT)].rearrange("p (b r) -> p b r", b=DB)[:, :, first:first + DT]

                def pool_lo(pg):
                    dve.wait_ge(S("pool_hi"), 4 * g + pg + 1)
                    dve.scalar_tensor_tensor(out=hv(PHL[:, 1, 0:T[g]], g), in0=aux(pg % 2, g), scalar=GC[:, G_POOL + pg:G_POOL + pg + 1],
                                             in1=hv(PHL[:, 0, 0:T[g]], g).bitcast(F32), op0=ALU.mult, op1=ALU.subtract).then_inc(S("pool_lo"), 1)

                def rotate(local):
                    r, p = 10 * g + local, local % 2
                    dve.wait_ge(S("rope_sw"), r + 1)
                    if local == 0:
                        dve.wait_ge(S("rope_in"), 16 * (g + 1))
                    wait(dve, S("rope_out"), r)
                    dve.tensor_tensor(hv(TT[:, 0, 0:T[g]], g), aux(p, g), hv(RP[:, 1, 0:T[g]], g), ALU.mult).then_inc(S("rope_t1"), 1)
                    dve.wait_ge(S("rope_t1"), r + 1)
                    dve.wait_ge(S("rope_t2"), r + 1)
                    if local < 8:
                        j = local // 2
                        if p == 0:
                            wait(dve, S(f"q_out{j % 2}"), 16 * (2 * g + j // 2))
                            dst = QT[:, j % 2, 0:T[g]]
                        else:
                            dst = IQ[:, j, 0:T[g]]
                    else:
                        dst = (KT, IKT)[p][:, 512 * g:512 * g + T[g]]
                    dve.tensor_tensor(dst, TT[:, 0, 0:T[g]], TT[:, 1, 0:T[g]], ALU.add).then_inc(S("rope_out"), 1)

                spans = [(2, score(2)), (3, score(3))]
                for local in range(16):
                    if local < 10:
                        rotate(local)
                    if local == 13:
                        dve.wait_ge(S("nat"), 4 * g + 4)
                        for lo, hi, w in ((0, 4, P), (4, 5, NS)):
                            if lo < NT[g]:
                                ins_ = dve.tensor_scalar(IW[0:w, 4 * g + lo:4 * g + hi, :],
                                                         PSF[0:w, 3072 + P * lo:3072 + P * hi].rearrange("p (k d) -> p k d", d=P)[:, :, 0:8],
                                                         8 ** -0.5, None, ALU.mult)
                        if g:
                            ins_ = dve.tensor_copy(IWT[:], SQ[0:8, 1, 512:T[1]])
                        ins_.then_inc(S("iw_rows"), 1)
                        pool_windows(0)
                    if local >= 14:
                        pool_windows(local - 13)
                    if local == 15:
                        pool_lo(0)
                    if g and local % 2:
                        for q in range(4):
                            top_round(spans, 4 * (local // 2) + q)
                pool_lo(1)
                pool_windows(3)
                pool_lo(2)
                pool_lo(3)
                if g:
                    dve.tensor_copy(GXS[:].rearrange("p g (b t) -> p g b t", b=DB),
                                    XPE[:, :, BUF + 512:EXT].rearrange("p g (b r) -> p g b r", b=DB)[:, :, :, BUF:]).then_inc(S("xs_cp"), 1)

            def index(g):
                n = 512 * (g + 1)
                dve.wait_ge(S("ik_hi"), g + 1)
                dve.tensor_tensor(IKS[:, 1, 0:n], IKT[:, 0:n], IKS[:, 0, 0:n].bitcast(F32), ALU.subtract).then_inc(S("ik_lo"), 1)
                if g:
                    dve.wait_ge(S("pool_out"), 128)
                    dve.wait_ge(S("xp_rows"), 1)
                for u, t in zip(IDX_U[g], IDX_T[g]):
                    s = score(t)
                    for h in range(8):
                        hh = 8 * u + h
                        dve.wait_ge(S("idx_r"), hh + 1)
                        w = IW[:, t, h:h + 1]
                        r = R[:, h % 2, 0:P * (t + 1)]
                        if h == 0:
                            if u == 0 or u == 2:
                                dve.wait_ge(S("iw_rows"), g + 1)
                            ins_ = dve.tensor_scalar(s, r, w, None, ALU.mult)
                        else:
                            dve.wait_ge(S("s_acc"), hh)
                            ins_ = dve.scalar_tensor_tensor(out=s, in0=r, scalar=w, in1=s, op0=ALU.mult, op1=ALU.add)
                        ins_.then_inc(S("s_acc"), 1)
                    diag = s[:, P * t:P * t + P]
                    dve.wait_ge(S("s_acc"), 8 * u + 8)
                    dve.tensor_tensor(diag, diag, TRIL, ALU.mult).then_inc(S("s_fix"), 1)
                    dve.wait_ge(S("s_fix"), 2 * u + 1)
                    dve.tensor_tensor(diag, diag, const("neg"), ALU.add).then_inc(S("s_fix"), 1)
                dve.wait_ge(S("s_fix"), 2 * IDX_U[g][-1] + 2)

            def index_sample():
                dve.wait_ge(S("spread_mm"), 1)
                g_b = PS[0:NS, 6:7, 0:NS].to_broadcast([NS, DB, NS])
                dve.scalar_tensor_tensor(out=MS[:], in0=const("dm", NS).rearrange("p (b c) -> p b c", b=DB), scalar=8 ** -0.5,
                                         in1=g_b, op0=ALU.mult, op1=ALU.mult).then_inc(S("ms"), 1)
                dve.memset(SCS[:, KCOL:KCOL + 8], DUMMY).then_inc(S("scs"), 1)
                dve.wait_ge(S("mix_mm"), DB)
                dve.tensor_copy(SCS[:, 0:PAST], PS[0:NS, 4, :]).then_inc(S("scs"), 1)
                dve.tensor_tensor(SCS[:, PAST:KCOL], PS[0:NS, 5, 0:NS], const("m01s", NS), ALU.mult).then_inc(S("scs"), 1)
                dve.wait_ge(S("scs"), 3)
                dve.tensor_tensor(SCS[:, PAST:KCOL], SCS[:, PAST:KCOL], const("negs", NS), ALU.add).then_inc(S("scs"), 1)
                dve.wait_ge(S("scs"), 4)

            def attend(g):
                n = 512 * (g + 1)
                dve.wait_ge(S("ks_hi"), g + 1)
                for kv in range(2):
                    src = slice(64 * kv, 64 * kv + 64)
                    for r in range(2):
                        dve.tensor_tensor(KS[64 * r:64 * r + 64, kv, 1, 0:n], KT[src, 0:n], KS[src, kv, 0, 0:n].bitcast(F32), ALU.subtract)
                dve.tensor_tensor(VS[:, 1, 0:4 * (g + 1), :], VN[:, 0:4 * (g + 1), :], VS[:, 0, 0:4 * (g + 1), :].bitcast(F32),
                                  ALU.subtract).then_inc(S("ks_lo"), 1)

                def mask(t):
                    if t >= 2:
                        if t == 2:
                            dve.wait_ge(S("top"), 64)
                        if t == 4:
                            dve.wait_ge(S("top"), 2 * (32 + 17 + 32))
                        if t >= 4:
                            dve.wait_ge(S("qk_mm"), 8 * (t - 1))
                        dve.tensor_scalar(MK[:, t % 2, 0:P * (t + 1)], score(t), SPLITTER, MASK, ALU.is_gt, ALU.mult).then_inc(S("mk"), 1)

                def norm(hh):
                    t = hh // 8
                    dve.wait_ge(S("exp"), hh + 1)
                    c = slice(hh % 16, hh % 16 + 1)
                    dve.reciprocal(MX[:, 3, c], MX[:, 2, c]).then_inc(S("inv"), 1)
                    dve.wait_ge(S("inv"), hh + 1)
                    pr = PR[:, hh % RING, 0:P * (t + 1)]
                    dve.tensor_scalar(pr, pr, MX[:, 3, c], None, ALU.mult).then_inc(S("p_norm"), 1)

                pending = []
                mask(4 * g)
                for kind, t, z in items(g):
                    if kind == "qk":
                        hh = 8 * t + z
                        dve.wait_ge(S("qk_mm"), hh + 1)
                        c = slice(hh % 16, hh % 16 + 1)
                        axes = AX.X if t < 4 else AX.XY
                        src = logits(z % 2, t)
                        if t < 4:
                            src = src.rearrange("p c n -> p (c n)")
                        dve.tensor_reduce(MX[:, 0, c], src, axes, ALU.max).then_inc(S("mx"), 1)
                        dve.wait_ge(S("mx"), hh + 1)
                        dve.tensor_scalar(MX[:, 1, c], MX[:, 0, c], -(HD ** -0.5), None, ALU.mult).then_inc(S("nm"), 1)
                        if z == 6 and t % 4 < 3:
                            mask(t + 1)
                        for q in pending:
                            norm(q)
                        pending = [hh]
                        continue
                    kv, k0 = z, kbase(t, z)
                    for q in pending:
                        norm(q)
                    pending = []
                    for kk in range(t + 1):
                        kc = k0 + kk
                        dve.wait_ge(S("pt_hi"), kc + 1)
                        dve.tensor_tensor(PT[:, kc % 2, 1, :], PS[:, 4 + kc % 2, :], PT[:, kc % 2, 0, :].bitcast(F32), ALU.subtract).then_inc(S("pt_lo"), 1)
                    dve.wait_ge(S("o_hi"), 2 * t + kv + 1)
                    r = slice(64 * kv, 64 * kv + 64)
                    at = slice(P * (t - 4 * g), P * (t - 4 * g) + P)
                    dve.tensor_tensor(AR[r, 1, 0:4, at], PS[r, 6 + kv, :].rearrange("p (j q) -> p j q", j=4),
                                      AR[r, 0, 0:4, at].bitcast(F32), ALU.subtract).then_inc(S("o_lo"), 1)

            def attend_sample():
                dve.wait_ge(S("qk_mm"), 64)
                dve.memset(QZ[:], 0.0).then_inc(S("qz0"), 1)
                dve.tensor_scalar(MKS[:], SCS[:, 0:KCOL], SPLITTER, MASK, ALU.is_gt, ALU.mult).then_inc(S("mks"), 1)
                for b in range(DB):
                    dve.wait_ge(S("qks_mm"), b + 1)
                    dve.tensor_reduce(MX[0:NS, 0, b:b + 1], PSF[0:NS, 1024 * (b % 2):1024 * (b % 2) + KCOL], AX.X, ALU.max).then_inc(S("mxs"), 1)
                    dve.wait_ge(S("mxs"), b + 1)
                    dve.tensor_scalar(MX[0:NS, 1, b:b + 1], MX[0:NS, 0, b:b + 1], -(HD ** -0.5), None, ALU.mult).then_inc(S("nms"), 1)
                    dve.wait_ge(S("exps"), b + 1)
                    dve.reciprocal(MX[0:NS, 3, b:b + 1], MX[0:NS, 2, b:b + 1]).then_inc(S("invs"), 1)
                    dve.wait_ge(S("invs"), b + 1)
                    pr = PRS[:, b % 2, :]
                    dve.tensor_scalar(pr, pr, MX[0:NS, 3, b:b + 1], None, ALU.mult).then_inc(S("ps_norm"), 1)
                dve.wait_ge(S("osc_hi"), 1)
                for half in range(2):
                    r = slice(64 * half, 64 * half + 64)
                    for j in range(4):
                        at = AR[r, 0, j, 512:T[1]].rearrange("p (b t) -> p b t", b=DB)
                        lo = AR[r, 1, j, 512:T[1]].rearrange("p (b t) -> p b t", b=DB)
                        ins_ = dve.tensor_tensor(lo, PS[r, 7, :].rearrange("p (b h t) -> p h b t", b=DB, h=8)[:, 4 * half + j],
                                                 at.bitcast(F32), ALU.subtract)
                ins_.then_inc(S("osc"), 1)

            def out_like(ph, g, s, extra=None):
                mp = norm_at("post", g, s)
                z = z_at(g, SZ[s])
                sum_zero(z)
                with dve.Fori(0, ph.iters) as i:
                    for p in (0, 1):
                        add_square(mp, 2 * i + p, p, g, z)
                        if extra:
                            extra(i, p)

            big = [(m, score(m + 4)) for m in range(4)]
            BIG0 = 32 + 17

            def gate_up(ph, first=None):
                g = ph.g
                with dve.Fori(0, ph.iters) as i:
                    wait(dve, S("w_used"), ph.c0 + 2 * i + 2)
                    wait(dve, S("free_a0"), ph.base["a", 0] + i + 1)
                    wait(dve, S("h_lo"), ph.hb + i)
                    dve.tensor_tensor(hv(TT[:, 1, 0:T[g]], g), lin(1, g), hv(TT[:, 0, 0:T[g]], g), ALU.mult).then_inc(S("free_d1"), 1)
                    wait(dve, S("h_hi"), ph.hb + i)
                    dve.tensor_tensor(flat(HR[:, 1, ds(i, 1), 0:T[g]]), TT[:, 1, 0:T[g]], flat(HR[:, 0, ds(i, 1), 0:T[g]].bitcast(F32)),
                                      ALU.subtract).then_inc(S("h_lo"), 1)
                    if first is not None:
                        top_round(big, first + i)

            def down(ph, s, first=None):
                g = ph.g
                if ph.half == 0:
                    if first is not None:
                        with dve.Fori(0, ph.iters) as i:
                            top_round(big, first + i)
                    return
                mp, z = norm_at("post", g, s), z_at(g, SZ[s])
                sum_zero(z)
                with dve.Fori(0, ph.iters) as i:
                    for p in (0, 1):
                        n = 2 * i + p
                        wait(dve, S("w_used"), ph.c0 + n + 1)
                        y = hv(flat(Y[:, ds(n, 1), 0:T[g]]), g)
                        dve.tensor_tensor(y, lin(p, g), y, ALU.add).then_inc(S(f"free_d{p}"), 1)
                        add_square(mp, n, p, g, z)
                    if first is not None:
                        top_round(big, first + i)

            def post(g, s):
                ph = (phase("out", g), phase("dn", g, 0, 1), phase("oo", g), phase("dn", g, 1, 1))[s]
                r = r_at(g, SPOST[s])
                diagonals(r, g)
                dve.wait_ge(S("n_b"), r + 1)
                for p in (0, 1):
                    dve.wait_ge(S(f"free_{ph.free[p]}{p}"), ph.end[ph.free[p], p])
                base, layer = ((G_MIX_POST, 0), (G_FFN_POST, 0), (G_MIX_POST, 1), (G_FFN_POST, 1))[s]
                q = 8 * (4 * g + s)
                if g and s == 0:
                    dve.wait_ge(S("xb_in"), 16)

                def scale(n):
                    if n >= 2:
                        dve.wait_ge(S("x_new"), q + n - 1)
                    dve.tensor_tensor(TT[:, n % 2, 0:T[g]], Y[:, n, 0:T[g]], spread(g), ALU.mult).then_inc(S("x_t"), 1)

                scale(0)
                for n in range(NB):
                    if n + 1 < NB:
                        scale(n + 1)
                    dve.wait_ge(S("x_t"), q + n + 1)
                    dve.scalar_tensor_tensor(out=X[:, n, 0:T[g]], in0=TT[:, n % 2, 0:T[g]], scalar=gain(base, layer, n),
                                             in1=X[:, n, 0:T[g]], op0=ALU.mult, op1=ALU.add).then_inc(S("x_new"), 1)
                if s == 3:
                    return
                r = r_at(g, SPRE[s])
                diagonals(r, g)
                dve.wait_ge(S("n_b"), r + 1)
                dve.wait_ge(S("x_new"), q + 8)
                base, layer = ((G_FFN_PRE, 0), (G_MIX_PRE, 1), (G_FFN_PRE, 1))[s]
                split(a_at_(g, SA_[s]), g, X, base, layer)

            def gate(g):
                ph = phase("v", g)
                z = z_at(g, 2)
                sum_zero(z)
                dve.wait_ge(S("w_used"), ph.c0)
                dve.memset(WS8[:], 0.0).then_inc(S("ws8_zero"), 1)

                def body(i, p):
                    n = 2 * i + p
                    wait(dve, S(f"free_a{p}"), ph.base["a", p] + i + 1)
                    wait(dve, S("lv"), 8 * g + n + 1)
                    dve.wait_ge(S("ss_zero"), z + 1)
                    dve.tensor_tensor(SS[:, 0:T[g]], SS[:, 0:T[g]], flat(Y[:, ds(n, 1), 0:T[g]]), ALU.add).then_inc(S("lv"), 1)

                with dve.Fori(0, 2) as i:
                    body(i, 0)
                    body(i, 1)
                    if g == 0:
                        top_round(big, BIG0 + 30 + i)
                with dve.Fori(2, 4) as i:
                    body(i, 0)
                    body(i, 1)
                dve.wait_ge(S("ws_in"), 16 * 10 * (g + 1))
                tril = TRIL.unsqueeze(1).to_broadcast([P, 8, P])
                dve.tensor_tensor(WS[:], WS[:], tril, ALU.mult).then_inc(S("ws_m"), 1)
                tril8 = TRIL[0:NS, 0:NS].unsqueeze(1).to_broadcast([NS, 8, NS])
                dve.tensor_tensor(WS8[:], WS8[:], tril8, ALU.mult).then_inc(S("ws_m"), 1)
                dve.wait_ge(S("mean"), g + 1)
                for n in range(NB):
                    dve.scalar_tensor_tensor(out=hv(Y[:, n, 0:T[g]], g), in0=aux(0, g), scalar=-1.0 / D, in1=hv(Y[:, n, 0:T[g]], g),
                                             op0=ALU.mult, op1=ALU.add).then_inc(S("ln_c"), 1)
                diagonals(r_at(g, 4), g)
                dve.wait_ge(S("n_b"), r_at(g, 4) + 1)
                for n in range(NB):
                    wait(dve, S("ln_z"), 8 * g + n - 1)
                    dve.wait_ge(S("ln_c"), 8 * g + n + 1)
                    dve.tensor_tensor(TT[:, n % 2, 0:T[g]], Y[:, n, 0:T[g]], spread(g), ALU.mult).then_inc(S("ln_t"), 1)
                a = a_at_(g, 2)

                def rows(n):
                    if n % 2:
                        return
                    dve.wait_ge(S("z_ps"), 8 * g + n + 1)
                    base = (4 + 2 * (1 - n % 2)) * 512
                    ins_ = dve.tensor_copy(ZN[:, 0:4, P * n:P * n + P], PSF[:, base:base + 512].rearrange("p (k d) -> p k d", d=P))
                    if g:
                        ins_ = dve.tensor_copy(ZN[0:NS, 4, P * n:P * n + P], PSF[0:NS, base + 512:base + 512 + P])
                    ins_.then_inc(S("zc_d"), 1)

                dve.wait_ge(S("ln_z"), 8 * g + 8)
                rows(0)
                for n in range(NB):
                    if n + 2 < NB:
                        rows(n + 2)
                    dve.wait_ge(S("s_mm"), 8 * g + n + 1)
                    bias = BS[:, n:n + 1, :].to_broadcast([P, 4, P])
                    ins_ = dve.tensor_tensor(SQ[:, n % 2, 0:512].rearrange("p (k t) -> p k t", t=P),
                                             PS[:, 2 * (n % 2), :].rearrange("p (k t) -> p k t", t=P), bias, ALU.add)
                    if g:
                        bias8 = BS[:, n:n + 1, 0:DT].to_broadcast([P, DB, DT])
                        ins_ = dve.tensor_tensor(SQ[:, n % 2, 512:T[1]].rearrange("p (b t) -> p b t", b=DB),
                                                 PS[:, 2 * (n % 2) + 1, 0:NS].rearrange("p (b t) -> p b t", b=DB), bias8, ALU.add)
                    ins_.then_inc(S("s_b"), 1)
                    dve.wait_ge(S("s_b"), 8 * g + n + 1)
                    wait(dve, S("a_lo"), 8 * a + n - 1)
                    dve.tensor_tensor(TT[:, n % 2, 0:T[g]], SQ[:, n % 2, 0:T[g]], U[:, n, 0:T[g]], ALU.mult).then_inc(S("a_t"), 1)

            for k, name in enumerate(("free_d0", "free_d1", "h_lo", "lv")):
                dve.memset(T16[:, k:k + 1], 0.0).then_inc(S(name), 1)
            dve.wait_ge(S("c_in"), 16)
            dve.tensor_copy(IDB[:], IDENT).then_inc(S("setup_d"), 1)
            dve.tensor_scalar(MCB[:], TRIL, 1.0, -MASK, ALU.subtract, ALU.mult).then_inc(S("setup_d"), 1)
            dve.wait_ge(S("g_in"), 16 * 9)
            dve.tensor_copy(EB[:].rearrange("p b c -> p (b c)"), EM[0:NS, :]).then_inc(S("setup_d"), 1)
            dve.memset(RT[:], 1.0).then_inc(S("setup_d"), 1)
            dve.wait_ge(S("setup_pe"), 5)
            dve.wait_ge(S("setup_d"), 4)
            dve.memset(XPE[:, :, 0:BUF], 0.0).then_inc(S("halo"), 1)
            load_x(0)
            in_stage(0)
            index(0)
            load_x(1)
            in_stage(1)
            index(1)
            dve.memset(IQZ[:], 0.0).then_inc(S("iqz0"), 1)
            index_sample()
            for g in range(2):
                attend(g)
                if g:
                    attend_sample()
                if g == 0:
                    def sample_rounds(i, p):
                        for q in range(2):
                            top_round([(4, SCS)], 32 + 4 * i + 2 * p + q)
                    out_like(phase("out", 0), 0, 0, sample_rounds)
                    dve.wait_ge(S("top"), 2 * 48)
                    dve.max(M8[0:NS, 4, :], SCS).then_inc(S("top"), 1)
                    dve.wait_ge(S("top"), 2 * 48 + 1)
                    dve.memset(M8[0:NS, 4, TOPK_S % 8:8], DUMMY).then_inc(S("m8_cut"), 1)
                    dve.wait_ge(S("m8_cut"), 1)
                    dve.match_replace(out=SCS, in_to_replace=M8[0:NS, 4, :], in_values=SCS, imm_value=CHOSEN).then_inc(S("top"), 1)
                else:
                    out_like(phase("out", 1), 1, 0)
                post(g, 0)
                at = BIG0
                for layer in range(2):
                    for half in range(2):
                        run = g == 0 and layer == 0
                        gate_up(phase("gu", g, layer, half), at if run else None)
                        at += FH
                        down(phase("dn", g, layer, half), 1 + 2 * layer, at if run else None)
                        at += 4
                    if layer == 0:
                        post(g, 1)
                        gate(g)
                        out_like(phase("oo", g), g, 2)
                        post(g, 2)
                    else:
                        post(g, 3)


_INS = ["x_prompt", "x_sample", "cache_k", "cache_v", "cache_idx_k", "state_pool", "page_table",
        "norm_mix_pre", "norm_mix_post", "norm_ffn_pre", "norm_ffn_post", "w_in_even", "w_out_even",
        "w_pool_group", "pool_scale", "w_in_odd", "sgu_norm_g", "sgu_norm_b", "w_spatial", "b_spatial",
        "w_out_odd", "w_ffn_gate_up", "w_ffn_down"]
_OUTS = [("y_prompt", (1, SEQ, D)), ("y_sample", (DB, DT, D)),
         ("new_k_prompt", (1, 1, SEQ, 2, HD)), ("new_v_prompt", (1, 1, SEQ, 2, HD)),
         ("new_idx_k_prompt", (1, 1, SEQ, HD)), ("new_pool_prompt", (1, 1, BUF, 512)),
         ("new_k_sample", (1, DB, DT, 2, HD)), ("new_v_sample", (1, DB, DT, 2, HD)),
         ("new_idx_k_sample", (1, DB, DT, HD)), ("new_pool_sample", (1, DB, BUF, 512)),
         ("new_sgu_v_sample", (1, DB, DT, D))]


def kernel(**inputs):
    import concourse.bacc as _bacc
    from concourse.bass_utils import run_bass_kernel_spmd as _run

    nc = _bacc.Bacc("TRN2", target_bir_lowering=False, num_devices=1)
    arrays, ins, outs = {}, {}, {}
    table, rope = constants()
    given = {name: np.ascontiguousarray(inputs[name]) for name in _INS}
    given["constants"], given["rope"] = table, rope
    for name, a in given.items():
        arrays[f"in_{name}"] = a
        ins[name] = nc.dram_tensor(f"in_{name}", a.shape, mybir.dt.from_np(a.dtype), kind="ExternalInput").ap()
    for name, shape in _OUTS:
        outs[name] = nc.dram_tensor(f"out_{name}", shape, F32, kind="ExternalOutput").ap()
    build_kernel(nc, ins, outs)
    r = _run(nc, [arrays], core_ids=[0])
    return tuple(r.results[0][f"out_{name}"] for name, _ in _OUTS)
```

```python
from contextlib import ExitStack

import numpy as np

import concourse.bass as bass
from concourse import mybir

F32 = mybir.dt.float32
F32R = mybir.dt.float32r
BF16 = mybir.dt.bfloat16
I32 = mybir.dt.int32
ALU = mybir.AluOpType
ACT = mybir.ActivationFunctionType
AX = mybir.AxisListType
ds = bass.ds

P = 128
D = 1024
NB = D // P
SEQ = 1024
DB, DT = 8, 8
NS = DB * DT
PAST = 512
PAGE = 128
NPG = PAST // PAGE
HEADS, HD = 8, 64
FF = 2816
FH = FF // P // 2
POOLW = (2, 4, 8, 16)
BUF = 15
TOPK_P, TOPK_S = 256, 130
EPS = 1e-6
T = (512, 512 + NS)
HALF = ((1, 512), (2, 288))
NT = (4, 5)
EXT = BUF + 512 + DB * (BUF + DT)
KCOL = PAST + NS
CHOSEN, INVALID, DUMMY, SPLITTER = -3.0e38, -1.0e38, -2.9e38, -2.0e38
MASK = -1.0e30
RING = 8
PGRP = 8
PGQ = 2
assert TOPK_P % 8 == 0 and TOPK_S % 8 == 2

CN = {}
_at = 0
for _name, _w in (("ident", P), ("ones", P), ("perm", P), ("tril", P), ("neg", P), ("inv", 64),
                  ("m01s", NS), ("negs", NS), ("sel", NS), ("dm", DB * NS), ("em", DB * NS)):
    CN[_name] = (_at, _at + _w)
    _at += _w
NKEEP = CN["em"][0]
NCONST = _at


def constants():
    c = np.zeros((P, NCONST), np.float32)

    def put(name, a):
        c[:a.shape[0], CN[name][0]:CN[name][0] + a.shape[1]] = a

    i = np.arange(P)
    put("ident", np.eye(P))
    put("ones", np.ones((P, P)))
    perm = np.zeros((P, P))
    for m in range(P):
        if m % HD < HD // 2:
            perm[m + HD // 2, m] = -1.0
        else:
            perm[m - HD // 2, m] = 1.0
    put("perm", perm)
    tril = (i[None, :] <= i[:, None]).astype(np.float64)
    put("tril", tril)
    put("neg", (1.0 - tril) * INVALID)
    inv = np.zeros((P, 64))
    for g, w in enumerate(POOLW):
        inv[:, 16 * g:16 * g + 16] = 1.0 / np.minimum(w, np.arange(16) + 1)
    put("inv", inv)
    r = np.arange(NS)
    same = (r[:, None] // DT == r[None, :] // DT) & (r[None, :] <= r[:, None])
    put("m01s", same.astype(np.float64))
    put("negs", (1.0 - same) * INVALID)
    put("sel", (np.arange(8)[:, None] == r[None, :] // DT).astype(np.float64))
    b = np.arange(DB)
    row, col = r[:, None, None], r[None, None, :]
    put("dm", ((row % DT == col % DT) & (col // DT == b[None, :, None])).reshape(NS, -1).astype(np.float64))
    put("em", ((row % DT == col % DT) & (row // DT == b[None, :, None])).reshape(NS, -1).astype(np.float64))
    half = HD // 2
    freq = np.float32(10000.0) ** (-np.arange(half, dtype=np.float32) / np.float32(half))
    pos = np.concatenate([np.arange(SEQ), PAST + r % DT]).astype(np.float32)
    ang = (pos[None, :] * freq.astype(np.float32)[np.arange(P) % half, None]).astype(np.float32)
    rope = np.stack([np.cos(ang), np.sin(ang)], axis=1).astype(np.float32)
    return c, rope


class Phase:

    def __init__(self, name, g, kt, iters, nd, free, layer=0, half=0):
        self.name, self.g, self.kt, self.iters, self.nd, self.free = name, g, kt, iters, nd, free
        self.layer, self.half = layer, half


def phases():
    out = [Phase("in", 0, 8, 8, 2, "aa"), Phase("in", 1, 8, 8, 2, "aa")]
    for g in range(2):
        def mixer(layer):
            for h in range(2):
                out.append(Phase("gu", g, 8, FH, 2, "dd", layer, h))
                out.append(Phase("dn", g, FH, 4, 2, "aa" if h == 0 else "dd", layer, h))
        out.append(Phase("out", g, 8, 4, 3, "aa"))
        mixer(0)
        out += [Phase("v", g, 8, 4, 2, "dd"), Phase("u", g, 8, 4, 2, "dd"), Phase("oo", g, 8, 4, 2, "aa")]
        mixer(1)
    chunk, win, freed, gus = 0, [0, 0], {("a", 0): 0, ("a", 1): 0, ("d", 0): 1, ("d", 1): 1}, 0
    prev = None
    for ph in out:
        ph.c0, ph.win = chunk, list(win)
        ph.base = {k: v for k, v in freed.items()}
        ph.prev = [(prev.free[p], freed[prev.free[p], p]) if prev else None for p in (0, 1)]
        ph.hb = FH * gus + 1
        gus += ph.name == "gu"
        chunk += 2 * ph.iters
        for p in (0, 1):
            win[p] += 16 * ph.nd * ph.iters
            freed[ph.free[p], p] += ph.iters
        ph.end = {k: v for k, v in freed.items()}
        prev = ph
    for a, b in zip(out, out[1:]):
        a.next = b
    out[-1].next = None
    return out


def wait(eng, sem, value):
    if isinstance(value, int):
        if value > 0:
            eng.wait_ge(sem, value)
        return
    eng.wait_ge(sem, value)
    eng.nop(nofuse=True)


def build_kernel(nc, ins, outs):
    ph_list = phases()
    by = {(q.name, q.g, q.layer, q.half): q for q in ph_list}

    def phase(name, g, layer=0, half=0):
        return by[name, g, layer, half]

    with ExitStack() as ctx:
        start = (nc.sbuf_base + 63) // 64 * 64
        cursor = [start]

        def place(name, shape, dt, at=None):
            size = 2 if dt == BF16 else 4
            n = size * int(np.prod(shape[1:]))
            if at is None:
                at = cursor[0]
                cursor[0] = (at + n + 31) // 32 * 32
                assert cursor[0] <= nc.sbuf_usable_end, (name, cursor[0], nc.sbuf_usable_end)
            return nc.alloc_sbuf_tensor_at(name, shape, dt, offset=at), at

        X, x_at = place("resid", [P, NB, T[1]], F32)
        AR, a_at = place("act_split", [P, 2, NB, T[1]], F32R)
        HR, h_at = place("hidden_split", [P, 2, FH, T[1]], F32R)
        Y, y_at = place("mixed", [P, NB, T[1]], F32)
        WR, _ = place("w_raw", [P, 2, FH * P], F32)
        WH, _ = place("w_hi", [P, 2, FH * P], F32R)
        WL, _ = place("w_lo", [P, 2, FH * P], F32R)
        KT, _ = place("keys_t", [P, SEQ + NS], F32)
        IKT, _ = place("idx_keys_t", [P, SEQ + NS], F32)
        VN, _ = place("values", [P, 9, P], F32)
        IW, _ = place("idx_weights", [P, 9, 8], F32)
        SB, sb_at = place("scores1", [P, 3328 + KCOL + 8], F32)
        SA, sa_at = place("scores0", [P, 896], F32)
        SQ, sq_at = place("squares", [P, 2, T[1]], F32)
        TT, tt_at = place("temps", [P, 2, T[1]], F32)
        SS, _ = place("square_sums", [P, 5 * P], F32)
        RT, _ = place("root_rstd", [P, 2, 5], F32)
        CT, _ = place("constants", [P, NKEEP], F32)
        GC, _ = place("gains", [P, 84], F32)
        IDB, _ = place("ident_bf16", [P, P], BF16)
        MCB, _ = place("causal_bf16", [P, P], BF16)
        EB, _ = place("spread_bf16", [NS, DB, NS], BF16)
        IWT, _ = place("idx_weights_t", [8, NS], F32)
        M8, _ = place("top8", [P, 5, 8], F32)
        MX, _ = place("row_stats", [P, 4, 16], F32)
        PGT, _ = place("pages", [1, DB * NPG], I32)
        T16, _ = place("first_windows", [P, 16], F32)

        def over(name, shape, dt, base, words):
            return place(name, shape, dt, base + 4 * words)[0]

        DG = over("diag_rstd", [P, 5, P], F32, tt_at, 0)

        RB = over("root_of_input", [P, T[1]], F32, sa_at, 0)

        IQ = over("idx_queries_t", [P, 4, T[1]], F32, h_at, 0)
        XPE = over("pool_in", [P, 4, EXT], F32, h_at, 2304)
        RP = over("rope", [P, 2, T[1]], F32, h_at, 5152)
        KN = over("keys_rows", [P, 5, P], F32, h_at, 6304)
        IKN = over("idx_keys_rows", [P, 5, HD], F32, h_at, 6944)
        XN = over("x_rows", [P, 5, D], F32, h_at, 7552)
        GN = over("gain_rows", [84, P], F32, h_at, 0)
        EM = over("spread_f32", [P, DB * NS], F32, h_at, 128)
        SPN = over("state_rows", [DB * BUF, 512], F32, h_at, 640)
        XNS = over("xp_rows", [P, 2, 512], F32, h_at, 7552)
        WPG = over("w_pool", [P, 4, P], F32, sb_at, 0)
        QT = over("queries_t", [P, 2, T[1]], F32, sb_at, 512)
        PD = over("pooled", [P, 2, T[1]], F32, sb_at, 512)
        PHL = [over("pool_split0", [P, 2, T[1]], F32R, sb_at, 1664), over("pool_split1", [P, 2, T[1]], F32R, y_at, 2048)]
        GXS = over("xp_sample", [P, 4, NS], F32, sb_at, 2816)
        PA = over("window_a", [P, 2 * T[1]], F32, sq_at, 0)
        PB = over("window_b", [P, 2 * T[1]], F32, tt_at, 0)
        IKS = over("idx_keys_split", [P, 2, SEQ], F32R, a_at, 0)
        IQS = over("idx_queries_split", [P, 2, 8, P], F32R, a_at, 2048)
        IKP = over("idx_key_pages", [P, DB * NPG, P], F32, a_at, 4096)
        IQZ = over("idx_queries_sample", [P, DB, NS], F32, a_at, 8192)
        IKTB = [over("idx_page_keys0", [P, PAST], F32, a_at, 8704), over("idx_page_keys1", [P, PAST], F32, y_at, 3712)]
        R = over("relu", [P, 2, SEQ], F32, y_at, 0)
        MS = over("head_mix", [NS, DB, NS], F32, y_at, 2048)
        RS = over("relu_sample", [NS, 2, KCOL], F32, y_at, 2560)
        KS = over("keys_split", [P, 2, 2, SEQ], F32R, h_at, 0)
        VS = over("values_split", [P, 2, 8, P], F32R, h_at, 4096)
        QST = over("queries_split", [P, 8, P], F32R, h_at, 6144)
        PT = over("probs_t", [P, 2, 2, 512], F32R, h_at, 7168)
        MK = over("mask", [P, 2, SEQ], BF16, h_at, 9216)
        QR = over("queries_tile", [P, 4, P], F32, y_at, 4096)
        PR_SHORT = over("probs_short", [P, RING, 512], F32, y_at, 0)
        PR_LONG = [over("probs_long_a", [P, 4, SEQ], F32, y_at, 0), over("probs_long_b", [P, 4, SEQ], F32, x_at, 0)]
        KP, VP = [], []
        for q, (base, at) in enumerate(((h_at, 10240), (sb_at, 0), (y_at, 0), (y_at, 2048))):
            KP.append(over(f"key_pages{q}", [P, PGRP, P], F32, base, at))
            VP.append(over(f"value_pages{q}", [P, PGRP, P], F32, base, at + 1024))
        QZ = over("queries_sample", [P, DB, NS], F32, h_at, 0)
        KTB = over("page_keys_t", [P, 2, PAST], F32, h_at, 512)
        PRS = over("probs_sample", [NS, 2, KCOL], F32, h_at, 1536)
        PTS = over("probs_sample_t", [P, 2, 5 * NS], F32, h_at, 2688)
        MKS = over("mask_sample", [NS, KCOL], BF16, h_at, 3328)
        ZN = over("z_rows", [P, 5, D], F32, h_at, 0)
        WS = over("w_spatial_rows", [P, 8, P], F32, h_at, 0)
        WS8 = over("w_spatial_sample_rows", [NS, 8, NS], F32, h_at, 1024)
        U = over("u_t", [P, NB, T[1]], F32, h_at, 5120)
        WMT = over("w_spatial_t", [P, 8, P], F32, h_at, 9728)
        WM8T = over("w_spatial_sample_t", [NS, 8, NS], F32, h_at, 10752)
        BS = over("b_spatial_all", [P, 8, P], F32, h_at, 11264)
        ON = over("y_rows", [P, 5, D], F32, a_at, 0)

        PS = ctx.enter_context(nc.psum_tensor("psum", [P, 8, 512], F32))
        PSF = PS[:].rearrange("p b n -> p (b n)")

        q_dram = nc.dram_tensor("queries_spill", [2, P, 4, T[1]], F32, kind="Internal").ap()
        c_dram = nc.dram_tensor("pool_spill", [2, P, 2, 4, T[1]], F32, kind="Internal").ap()
        x_dram = nc.dram_tensor("resid_spill", [P, NB, T[1]], F32, kind="Internal").ap()

        def const(name, rows=P):
            a, b = CN[name]
            return CT[0:rows, a:b]

        IDENT, ONES, TRIL = const("ident"), const("ones"), const("tril")
        sems = {}

        def S(name):
            if name not in sems:
                sems[name] = ctx.enter_context(nc.semaphore(name))
            return sems[name]

        G_MIX_PRE, G_MIX_POST, G_FFN_PRE, G_FFN_POST, G_LN, B_LN, G_POOL = 0, 16, 32, 48, 64, 72, 80

        def gain(base, layer, n):
            return GC[:, base + 8 * layer + n:base + 8 * layer + n + 1]

        def lin(p, g):
            h, w = HALF[g]
            return PS[:, 2 * p:2 * p + h, 0:w]

        def aux(x, g):
            h, w = HALF[g]
            return PS[:, 4 + 2 * x:4 + 2 * x + h, 0:w]

        def hv(ap, g):
            return ap.rearrange("p (h w) -> p h w", h=HALF[g][0])

        def halves(g):
            h, w = HALF[g]
            return [(b, b * w, (b + 1) * w) for b in range(h)]

        def tiles(g):
            return [(k, P * k, min(P, T[g] - P * k)) for k in range(NT[g])]

        def flat(ap):
            return ap.rearrange("p a n -> p (a n)")

        def norm_at(kind, g, s):
            if kind == "load":
                return g
            return 2 + 4 * g + s

        def r_at(g, s):
            return 2 + 8 * g + s

        def a_at_(g, s):
            return 2 + 4 * g + s

        def z_at(g, s):
            return 2 + 5 * g + s

        SPOST = (0, 2, 5, 7)
        SPRE = (1, 3, 6)
        SA_ = (0, 1, 3)
        SZ = (0, 1, 3, 4)

        IDX_T = ((2, 3), (4, 5, 6, 7))
        IDX_U = ((0, 1), (2, 3, 4, 5))
        SB_AT = {4: 0, 5: 640, 6: 1408, 7: 2304}
        SS_AT = 3328

        def score(t):
            n = P * (t + 1)
            return SA[:, 384 * (t - 2):384 * (t - 2) + n] if t < 4 else SB[:, SB_AT[t]:SB_AT[t] + n]

        SCS = SB[0:NS, SS_AT:SS_AT + KCOL + 8]

        def kbase(t, kv):
            return sum(2 * (u + 1) for u in range(t)) + kv * (t + 1)

        def probs(hh):
            if hh < 32:
                return PR_SHORT[:, hh % RING, :]
            return PR_LONG[hh % RING // 4][:, hh % 4, :]

        def items(g):
            out = [("qk", 4 * g, h, 0) for h in range(4)]
            last, done = 4 * g + 3, None
            for t in range(4 * g, 4 * g + 4):
                for kv in range(2):
                    ahead = [("qk", t, h, 0) for h in range(4, 8)] if kv == 0 else \
                        [("qk", t + 1, h, 0) for h in range(4)] if t < last else []
                    out.append(("tr", t, kv, 0))
                    out += ahead[:1]
                    for kk in range(t + 1):
                        if kk < t:
                            out.append(("tr", t, kv, kk + 1))
                        out += [q for j, q in enumerate(ahead) if j and (j - 1) * (t + 1) // 5 == kk]
                        out.append(("pv", t, kv, kk))
                        if kk == 0 and done:
                            out.append(done)
                    done = ("o", t, kv, 0)
            return out + [done]

        def logits(x, t, rows=P):
            n = P * (t + 1)
            k = 1 if n <= 512 else 2
            return PS[0:rows, 2 * x:2 * x + k, 0:n // k]

        def cut(ap, t):
            k = 1 if t < 4 else 2
            return ap.rearrange("p (c n) -> p c n", c=k)

        block = ctx.enter_context(nc.Block())

        @block.sync
        def _(sp):
            w_ge, w_oe = ins["w_in_even"][0], ins["w_out_even"][0]
            w_io, w_oo = ins["w_in_odd"][0], ins["w_out_odd"][0]

            def cols(w, first, k0, k1, n=P):
                return w[P * k0:P * k1, :].rearrange("(k p) c -> p k c", p=P)[:, :, ds(first, n)]

            def load_chunk(ph, i, p):
                c = ph.c0 + 2 * i + p
                if not (isinstance(c, int) and c < 2):
                    sp.wait_ge(S("w_lo"), c - 1)
                slot = WR[:, p, :].rearrange("p (k c) -> p k c", c=P)
                sem = S(f"w_in{p}")

                def put(dst, src):
                    sp.dma_start(dst, src).then_inc(sem, 16)

                if ph.name == "in":
                    local = 2 * i + p
                    if local < 8:
                        first = 64 * i + (768 if p else 0)
                        parts = [(first, 0), (first + 256, 64)]
                    elif local == 8:
                        parts = [(512, 0), (576, 64)]
                    elif local == 9:
                        parts = [(1280, 0), (1280, 64)]
                    elif local == 10:
                        parts = [(640, 0), (704, 64)]
                    elif local == 11:
                        parts = [(1344, 0), (1408, 64)]
                    else:
                        parts = [(1352 + P * (local - 12), 0), (1352 + P * (local - 12) + 64, 64)]
                    for first, at in parts:
                        put(slot[:, 0:8, at:at + 64], cols(w_ge, first, 0, 8, 64))
                elif ph.name == "out":
                    first = P * (2 * i + p)
                    for r in range(2):
                        put(slot[64 * r:64 * r + 64, 0:4, :],
                            w_oe[256 * r:256 * r + 256, :].rearrange("(k p) c -> p k c", p=64)[:, :, ds(first, P)])
                    put(slot[:, 4:8, :], cols(w_oe, first, 4, 8))
                else:
                    if ph.name == "gu":
                        w, first, row = ins["w_ffn_gate_up"][ph.layer], FF * p + P * (FH * ph.half + i), 0
                    elif ph.name == "dn":
                        w, first, row = ins["w_ffn_down"][ph.layer], P * (2 * i + p), FH * ph.half
                    elif ph.name == "v":
                        w, first, row = w_io, D + P * (2 * i + p), 0
                    elif ph.name == "u":
                        w, first, row = w_io, P * (2 * i + p), 0
                    else:
                        w, first, row = w_oo, P * (2 * i + p), 0
                    mid = (ph.kt + 1) // 2
                    put(slot[:, 0:mid, :], cols(w, first, row, row + mid))
                    put(slot[:, mid:ph.kt, :], cols(w, first, row + mid, row + ph.kt))

            def head(ph):
                load_chunk(ph, 0, 0)
                load_chunk(ph, 0, 1)

            def rest(ph):
                with sp.Fori(1, ph.iters) as i:
                    load_chunk(ph, i, 0)
                    load_chunk(ph, i, 1)

            def load_x(g):
                for k in range(4):
                    sp.dma_start(XN[:, k, :], ins["x_prompt"][0, 512 * g + P * k:512 * g + P * k + P, :]).then_inc(S("x_in"), 16)
                if g:
                    sp.dma_start(XN[0:NS, 4, :], ins["x_sample"].rearrange("b t d -> (b t) d")).then_inc(S("x_in"), 16)

            def index_pages(first, count):
                with sp.Fori(first, first + count) as i:
                    page = sp.value_load(PGT[0:1, ds(i, 1)], min_val=0, max_val=DB * NPG * 5 // 4 - 1)
                    src = ins["cache_idx_k"][0][ds(page, 1)].rearrange("a s d -> s a d").to_broadcast([P, 2, HD])
                    dst = IKP[:, ds(i, 1), :].rearrange("p a (c d) -> p (a c) d", c=2)
                    sp.dma_start(dst, src).then_inc(S("ikp_in"), 16)

            def in_stage(g):
                ph = phase("in", g)

                def after(local):
                    if 0 <= local < 8 and local % 2 == 0:
                        j = local // 2
                        sp.wait_ge(S("rope_out"), 10 * g + local + 1)
                        sp.dma_start(q_dram[g, :, j, 0:T[g]], QT[:, j % 2, 0:T[g]]).then_inc(S(f"q_out{j % 2}"), 16)

                for local in range(2, 16):
                    load_chunk(ph, local // 2, local % 2)
                    after(local - 6)
                    if g and local == 4:
                        sp.wait_ge(S("a_t"), 16)
                        sp.dma_start(x_dram, Y[:]).then_inc(S("x_out"), 16)
                nxt = phase("in", 1) if g == 0 else phase("out", 0)
                head(nxt)
                if g:
                    sp.wait_ge(S("pt_in"), 16)
                    sp.wait_ge(S("w_used"), ph.c0 + 16)
                rows = slice(512 * g, 512 * g + 512)
                kn = [outs["new_k_prompt"], outs["new_v_prompt"]]
                sp.wait_ge(S("nat_a"), 3 * g + 2)
                for k in range(4):
                    r0 = 512 * g + P * k
                    sp.dma_start(kn[0][0, 0, r0:r0 + P].rearrange("t h d -> t (h d)"), KN[:, k, :]).then_inc(S("kv_out"), 16)
                    sp.dma_start(outs["new_idx_k_prompt"][0, 0, r0:r0 + P], IKN[:, k, :]).then_inc(S("kv_out"), 16)
                if g:
                    sp.dma_start(outs["new_k_sample"][0].rearrange("b t h d -> (b t) (h d)"), KN[0:NS, 4, :]).then_inc(S("kv_out"), 16)
                    sp.dma_start(outs["new_idx_k_sample"][0].rearrange("b t d -> (b t) d"), IKN[0:NS, 4, :]).then_inc(S("kv_out"), 16)
                sp.wait_ge(S("nat_a"), 3 * g + 3)
                for k in range(4):
                    r0 = 512 * g + P * k
                    sp.dma_start(kn[1][0, 0, r0:r0 + P].rearrange("t h d -> t (h d)"), VN[:, 4 * g + k, :]).then_inc(S("kv_out"), 16)
                if g:
                    sp.dma_start(outs["new_v_sample"][0].rearrange("b t h d -> (b t) (h d)"), VN[0:NS, 8, :]).then_inc(S("kv_out"), 16)
                for pg in range(4):
                    sp.wait_ge(S("pool_lo"), 4 * g + pg + 1)
                    sp.dma_start(c_dram[g, :, :, pg, 0:T[g]], PHL[pg % 2][:, :, 0:T[g]].bitcast(F32)).then_inc(S(f"pool_out{pg % 2}"), 16)
                    if g:
                        index_pages(PGQ * pg, PGQ)
                if g:
                    sp.wait_ge(S("xp_rows"), 1)
                    sp.dma_start(outs["new_pool_prompt"][0, 0], XNS[0:BUF, 0, :]).then_inc(S("st_out"), 16)
                    for b in range(DB):
                        sp.dma_start(outs["new_pool_sample"][0, b, BUF - DT:BUF], XNS[DT * b:DT * b + DT, 1, :]).then_inc(S("st_out"), 16)

            def key_value_pages(q):
                with sp.Fori(0, PGRP) as i:
                    page = sp.value_load(PGT[0:1, ds(i + PGRP * q, 1)], min_val=0, max_val=DB * NPG * 5 // 4 - 1)
                    for dst, name, sem in ((KP[q], "cache_k", "kp_in"), (VP[q], "cache_v", "vp_in")):
                        src = ins[name][0].rearrange("n s h d -> n s (h d)")[ds(page, 1)].rearrange("a s d -> (a s) d")
                        sp.dma_start(dst[:, ds(i, 1), :].rearrange("p a d -> p (a d)"), src).then_inc(S(f"{sem}{q}"), 16)

            def attend(g):
                if g == 0:
                    sp.wait_ge(S("mix_mm"), DB)
                sp.dma_start(QR[:], q_dram[g, :, :, 0:P]).then_inc(S("q_in"), 16)
                sp.dma_start(AR[:, 0, 4:8, 0:T[g]].bitcast(F32), c_dram[g, :, 0, :, 0:T[g]]).then_inc(S("pool_in"), 16)
                sp.dma_start(AR[:, 1, 4:8, 0:T[g]].bitcast(F32), c_dram[g, :, 1, :, 0:T[g]]).then_inc(S("pool_in"), 16)
                if g:
                    key_value_pages(0)
                for k in range(1, 4):
                    sp.wait_ge(S("qst_lo"), 2 * (4 * g + k))
                    sp.dma_start(QR[:], q_dram[g, :, :, P * k:P * k + P]).then_inc(S("q_in"), 16)
                if g:
                    sp.wait_ge(S("mk"), 6)
                    key_value_pages(1)
                    sp.wait_ge(S("qst_lo"), 16)
                    sp.dma_start(QR[:, :, 0:NS], q_dram[1, :, :, 512:T[1]]).then_inc(S("q_in"), 16)
                    sp.wait_ge(S("p_tr"), kbase(7, 1))
                    key_value_pages(2)
                    key_value_pages(3)
                    sp.wait_ge(S("p_tr"), kbase(8, 0))
                    sp.dma_start(X[:], x_dram).then_inc(S("xb_in"), 16)

            def spatial_weights(g):
                sp.wait_ge(S("w_used"), phase("dn", g, 0, 1).c0 + 8)
                sp.dma_start(WS[:], ins["w_spatial"][0].rearrange("g t s -> t g s")).then_inc(S("ws_in"), 16)
                sp.dma_start(BS[:], ins["b_spatial"][0].unsqueeze(0).to_broadcast([P, 8, P])).then_inc(S("ws_in"), 16)
                sp.wait_ge(S("ws8_zero"), g + 1)
                for b in range(DB):
                    sp.dma_start(WS8[DT * b:DT * b + DT, :, DT * b:DT * b + DT],
                                 ins["w_spatial"][0, :, 0:DT, 0:DT].rearrange("g t s -> t g s")).then_inc(S("ws_in"), 16)

            sp.dma_start(CT[:], ins["constants"][:, 0:NKEEP]).then_inc(S("c_in"), 16)
            load_x(0)
            row = 0
            for name in ("norm_mix_pre", "norm_mix_post", "norm_ffn_pre", "norm_ffn_post", "sgu_norm_g", "sgu_norm_b", "pool_scale"):
                src = ins[name].rearrange("l (n p) -> (l n) p", p=P)
                sp.dma_start(GN[row:row + src.shape[0], :], src).then_inc(S("g_in"), 16)
                row += src.shape[0]
            head(phase("in", 0))
            sp.dma_start(RP[:, :, 0:T[0]], ins["rope"][:, :, 0:T[0]]).then_inc(S("rope_in"), 16)
            sp.dma_start(SPN[:], ins["state_pool"][0].rearrange("b r d -> (b r) d")).then_inc(S("s_in"), 16)
            sp.dma_start(EM[:], ins["constants"][:, NKEEP:NCONST]).then_inc(S("s_in"), 16)
            sp.dma_start(PGT[:], ins["page_table"].rearrange("b n -> (b n)").unsqueeze(0)).then_inc(S("pt_in"), 16)
            sp.dma_start(WPG[:], ins["w_pool_group"][0].rearrange("g c e -> c g e")).then_inc(S("wp_in"), 16)
            sp.dma_start(outs["new_pool_sample"][0, :, 0:BUF - DT], ins["state_pool"][0, :, DT:BUF]).then_inc(S("st_out"), 16)
            in_stage(0)
            load_x(1)
            sp.wait_ge(S("rope_out"), 10)
            sp.dma_start(RP[:], ins["rope"][:, :, 512:SEQ + NS]).then_inc(S("rope_in"), 16)
            in_stage(1)
            index_pages(4 * PGQ, DB * NPG - 4 * PGQ)
            for g in range(2):
                attend(g)
                rest(phase("out", g))
                for layer in range(2):
                    for half in range(2):
                        for name in ("gu", "dn"):
                            q = phase(name, g, layer, half)
                            head(q)
                            rest(q)
                    if layer == 0:
                        head(phase("v", g))
                        spatial_weights(g)
                        rest(phase("v", g))
                        for name in ("u", "oo"):
                            head(phase(name, g))
                            if g and name == "oo":
                                sp.wait_ge(S("zc_d"), 8)
                                sp.wait_ge(S("zc_a"), 8)
                                sp.dma_start(outs["new_sgu_v_sample"][0].rearrange("b t d -> (b t) d"), ZN[0:NS, 4, :]).then_inc(S("z_out"), 16)
                            rest(phase(name, g))
                if g == 0:
                    head(phase("out", 1))
                for k, _, w in tiles(g):
                    sp.wait_ge(S("y_cp"), 5 * g + k + 1 - g)
                    dst = outs["y_prompt"][0, 512 * g + P * k:512 * g + P * k + P] if k < 4 else \
                        outs["y_sample"].rearrange("b t d -> (b t) d")
                    sp.dma_start(dst, ON[0:w, k, :]).then_inc(S("y_out"), 16)
                if g == 0:
                    sp.wait_ge(S("y_out"), 64)
            sp.wait_ge(S("y_out"), 16 * 9)
            sp.wait_ge(S("kv_out"), 16 * 27)
            sp.wait_ge(S("st_out"), 16 * 10)
            for b in range(2):
                sp.wait_ge(S(f"q_out{b}"), 64)
                sp.wait_ge(S(f"pool_out{b}"), 64)
            sp.wait_ge(S("x_out"), 16)
            sp.wait_ge(S("z_out"), 16)

        @block.tensor
        def _(pe):
            def chunk(ph, i, p, x_hi, x_lo, ready=None):
                c = ph.c0 + 2 * i + p
                g = ph.g
                pe.wait_ge(S("w_lo"), c + 1)
                e, n = ph.free[p], ph.base[ph.free[p], p]
                if ph.prev[p] and ph.prev[p][0] != e:
                    wait(pe, S(f"free_{ph.prev[p][0]}{p}"), ph.prev[p][1])
                if isinstance(n + i, int):
                    wait(pe, S(f"free_{e}{p}"), n + i)
                else:
                    pe.wait_ge(S(f"free_{e}{p}"), n + i)
                for k in range(ph.kt):
                    if ready:
                        ready(k)
                    at = slice(P * k, P * k + P)
                    for w, x in ((WH, x_hi), (WH, x_lo), (WL, x_hi)):
                        for b, lo, hi in halves(g):
                            mm = pe.matmul(PS[:, 2 * p + b, 0:hi - lo], w[:, p, at], x(k)[:, lo:hi],
                                           start=(k == 0 and w is WH and x is x_hi),
                                           stop=(k == ph.kt - 1 and w is WL))
                mm.then_inc(S("w_used"), 1)

            def a_hi(k):
                return AR[:, 0, k, :]

            def a_lo(k):
                return AR[:, 1, k, :]

            def h_hi(k):
                return HR[:, 0, k, :]

            def h_lo(k):
                return HR[:, 1, k, :]

            def first_pair(ph, split, m=None, root_at=None):
                g = ph.g
                for p in (0, 1):
                    pe.wait_ge(S("w_lo"), ph.c0 + p + 1)
                    e = ph.free[p]
                    if ph.prev[p][0] != e:
                        pe.wait_ge(S(f"free_{ph.prev[p][0]}{p}"), ph.prev[p][1])
                    wait(pe, S(f"free_{e}{p}"), ph.base[e, p])
                def products(k, p, parts):
                    at = slice(P * k, P * k + P)
                    for w, x in parts:
                        for b, lo, hi in halves(g):
                            mm = pe.matmul(PS[:, 2 * p + b, 0:hi - lo], w[:, p, at], x(k)[:, lo:hi],
                                           start=(k == 0 and w is WH and x is a_hi),
                                           stop=(k == ph.kt - 1 and x is a_lo))
                    return mm

                first, second = ((WH, a_hi), (WL, a_hi)), ((WH, a_lo),)
                for k in range(ph.kt - 2):
                    pe.wait_ge(S("a_hi"), 8 * split + k + 1)
                    for p in (0, 1):
                        products(k, p, first)
                    pe.wait_ge(S("a_lo"), 8 * split + k + 1)
                    for p in (0, 1):
                        products(k, p, second)
                for p in (0, 1):
                    for k in (ph.kt - 2, ph.kt - 1):
                        pe.wait_ge(S("a_lo"), 8 * split + k + 1)
                        if m is not None and p and k == ph.kt - 1:
                            spread(root_at, g)
                        mm = products(k, p, first + second)
                    mm.then_inc(S("w_used"), 1)
                    if m is not None and p == 0:
                        token_sums(g, "ss_m", 8 * m + 8)

            def linear(ph, split=None, m=None, root_at=None):
                if split is None:
                    chunk(ph, 0, 0, a_hi, a_lo)
                    chunk(ph, 0, 1, a_hi, a_lo)
                else:
                    first_pair(ph, split, m, root_at)
                with pe.Fori(1, ph.iters) as i:
                    chunk(ph, i, 0, a_hi, a_lo)
                    chunk(ph, i, 1, a_hi, a_lo)

            def down(ph):
                def ready(k):
                    if k == 0:
                        pe.wait_ge(S("h_lo"), ph.hb - 1)
                    if k == FH - 1:
                        pe.wait_ge(S("h_lo"), ph.hb)
                with pe.Fori(0, ph.iters) as i:
                    chunk(ph, i, 0, h_hi, h_lo, ready)
                    chunk(ph, i, 1, h_hi, h_lo)

            def token_sums(g, sem, value):
                pe.wait_ge(S(sem), value)
                for k, lo, w in tiles(g):
                    mm = pe.matmul(PS[0:w, 6, 2 * k:2 * k + 1], SS[:, lo:lo + w], ONES[:, 0:1], start=True, stop=True)
                mm.then_inc(S("n_sum"), 1)

            def spread(r, g):
                pe.wait_ge(S("n_dg"), r + 1)
                for k, lo, w in tiles(g):
                    mm = pe.matmul(PSF[:, 4 * 512 + lo:4 * 512 + lo + w], ONES, DG[:, k, 0:w], start=True, stop=True)
                mm.then_inc(S("n_b"), 1)

            def load_x(g):
                pe.wait_ge(S("x_in"), 64 if g == 0 else 144)
                if g:
                    for p in (0, 1):
                        pe.wait_ge(S(f"free_a{p}"), phase("in", 0).end["a", p])
                for n in range(NB):
                    wait(pe, S("xt_cp"), 8 * g + n - 1)
                    for k, lo, w in tiles(g):
                        mm = pe.transpose(PSF[:, 1024 * (n % 2) + lo:1024 * (n % 2) + lo + w],
                                          XN[0:w, k, P * n:P * n + P], IDENT[0:w, 0:w])
                    mm.then_inc(S("xt_ps"), 1)
                if g:
                    pe.wait_ge(S("idx_r"), 16)
                token_sums(g, "ss_p", 8 * g + 8)
                spread(g, g)
                pe.wait_ge(S("xt_cp"), 8 * g + 8)

            def rows_of(src, rows, x, g, idn):
                for k, lo, w in tiles(g):
                    mm = pe.transpose(PSF[0:w, (4 + 2 * x) * 512 + P * k:(4 + 2 * x) * 512 + P * k + rows],
                                      src[:, lo:lo + w], idn)
                mm.then_inc(S("nat"), 1)

            def in_stage(g):
                ph = phase("in", g)

                def rotate(local):
                    r = 10 * g + local
                    p = local % 2
                    pe.wait_ge(S(f"free_a{p}"), ph.base["a", p] + local // 2 + 1)
                    wait(pe, S("rope_t1"), r - 1)
                    for b, lo, hi in halves(g):
                        mm = pe.matmul(PS[:, 4 + 2 * p + b, 0:hi - lo], const("perm"), SQ[:, p, lo:hi], start=True, stop=True)
                    mm.then_inc(S("rope_sw"), 1)

                def pooled(pg):
                    pe.wait_ge(S("pool_d"), 4 * g + pg + 1)
                    if pg == 0:
                        pe.wait_ge(S("nat_a"), 3 * g + 3)
                    elif pg == 1:
                        pe.wait_ge(S("iw_rows"), g + 1)
                    else:
                        pe.wait_ge(S("pool_lo"), 4 * g + pg - 1)
                    for b, lo, hi in halves(g):
                        mm = pe.matmul(PS[:, 4 + 2 * (pg % 2) + b, 0:hi - lo], WPG[:, pg, :], PD[:, pg % 2, lo:hi], start=True, stop=True)
                    mm.then_inc(S("pool_mm"), 1)

                for local in range(16):
                    def ready(k):
                        if local == 0:
                            pe.wait_ge(S("a_lo"), 8 * g + k + 1)
                    chunk(ph, local // 2, local % 2, a_hi, a_lo, ready)
                    if 1 <= local <= 10:
                        rotate(local - 1)
                    if local == 11:
                        c0 = 512 * g
                        pe.wait_ge(S("rope_t1"), 10 * g + 10)
                        pe.wait_ge(S("rope_out"), 10 * g + 10)
                        rows_of(KT[:, c0:c0 + T[g]], P, 0, g, IDENT)
                        rows_of(IKT[0:HD, c0:c0 + T[g]], HD, 1, g, IDENT[0:HD, 0:HD])
                    if local == 12:
                        pe.wait_ge(S("nat_a"), 3 * g + 1)
                        pe.wait_ge(S("free_a0"), ph.base["a", 0] + 6)
                        rows_of(SQ[:, 0, 0:T[g]], P, 0, g, IDENT)
                    if local == 13:
                        pe.wait_ge(S("nat_a"), 3 * g + 2)
                        pe.wait_ge(S("free_a1"), ph.base["a", 1] + 6)
                        rows_of(SQ[:, 1, 0:T[g]], P, 1, g, IDENT)
                    if local == 14:
                        pe.wait_ge(S("wp_in"), 16)
                        pooled(0)
                    if local == 15:
                        pooled(1)
                pooled(2)
                if g:
                    for p in (0, 1):
                        pe.wait_ge(S(f"free_a{p}"), ph.end["a", p])
                    for pg in range(4):
                        pe.transpose(PS[0:BUF, 0, P * pg:P * pg + P], XPE[:, pg, 512:512 + BUF], IDENT)
                    pe.wait_ge(S("xs_cp"), 1)
                    for pg in range(4):
                        mm = pe.transpose(PS[0:NS, 1, P * pg:P * pg + P], GXS[:, pg, :], IDENT)
                    mm.then_inc(S("xp_ps"), 1)
                pooled(3)

            def index(g):
                pe.wait_ge(S("ik_lo"), g + 1)
                pe.wait_ge(S("pool_lo"), 4 * g + 4)
                for u, t in zip(IDX_U[g], IDX_T[g]):
                    n = P * (t + 1)
                    k = 1 if n <= 512 else 2
                    pe.wait_ge(S("iq_lo"), 2 * u + 2)
                    for h in range(8):
                        wait(pe, S("idx_r"), 8 * u + h - 1)
                        x = h % 2
                        for part in range(2):
                            for b in range(k):
                                w = n // k
                                mm = pe.matmul(PS[:, 4 + 2 * x + b, 0:w], IQS[:, u % 2, h, :], IKS[:, part, b * w:b * w + w],
                                               start=part == 0, stop=part == 1)
                        mm.then_inc(S("idx_mm"), 1)

            def index_sample():
                pe.wait_ge(S("idx_r"), 48)
                pe.wait_ge(S("iw_rows"), 2)
                pe.wait_ge(S("c_in"), 16)
                pe.matmul(PS[0:NS, 6, 0:NS], const("sel", 8), IWT[:, :], start=True, stop=True).then_inc(S("spread_mm"), 1)
                pe.wait_ge(S("ikp_in"), 16 * DB * NPG)
                pe.wait_ge(S("xp_rows"), 1)

                def turn(b):
                    wait(pe, S("ikt_cp"), b - 1)
                    for j in range(NPG):
                        mm = pe.transpose(PS[:, b % 2, P * j:P * j + P], IKP[:, NPG * b + j, :], IDENT)
                    mm.then_inc(S("ikt_ps"), 1)

                def mix(b):
                    pe.wait_ge(S("rs"), b + 1)
                    if b == 0:
                        pe.wait_ge(S("ms"), 1)
                    for bank, lo, hi in ((4, 0, PAST), (5, PAST, KCOL)):
                        mm = pe.matmul(PS[0:NS, bank, 0:hi - lo], MS[:, b, :], RS[:, b % 2, lo:hi], start=b == 0, stop=b == DB - 1)
                    mm.then_inc(S("mix_mm"), 1)

                turn(0)
                for b in range(DB):
                    if b + 1 < DB:
                        turn(b + 1)
                    pe.wait_ge(S("ikt_cp"), b + 1)
                    pe.wait_ge(S("iqz"), 1)
                    wait(pe, S("rs"), b)
                    pe.matmul(PS[0:NS, 2, 0:PAST], IQZ[:, b, :], IKTB[b % 2][:], start=True, stop=True)
                    pe.matmul(PS[0:NS, 3, 0:NS], IQZ[:, b, :], IKT[:, SEQ:SEQ + NS], start=True, stop=True).then_inc(S("rel_mm"), 1)
                    if b:
                        mix(b - 1)
                mix(DB - 1)

            def attend(g):
                pe.wait_ge(S("ks_lo"), 5 * g + 5)
                if g:
                    pe.wait_ge(S("y_cp"), 4)
                for kind, t, z, kk in items(g):
                    kc = kbase(t, z) + kk
                    if kind == "qk":
                        h, hh, x = z, 8 * t + z, z % 2
                        n = P * (t + 1)
                        k = 1 if n <= 512 else 2
                        w = n // k
                        pe.wait_ge(S("qst_lo"), 2 * t + h // 4 + 1)
                        wait(pe, S("exp"), hh - 1)
                        if t >= 2:
                            pe.wait_ge(S("mk"), t - 1)
                            for b in range(k):
                                pe.matmul(PS[:, 2 * x + b, 0:w], IDB[:], MK[:, t % 2, b * w:b * w + w], start=True, stop=False)
                        for part in range(2):
                            for b in range(k):
                                mm = pe.matmul(PS[:, 2 * x + b, 0:w], QST[:, h, :], KS[:, h // 4, part, b * w:b * w + w],
                                               start=t < 2 and part == 0, stop=t >= 2 and part == 1)
                        if t < 2:
                            mm = pe.matmul(PS[:, 2 * x, P * t:P * t + P], IDB[:], MCB[:], start=False, stop=True)
                        mm.then_inc(S("qk_mm"), 1)
                    elif kind == "tr":
                        if kk == 0:
                            pe.wait_ge(S("p_norm"), 8 * t + 4 * z + 4)
                        wait(pe, S("pt_lo"), kc - 1)
                        for j in range(4):
                            mm = pe.transpose(PS[:, 4 + kc % 2, P * j:P * j + P], probs(8 * t + 4 * z + j)[:, P * kk:P * kk + P], IDENT)
                        mm.then_inc(S("p_tr"), 1)
                    elif kind == "pv":
                        if kk == 0:
                            wait(pe, S("o_lo"), 2 * t + z - 1)
                        pe.wait_ge(S("pt_lo"), kc + 1)
                        for v, q in ((0, 0), (0, 1), (1, 0)):
                            mm = pe.matmul(PS[:, 6 + z, :], VS[:, v, kk, :], PT[:, kc % 2, q, :],
                                           start=kk == 0 and v == 0 and q == 0, stop=kk == t and v == 1)
                        mm.then_inc(S("pv_mm"), 1)

            def attend_sample():
                pe.wait_ge(S("pt_lo"), kbase(8, 0))
                pe.wait_ge(S("o_lo"), 16)
                pe.wait_ge(S("exp"), 64)

                def turn(b):
                    q, at = divmod(NPG * b, PGRP)
                    wait(pe, S("ktb"), b - 1)
                    if at == 0:
                        pe.wait_ge(S(f"kp_in{q}"), 16 * PGRP)
                    for j in range(NPG):
                        mm = pe.transpose(PS[:, 4 + b % 2, P * j:P * j + P], KP[q][:, at + j, :], IDENT)
                    mm.then_inc(S("kt_ps"), 1)

                def turn_probs(b):
                    pe.wait_ge(S("ps_norm"), b + 1)
                    wait(pe, S("pts"), b)
                    for j in range(NPG):
                        pe.transpose(PS[:, 6, NS * j:NS * j + NS], PRS[:, b % 2, P * j:P * j + P], IDENT[0:NS, 0:NS])
                    pe.transpose(PS[0:NS, 6, NS * NPG:NS * NPG + NS], PRS[:, b % 2, PAST:KCOL], IDENT[0:NS, 0:NS]).then_inc(S("ps_tr"), 1)

                def values(b):
                    q, at = divmod(NPG * b, PGRP)
                    if at == 0:
                        pe.wait_ge(S(f"vp_in{q}"), 16 * PGRP)
                    pe.wait_ge(S("pts"), b + 1)
                    for j in range(NPG):
                        pe.matmul(PS[:, 7, NS * b:NS * b + NS], VP[q][:, at + j, :], PTS[:, b % 2, NS * j:NS * j + NS],
                                  start=j == 0, stop=False)
                    pe.matmul(PS[:, 7, NS * b:NS * b + NS], VN[0:NS, 8, :], PTS[0:NS, b % 2, NS * NPG:NS * NPG + NS],
                              start=False, stop=True).then_inc(S("pvs_mm"), 1)

                turn(0)
                for b in range(DB + 2):
                    if b + 1 < DB:
                        turn(b + 1)
                    if b < DB:
                        x = b % 2
                        pe.wait_ge(S("ktb"), b + 1)
                        pe.wait_ge(S("qz"), 1)
                        pe.wait_ge(S("mks"), 1)
                        wait(pe, S("exps"), b - 1)
                        for bank, lo, hi, keys in ((2 * x, 0, PAST, KTB[:, x, :]), (2 * x + 1, PAST, KCOL, KT[:, SEQ:SEQ + NS])):
                            pe.matmul(PS[0:NS, bank, 0:hi - lo], EB[:, b, :], MKS[:, lo:hi], start=True, stop=False)
                            mm = pe.matmul(PS[0:NS, bank, 0:hi - lo], QZ[:, b, :], keys, start=False, stop=True)
                        mm.then_inc(S("qks_mm"), 1)
                    if 2 <= b:
                        values(b - 2)
                    if 1 <= b < DB + 1:
                        turn_probs(b - 1)

            def post(g, s):
                mp = norm_at("post", g, s)
                token_sums(g, "ss_p", 8 * mp + 8)
                spread(r_at(g, SPOST[s]), g)

            def gate(g):
                ph = phase("u", g)
                pe.wait_ge(S("ws_m"), 2 * g + 2)
                for q in range(8):
                    pe.transpose(PS[:, 4 + q // 4, P * (q % 4):P * (q % 4) + P], WS[:, q, :], IDENT)
                for q in range(8):
                    mm = pe.transpose(PS[0:NS, 6, NS * q:NS * q + NS], WS8[:, q, :], IDENT[0:NS, 0:NS])
                mm.then_inc(S("ws_t"), 1)
                for local in range(8):
                    chunk(ph, local // 2, local % 2, a_hi, a_lo)
                    if local == 0:
                        pe.wait_ge(S("wmt"), g + 1)
                        pe.wait_ge(S("lv"), 8 * g + 9)
                        for b, lo, hi in halves(g):
                            mm = pe.matmul(PS[:, 4 + b, 0:hi - lo], ONES, SS[:, lo:hi], start=True, stop=True)
                        mm.then_inc(S("mean"), 1)
                    if local == 4:
                        token_sums(g, "ln_ss", 8 * g + 8)
                    if local == 5:
                        spread(r_at(g, 4), g)

                def turn(n):
                    x = 1 - n % 2
                    pe.wait_ge(S("ln_z"), 8 * g + n + 1)
                    if n == 1:
                        pe.wait_ge(S("ln_t"), 8 * g + 8)
                    if n >= 2:
                        pe.wait_ge(S("zc_d" if n % 2 == 0 else "zc_a"), 4 * g + n // 2)
                    for k, lo, w in tiles(g):
                        mm = pe.transpose(PSF[0:w, (4 + 2 * x) * 512 + lo:(4 + 2 * x) * 512 + lo + P], Y[:, n, lo:lo + w], IDENT)
                    mm.then_inc(S("z_ps"), 1)

                for p in (0, 1):
                    pe.wait_ge(S(f"free_d{p}"), ph.end["d", p])
                turn(0)
                turn(1)
                for n in range(NB):
                    if n + 2 < NB:
                        turn(n + 2)
                    pe.wait_ge(S("zc_d" if n % 2 == 0 else "zc_a"), 4 * g + n // 2 + 1)
                    wait(pe, S("s_b"), 8 * g + n - 1)
                    for k in range(4):
                        mm = pe.matmul(PS[:, 2 * (n % 2), P * k:P * k + P], ZN[:, k, P * n:P * n + P], WMT[:, n, :], start=True, stop=True)
                    if g:
                        mm = pe.matmul(PS[:, 2 * (n % 2) + 1, 0:NS], ZN[0:NS, 4, P * n:P * n + P], WM8T[:, n, :], start=True, stop=True)
                    mm.then_inc(S("s_mm"), 1)
                pe.wait_ge(S("s_b"), 8 * g + 8)

            def result(g):
                for k, lo, w in tiles(g):
                    if k == 0:
                        for p in (0, 1):
                            pe.wait_ge(S(f"free_d{p}"), phase("dn", g, 1, 1).end["d", p])
                    if k >= 2:
                        pe.wait_ge(S("y_cp"), 4 * g + k - 1)
                    for n in range(NB):
                        if k == 0:
                            pe.wait_ge(S("x_new"), 8 * (4 * g + 3) + n + 1)
                        mm = pe.transpose(PS[0:w, 6 - 2 * (k % 2) + n // 4, P * (n % 4):P * (n % 4) + P], X[:, n, lo:lo + w], IDENT)
                    mm.then_inc(S("y_ps"), 1)

            pe.wait_ge(S("c_in"), 16)
            pe.wait_ge(S("g_in"), 16 * 7)
            pe.transpose(PS[:, 6, 0:84], GN[:], IDENT[0:84, 0:84]).then_inc(S("setup_pe"), 1)
            load_x(0)
            pe.wait_ge(S("s_in"), 32)
            for pg in range(4):
                pe.transpose(PS[:, 7, P * pg:P * pg + DB * BUF], SPN[:, P * pg:P * pg + P],
                             IDENT[0:DB * BUF, 0:DB * BUF]).then_inc(S("setup_pe"), 1)
            in_stage(0)
            index(0)
            load_x(1)
            in_stage(1)
            index(1)
            index_sample()
            for g in range(2):
                attend(g)
                if g:
                    attend_sample()
                    pe.wait_ge(S("osc"), 1)
                    pe.wait_ge(S("exps"), 8)
                pe.wait_ge(S("exp"), 32 * g + 32)
                pe.wait_ge(S("o_lo"), 8 * g + 8)
                pe.wait_ge(S("pool_in"), 32 * g + 32)
                linear(phase("out", g))
                post(g, 0)
                for layer in range(2):
                    for half in range(2):
                        q = phase("gu", g, layer, half)
                        if half == 0:
                            s = 2 * layer
                            linear(q, a_at_(g, SA_[s]), 3 * g + s, r_at(g, SPRE[s]))
                        else:
                            linear(q)
                        down_ph = phase("dn", g, layer, half)
                        down(down_ph)
                    if layer == 0:
                        post(g, 1)
                        linear(phase("v", g), a_at_(g, 1), 3 * g + 1, r_at(g, SPRE[1]))
                        gate(g)
                        linear(phase("oo", g), a_at_(g, 2))
                        post(g, 2)
                    else:
                        post(g, 3)
                result(g)

        @block.scalar
        def _(act):
            def hi_part(ph, i, p):
                wait(act, S(f"w_in{p}"), ph.win[p] + 16 * ph.nd * (i + 1))
                n = ph.kt * P
                act.activation(WH[:, p, 0:n], WR[:, p, 0:n], ACT.Copy).then_inc(S("w_hi"), 1)

            def loop(ph, take, early=False):
                def body(i, last, made=False):
                    for p in (0, 1):
                        wait(act, S("w_used"), ph.c0 + 2 * i + p + 1)
                        if made and p == 0:
                            pass
                        elif not last:
                            hi_part(ph, i + 1, p)
                        elif ph.next:
                            hi_part(ph.next, 0, p)
                        take(i, p)
                if early:
                    body(0, False, True)
                with act.Fori(1 if early else 0, ph.iters - 1) as i:
                    body(i, False)
                body(ph.iters - 1, True)

            def warm(func):
                act.activation(MX[0:1, 3, 0:1], const("ident")[0:1, 0:1], func).then_inc(S("warm"), 1)

            def root(r, g):
                act.wait_ge(S("n_sum"), r + 1)
                for lo, hi, w in ((0, 4, P), (4, 5, NS)):
                    if lo < NT[g]:
                        ins_ = act.activation(RT[0:w, 0, lo:hi], PS[0:w, 6, 2 * lo:2 * hi].rearrange("p (k a) -> p k a", a=2)[:, :, 0],
                                              ACT.Sqrt, scale=1.0 / D, bias=EPS)
                ins_.then_inc(S("n_rt"), 1)

            def split(a, n, g):
                act.wait_ge(S("a_t"), 8 * (a if a < 2 else 2 + g) + n + 1)
                act.activation(AR[:, 0, n, 0:T[g]], TT[:, n % 2, 0:T[g]], ACT.Copy).then_inc(S("a_hi"), 1)

            def load_x(g):
                dst = Y if g else X
                if g:
                    act.wait_ge(S("s_acc"), 16)
                    act.wait_ge(S("pool_out1"), 32)
                for n in range(NB):
                    act.wait_ge(S("xt_ps"), 8 * g + n + 1)
                    wait(act, S("ss_p"), 8 * g + n - 1)
                    src = PSF[:, 1024 * (n % 2):1024 * (n % 2) + T[g]]
                    act.activation(SQ[:, n % 2, 0:T[g]], src, ACT.Square).then_inc(S("sq_p"), 1)
                    act.activation(dst[:, n, 0:T[g]], src, ACT.Copy).then_inc(S("xt_cp"), 1)
                if g == 0:
                    for p in (0, 1):
                        hi_part(phase("in", 0), 0, p)
                root(g, g)
                for n in range(NB):
                    split(g, n, g)

            def index_queries(g, u):
                k = IDX_T[g][u - IDX_U[g][0]] - 4 * g
                wait(act, S("idx_mm"), 8 * (u - 1))
                for half in range(2):
                    r = slice(64 * half, 64 * half + 64)
                    ins_ = act.activation(IQS[r, u % 2, 4 * half:4 * half + 4, :], IQ[r, :, P * k:P * k + P], ACT.Copy)
                ins_.then_inc(S("iq_hi"), 1)

            def in_stage(g):
                ph = phase("in", g)
                for local in range(16):
                    p = local % 2
                    act.wait_ge(S("w_used"), ph.c0 + local + 1)
                    if local < 14:
                        hi_part(ph, (local + 2) // 2, p)
                    else:
                        hi_part(ph.next, 0, p)
                    free = S(f"free_a{p}")
                    if local < 12:
                        if local >= 2:
                            r = 10 * g + local - 2
                            act.wait_ge(S("rope_sw"), r + 1)
                            act.wait_ge(S("rope_t2"), r + 1)
                        act.activation(hv(SQ[:, p, 0:T[g]], g), lin(p, g), ACT.Copy).then_inc(free, 1)
                    else:
                        pg = local - 12
                        act.wait_ge(S("halo"), g + 1)
                        if g == 0:
                            act.activation(XPE[:, pg, BUF:BUF + 512], PS[:, 2 * p, :], ACT.Copy).then_inc(free, 1)
                        else:
                            act.activation(XPE[:, pg, BUF:BUF + 288], PS[:, 2 * p, 0:288], ACT.Copy)
                            act.activation(XPE[:, pg, BUF + 288:BUF + 512], PS[:, 2 * p + 1, 0:224], ACT.Copy)
                            dst = XPE[:, pg, BUF + 512:EXT].rearrange("p (b r) -> p b r", b=DB)[:, :, BUF:]
                            act.activation(dst, PS[:, 2 * p + 1, 224:288].rearrange("p (b t) -> p b t", b=DB), ACT.Copy).then_inc(free, 1)
                    if local == 12:
                        if g:
                            act.wait_ge(S("kv_out"), 16 * 12)
                        act.wait_ge(S("nat"), 4 * g + 1)
                        for lo, hi, w in ((0, 4, P), (4, 5, NS)):
                            if lo < NT[g]:
                                ins_ = act.activation(KN[0:w, lo:hi, :], PSF[0:w, 2048 + P * lo:2048 + P * hi].rearrange("p (k d) -> p k d", d=P), ACT.Copy)
                        ins_.then_inc(S("nat_a"), 1)
                        act.wait_ge(S("nat"), 4 * g + 2)
                        for lo, hi, w in ((0, 4, P), (4, 5, NS)):
                            if lo < NT[g]:
                                ins_ = act.activation(IKN[0:w, lo:hi, :], PSF[0:w, 3072 + P * lo:3072 + P * hi].rearrange("p (k d) -> p k d", d=P)[:, :, 0:HD], ACT.Copy)
                        ins_.then_inc(S("nat_a"), 1)
                    if local == 13:
                        act.wait_ge(S("nat"), 4 * g + 3)
                        for lo, hi, w in ((0, 4, P), (4, 5, NS)):
                            if lo < NT[g]:
                                ins_ = act.activation(VN[0:w, 4 * g + lo:4 * g + hi, :], PSF[0:w, 2048 + P * lo:2048 + P * hi].rearrange("p (k d) -> p k d", d=P), ACT.Copy)
                        ins_.then_inc(S("nat_a"), 1)
                n = 512 * (g + 1)
                act.activation(IKS[:, 0, 0:n], IKT[:, 0:n], ACT.Copy).then_inc(S("ik_hi"), 1)
                for pg in range(4):
                    act.wait_ge(S("pool_mm"), 4 * g + pg + 1)
                    wait(act, S(f"pool_out{pg % 2}"), 16 * (2 * g + pg // 2))
                    act.activation(hv(PHL[pg % 2][:, 0, 0:T[g]], g), aux(pg % 2, g), ACT.Identity,
                                   scale=GC[:, G_POOL + pg:G_POOL + pg + 1]).then_inc(S("pool_hi"), 1)
                index_queries(g, IDX_U[g][0])
                if g:
                    act.wait_ge(S("xp_ps"), 1)
                    act.activation(XNS[0:BUF, 0, :], PS[0:BUF, 0, :], ACT.Copy)
                    act.activation(XNS[0:NS, 1, :], PS[0:NS, 1, :], ACT.Copy).then_inc(S("xp_rows"), 1)

            def index(g):
                if g:
                    act.wait_ge(S("x_out"), 16)
                for u, t in zip(IDX_U[g], IDX_T[g]):
                    if u < IDX_U[g][-1]:
                        index_queries(g, u + 1)
                    m = P * (t + 1)
                    k = 1 if m <= 512 else 2
                    for h in range(8):
                        act.wait_ge(S("idx_mm"), 8 * u + h + 1)
                        wait(act, S("s_acc"), 8 * u + h - 1)
                        act.activation(R[:, h % 2, 0:m].rearrange("p (c n) -> p c n", c=k),
                                       PS[:, 4 + 2 * (h % 2):4 + 2 * (h % 2) + k, 0:m // k],
                                       ACT.Relu, scale=HD ** -0.5).then_inc(S("idx_r"), 1)

            def index_sample():
                act.wait_ge(S("iqz0"), 1)
                src = IQ[:, :, 512:T[1]].rearrange("p j (b t) -> p j b t", b=DB)
                dst = IQZ[:].rearrange("p b (a j t) -> p a j b t", a=2, j=4)
                for j in range(4):
                    act.activation(dst[0:64, 0, j], src[0:64, j], ACT.Copy)
                    ins_ = act.activation(dst[64:128, 1, j], src[64:128, j], ACT.Copy)
                ins_.then_inc(S("iqz"), 1)
                split_keys(0)
                act.wait_ge(S("s_acc"), 48)
                for b in range(DB + 1):
                    if b < DB:
                        act.wait_ge(S("ikt_ps"), b + 1)
                        wait(act, S("rel_mm"), b - 1)
                        act.activation(IKTB[b % 2][:], PS[:, b % 2, :], ACT.Copy).then_inc(S("ikt_cp"), 1)
                    if b:
                        act.wait_ge(S("rel_mm"), b)
                        wait(act, S("mix_mm"), b - 2)
                        act.activation(RS[:, (b - 1) % 2, :], PSF[0:NS, 1024:1024 + KCOL], ACT.Relu, scale=HD ** -0.5).then_inc(S("rs"), 1)

            def split_keys(g):
                n = 512 * (g + 1)
                if g:
                    act.wait_ge(S("w_used"), phase("dn", 0, 1, 1).c0 + 8)
                else:
                    act.wait_ge(S("iqz"), 1)
                for kv in range(2):
                    for r in range(2):
                        act.activation(KS[64 * r:64 * r + 64, kv, 0, 0:n], KT[64 * kv:64 * kv + 64, 0:n], ACT.Copy).then_inc(S("ks_hi"), 1)
                act.activation(VS[:, 0, 0:4 * (g + 1), :], VN[:, 0:4 * (g + 1), :], ACT.Copy).then_inc(S("ks_hi"), 1)

            def attend(g):
                def queries(t, half):
                    r = slice(64 * half, 64 * half + 64)
                    act.wait_ge(S("q_in"), 16 * (t + 1))
                    if t:
                        act.wait_ge(S("qk_mm"), 8 * (t - 1) + 4 * half + 4)
                    act.activation(QST[r, 4 * half:4 * half + 4, :], QR[r, :, :], ACT.Copy).then_inc(S("qst_hi"), 1)

                def exponentials(t, z):
                    hh = 8 * t + z
                    act.wait_ge(S("nm"), hh + 1)
                    if t % 4:
                        act.wait_ge(S("p_tr"), kbase(t - 1, z // 4) + t)
                    act.activation(cut(probs(hh)[:, 0:P * (t + 1)], t), logits(z % 2, t), ACT.Exp,
                                   bias=MX[:, 1, hh % 16:hh % 16 + 1], scale=HD ** -0.5,
                                   accum_out=MX[:, 2, hh % 16:hh % 16 + 1]).then_inc(S("exp"), 1)

                if g == 0:
                    act.wait_ge(S("mix_mm"), DB)
                    act.wait_ge(S("kv_out"), 16 * 27)
                    act.wait_ge(S("st_out"), 16 * 10)
                queries(4 * g, 0)
                queries(4 * g, 1)
                late = []
                for kind, t, z, kk in items(g):
                    if late and (kind == "qk" or kind == "tr" and kk == 0):
                        exponentials(*late.pop())
                    if kind == "qk":
                        if z == 4 and t % 4 < 3:
                            queries(t + 1, 0)
                        if z == 0 and t % 4 > 0:
                            queries(t, 1)
                        late = [(t, z)]
                    elif kind == "tr":
                        kc = kbase(t, z) + kk
                        act.wait_ge(S("p_tr"), kc + 1)
                        wait(act, S("pv_mm"), kc - 1)
                        act.activation(PT[:, kc % 2, 0, :], PS[:, 4 + kc % 2, :], ACT.Copy).then_inc(S("pt_hi"), 1)
                        if late:
                            exponentials(*late.pop())
                    elif kind == "o":
                        act.wait_ge(S("pv_mm"), kbase(t, z) + t + 1)
                        if g and t == 4 and z == 0:
                            act.wait_ge(S("y_out"), 64)
                        at = slice(P * (t - 4 * g), P * (t - 4 * g) + P)
                        act.activation(AR[64 * z:64 * z + 64, 0, 0:4, at],
                                       PS[64 * z:64 * z + 64, 6 + z, :].rearrange("p (j q) -> p j q", j=4), ACT.Copy).then_inc(S("o_hi"), 1)

            def attend_sample():
                act.wait_ge(S("q_in"), 16 * 9)
                act.wait_ge(S("qz0"), 1)
                src = QR[:, :, 0:NS].rearrange("p j (b t) -> p j b t", b=DB)
                dst = QZ[:].rearrange("p b (a j t) -> p a j b t", a=2, j=4)
                for j in range(4):
                    act.activation(dst[0:64, 0, j], src[0:64, j], ACT.Copy)
                    ins_ = act.activation(dst[64:128, 1, j], src[64:128, j], ACT.Copy)
                ins_.then_inc(S("qz"), 1)

                def page_keys(b):
                    act.wait_ge(S("kt_ps"), b + 1)
                    wait(act, S("qks_mm"), b - 1)
                    act.activation(KTB[:, b % 2, :], PS[:, 4 + b % 2, :], ACT.Copy).then_inc(S("ktb"), 1)

                def turned(b):
                    act.wait_ge(S("ps_tr"), b + 1)
                    wait(act, S("pvs_mm"), b - 1)
                    act.activation(PTS[:, b % 2, 0:NS * NPG], PS[:, 6, 0:NS * NPG], ACT.Copy)
                    act.activation(PTS[0:NS, b % 2, NS * NPG:NS * NPG + NS], PS[0:NS, 6, NS * NPG:NS * NPG + NS], ACT.Copy).then_inc(S("pts"), 1)

                page_keys(0)
                for b in range(DB):
                    if b + 1 < DB:
                        page_keys(b + 1)
                    act.wait_ge(S("nms"), b + 1)
                    wait(act, S("ps_tr"), b - 1)
                    act.activation(PRS[:, b % 2, :], PSF[0:NS, 1024 * (b % 2):1024 * (b % 2) + KCOL], ACT.Exp,
                                   bias=MX[0:NS, 1, b:b + 1], scale=HD ** -0.5, accum_out=MX[0:NS, 2, b:b + 1]).then_inc(S("exps"), 1)
                    if b:
                        turned(b - 1)
                turned(DB - 1)
                act.wait_ge(S("pvs_mm"), DB)
                for half in range(2):
                    r = slice(64 * half, 64 * half + 64)
                    for j in range(4):
                        ins_ = act.activation(AR[r, 0, j, 512:T[1]].rearrange("p (b t) -> p b t", b=DB),
                                              PS[r, 7, :].rearrange("p (b h t) -> p h b t", b=DB, h=8)[:, 4 * half + j], ACT.Copy)
                ins_.then_inc(S("osc_hi"), 1)

            def out_like(ph, mp):
                g = ph.g

                def take(i, p):
                    n = 2 * i + p
                    wait(act, S("ss_p"), 8 * mp + n - 1)
                    act.activation(hv(SQ[:, p, 0:T[g]], g), lin(p, g), ACT.Square).then_inc(S("sq_p"), 1)
                    act.activation(hv(flat(Y[:, ds(n, 1), 0:T[g]]), g), lin(p, g), ACT.Copy).then_inc(S(f"free_a{p}"), 1)
                loop(ph, take)

            def gate_up(ph):
                g = ph.g
                if g and ph.layer:
                    act.wait_ge(S("z_out"), 16)

                def take(i, p):
                    if p == 0:
                        wait(act, S("free_d0"), ph.base["d", 0] + i + 1)
                        act.activation(TT[:, 0, 0:T[g]], TT[:, 0, 0:T[g]], ACT.Silu).then_inc(S("silu"), 1)
                    else:
                        wait(act, S("free_d1"), ph.base["d", 1] + i + 1)
                        act.activation(flat(HR[:, 0, ds(i, 1), 0:T[g]]), TT[:, 1, 0:T[g]], ACT.Copy).then_inc(S("h_hi"), 1)
                warm(ACT.Silu)
                loop(ph, take, ph.half == 0)

            def down(ph, mp):
                g = ph.g

                def first(i, p):
                    act.activation(hv(flat(Y[:, ds(2 * i + p, 1), 0:T[g]]), g), lin(p, g), ACT.Copy).then_inc(S(f"free_a{p}"), 1)

                def second(i, p):
                    n = 2 * i + p
                    wait(act, S(f"free_d{p}"), ph.base["d", p] + i + 1)
                    wait(act, S("ss_p"), 8 * mp + n - 1)
                    act.activation(SQ[:, p, 0:T[g]], flat(Y[:, ds(n, 1), 0:T[g]]), ACT.Square).then_inc(S("sq_p"), 1)
                loop(ph, second if ph.half else first)

            def post(g, s):
                root(r_at(g, SPOST[s]), g)
                if s == 3:
                    return
                m = 3 * g + s
                for n in range(NB):
                    base, layer = ((G_FFN_PRE, 0), (G_MIX_PRE, 1), (G_FFN_PRE, 1))[s]
                    act.wait_ge(S("x_new"), 8 * (4 * g + s) + n + 1)
                    act.activation(AR[:, 0, n, 0:T[g]], X[:, n, 0:T[g]], ACT.Identity, scale=gain(base, layer, n)).then_inc(S("a_hi"), 1)
                    act.activation(Y[:, n, 0:T[g]], X[:, n, 0:T[g]], ACT.Identity, scale=gain(base, layer, n)).then_inc(S("z_in"), 1)
                    if n >= 2:
                        act.wait_ge(S("ss_m"), 8 * m + n - 1)
                    act.activation(SQ[:, n % 2, 0:T[g]], X[:, n, 0:T[g]], ACT.Square).then_inc(S("sq_m"), 1)
                nxt = (phase("gu", g), phase("v", g), phase("gu", g, 1))[s]
                act.wait_ge(S("w_used"), nxt.c0 + 1)
                hi_part(nxt, 1, 0)
                root(r_at(g, SPRE[s]), g)
                act.wait_ge(S("n_b"), r_at(g, SPRE[s]) + 1)
                act.activation(RB[:, 0:T[g]], PSF[:, 2048:2048 + T[g]], ACT.Copy).then_inc(S("rb"), 1)

            def gate(g):
                ph = phase("v", g)
                warm(ACT.Gelu)

                def take(i, p):
                    wait(act, S(f"free_d{p}"), ph.base["d", p] + i + 1)
                    v = flat(Y[:, ds(2 * i + p, 1), 0:T[g]])
                    act.activation(v, v, ACT.Gelu).then_inc(S("v_gelu"), 1)
                loop(ph, take, True)
                act.wait_ge(S("ws_t"), g + 1)
                act.activation(WMT[:].rearrange("p g s -> p (g s)"), PSF[:, 2048:3072], ACT.Copy)
                act.activation(WM8T[:].rearrange("p g s -> p (g s)"), PS[0:NS, 6, :], ACT.Copy).then_inc(S("wmt"), 1)
                ph = phase("u", g)

                def centred(n):
                    act.wait_ge(S("ln_c"), 8 * g + n + 1)
                    if n >= 2:
                        act.wait_ge(S("ln_ss"), 8 * g + n - 1)
                    act.activation(SQ[:, n % 2, 0:T[g]], Y[:, n, 0:T[g]], ACT.Square).then_inc(S("ln_sq"), 1)

                def scaled(n):
                    act.wait_ge(S("ln_t"), 8 * g + n + 1)
                    act.activation(Y[:, n, 0:T[g]], TT[:, n % 2, 0:T[g]], ACT.Identity, scale=gain(G_LN, 0, n),
                                   bias=gain(B_LN, 0, n)).then_inc(S("ln_z"), 1)

                for local in range(8):
                    p = local % 2
                    act.wait_ge(S("w_used"), ph.c0 + local + 1)
                    if local < 6:
                        hi_part(ph, (local + 2) // 2, p)
                    else:
                        hi_part(ph.next, 0, p)
                    act.wait_ge(S(f"free_d{p}"), ph.base["d", p] + local // 2 + 1)
                    act.activation(U[:, local, 0:T[g]], U[:, local, 0:T[g]], ACT.Gelu).then_inc(S("u_gelu"), 1)
                    if 1 <= local <= 3:
                        for n in range(3 * local - 3, min(3 * local, NB)):
                            centred(n)
                    if local == 4:
                        root(r_at(g, 4), g)
                    if local >= 6:
                        for n in range(4 * local - 24, 4 * local - 20):
                            scaled(n)
                a = a_at_(g, 2)
                for n in range(NB):
                    if n % 2:
                        act.wait_ge(S("z_ps"), 8 * g + n + 1)
                        z_rows(act, g, n).then_inc(S("zc_a"), 1)
                    if n >= 2:
                        split(a, n - 2, g)
                split(a, 6, g)
                split(a, 7, g)

            def z_rows(eng, g, n):
                x = 1 - n % 2
                base = (4 + 2 * x) * 512
                ins_ = eng.activation(ZN[:, 0:4, P * n:P * n + P], PSF[:, base:base + 512].rearrange("p (k d) -> p k d", d=P), ACT.Copy)
                if g:
                    ins_ = eng.activation(ZN[0:NS, 4, P * n:P * n + P], PSF[0:NS, base + 512:base + 512 + P], ACT.Copy)
                return ins_

            def result(g):
                if g == 0:
                    split_keys(1)
                for k, lo, w in tiles(g):
                    act.wait_ge(S("y_ps"), 4 * g + k + 1)
                    act.activation(ON[0:w, k, :], PSF[0:w, 3072 - 1024 * (k % 2):3072 - 1024 * (k % 2) + D], ACT.Copy).then_inc(S("y_cp"), 1)

            act.wait_ge(S("setup_pe"), 1)
            act.activation(GC[:], PS[:, 6, 0:84], ACT.Copy).then_inc(S("setup_a"), 1)
            load_x(0)
            act.wait_ge(S("setup_pe"), 5)
            for pg in range(4):
                act.activation(XPE[:, pg, BUF + 512:EXT].rearrange("p (b r) -> p b r", b=DB)[:, :, 0:BUF],
                               PS[:, 7, P * pg:P * pg + DB * BUF].rearrange("p (b r) -> p b r", b=DB), ACT.Copy).then_inc(S("setup_a"), 1)
            in_stage(0)
            index(0)
            load_x(1)
            in_stage(1)
            index(1)
            index_sample()
            for g in range(2):
                attend(g)
                if g:
                    attend_sample()
                out_like(phase("out", g), norm_at("post", g, 0))
                post(g, 0)
                for layer in range(2):
                    for half in range(2):
                        gate_up(phase("gu", g, layer, half))
                        down(phase("dn", g, layer, half), norm_at("post", g, 1 + 2 * layer))
                    if layer == 0:
                        post(g, 1)
                        gate(g)
                        out_like(phase("oo", g), norm_at("post", g, 2))
                        post(g, 2)
                    else:
                        post(g, 3)
                result(g)

        @block.gpsimd
        def _(pool):
            def lo_part(ph, i, p):
                wait(pool, S("w_hi"), ph.c0 + 2 * i + p + 1)
                n = ph.kt * P
                pool.tensor_tensor(WL[:, p, 0:n], WR[:, p, 0:n], WH[:, p, 0:n].bitcast(F32), ALU.subtract).then_inc(S("w_lo"), 1)

            def loop(ph):
                with pool.Fori(0, ph.iters - 1) as i:
                    lo_part(ph, i + 1, 0)
                    lo_part(ph, i + 1, 1)
                if ph.next:
                    lo_part(ph.next, 0, 0)
                    lo_part(ph.next, 0, 1)

            def gated_loop(ph, m):
                g = ph.g

                def turn(i, nxt, j):
                    lo_part(nxt, j, 0)
                    if isinstance(i, int) and i == 0:
                        pool.wait_ge(S("rb"), m + 1)
                    wait(pool, S("silu"), ph.hb + i)
                    pool.tensor_tensor(TT[:, 0, 0:T[g]], TT[:, 0, 0:T[g]], RB[:, 0:T[g]], ALU.mult).then_inc(S("gated"), 1)
                    lo_part(nxt, j, 1)

                turn(0, ph, 1)
                with pool.Fori(1, ph.iters - 1) as i:
                    turn(i, ph, i + 1)
                turn(ph.iters - 1, ph.next, 0)

            def split(a, n, g, src=None, m=0):
                pool.wait_ge(S("a_hi"), 8 * a + n + 1)
                if src is not None:
                    pool.wait_ge(S("z_in"), 8 * m + n + 1)
                src = TT[:, n % 2, 0:T[g]] if src is None else src
                pool.tensor_tensor(AR[:, 1, n, 0:T[g]], src, AR[:, 0, n, 0:T[g]].bitcast(F32), ALU.subtract).then_inc(S("a_lo"), 1)

            def in_stage(g):
                ph = phase("in", g)
                pool.wait_ge(S("rope_in"), 16 * (g + 1))
                for local in range(16):
                    p = local % 2
                    if local < 14:
                        lo_part(ph, (local + 2) // 2, p)
                    else:
                        lo_part(ph.next, 0, p)
                    if local < 10:
                        r = 10 * g + local
                        pool.wait_ge(S(f"free_a{p}"), ph.base["a", p] + local // 2 + 1)
                        wait(pool, S("rope_out"), r)
                        pool.tensor_tensor(TT[:, 1, 0:T[g]], SQ[:, p, 0:T[g]], RP[:, 0, 0:T[g]], ALU.mult).then_inc(S("rope_t2"), 1)

            def index(g):
                pool.wait_ge(S("w_lo"), phase("in", g).c0 + 18)
                for u, t in zip(IDX_U[g], IDX_T[g]):
                    at = slice(P * (t - 4 * g), P * (t - 4 * g) + P)
                    pool.wait_ge(S("iq_hi"), u + 1)
                    for half in range(2):
                        r, o = slice(64 * half, 64 * half + 64), slice(64 - 64 * half, 128 - 64 * half)
                        pool.tensor_tensor(IQS[o, u % 2, 4 * half:4 * half + 4, :], IQ[r, :, at],
                                           IQS[r, u % 2, 4 * half:4 * half + 4, :].bitcast(F32), ALU.subtract).then_inc(S("iq_lo"), 1)
                        pool.wait_ge(S("iq_lo"), 2 * u + half + 1)

            def split_keys(g):
                n = 512 * (g + 1)
                pool.wait_ge(S("w_lo"), phase("out", g).c0 + 2)
                for kv in range(2):
                    src = slice(64 * kv, 64 * kv + 64)
                    pool.wait_ge(S("ks_hi"), 5 * g + 2 * kv + 2)
                    for r in range(2):
                        pool.tensor_tensor(KS[64 * r:64 * r + 64, kv, 1, 0:n], KT[src, 0:n], KS[src, kv, 0, 0:n].bitcast(F32),
                                           ALU.subtract).then_inc(S("ks_lo"), 1)
                        pool.wait_ge(S("ks_lo"), 5 * g + 2 * kv + r + 1)
                pool.wait_ge(S("ks_hi"), 5 * g + 5)
                pool.tensor_tensor(VS[:, 1, 0:4 * (g + 1), :], VN[:, 0:4 * (g + 1), :], VS[:, 0, 0:4 * (g + 1), :].bitcast(F32),
                                   ALU.subtract).then_inc(S("ks_lo"), 1)
                pool.wait_ge(S("ks_lo"), 5 * g + 5)

            def attend(g):
                def queries(t, half):
                    r, o = slice(64 * half, 64 * half + 64), slice(64 - 64 * half, 128 - 64 * half)
                    pool.wait_ge(S("qst_hi"), 2 * t + half + 1)
                    pool.tensor_tensor(QST[o, 4 * half:4 * half + 4, :], QR[r, :, :],
                                       QST[r, 4 * half:4 * half + 4, :].bitcast(F32), ALU.subtract).then_inc(S("qst_lo"), 1)
                    pool.wait_ge(S("qst_lo"), 2 * t + half + 1)

                queries(4 * g, 0)
                queries(4 * g, 1)
                for kind, t, z, kk in items(g):
                    if kind != "qk":
                        continue
                    hh = 8 * t + z
                    wait(pool, S("p_norm"), hh)
                    if z == 4 and t % 4 < 3:
                        queries(t + 1, 0)
                    if z == 0 and t % 4 > 0:
                        queries(t, 1)
                    pool.wait_ge(S("inv"), hh + 1)
                    pr = probs(hh)[:, 0:P * (t + 1)]
                    pool.tensor_tensor(pr, pr, MX[:, 3, hh % 16:hh % 16 + 1].to_broadcast([P, P * (t + 1)]), ALU.mult).then_inc(S("p_norm"), 1)

            def post(g, s):
                if s == 3:
                    return
                for n in range(NB):
                    split(a_at_(g, SA_[s]), n, g, Y[:, n, 0:T[g]], 3 * g + s)

            for p in (0, 1):
                lo_part(phase("in", 0), 0, p)
            for n in range(NB):
                split(0, n, 0)
            in_stage(0)
            index(0)
            for n in range(NB):
                split(1, n, 1)
            in_stage(1)
            index(1)
            for g in range(2):
                split_keys(g)
                attend(g)
                loop(phase("out", g))
                post(g, 0)
                for layer in range(2):
                    for half in range(2):
                        gated_loop(phase("gu", g, layer, half), 3 * g + 2 * layer)
                        loop(phase("dn", g, layer, half))
                    if layer == 0:
                        pool.wait_ge(S("w_used"), phase("dn", g, 0, 1).c0 + 8)
                        pool.memset(WS8[:], 0.0).then_inc(S("ws8_zero"), 1)
                        post(g, 1)
                        loop(phase("v", g))
                        ph = phase("u", g)
                        for local in range(8):
                            if local < 6:
                                lo_part(ph, (local + 2) // 2, local % 2)
                            else:
                                lo_part(ph.next, 0, local % 2)
                        for n in range(NB):
                            split(a_at_(g, 2), n, g)
                        loop(phase("oo", g))
                        post(g, 2)

        @block.vector
        def _(dve):
            def sum_zero(z):
                dve.memset(SS[:], 0.0).then_inc(S("ss_zero"), 1)

            def add_square(mp, n, p, g, z):
                wait(dve, S("sq_p"), 8 * mp + n + 1)
                wait(dve, S("ss_p"), 8 * mp + n)
                dve.wait_ge(S("ss_zero"), z + 1)
                dve.tensor_tensor(SS[:, 0:T[g]], SS[:, 0:T[g]], SQ[:, p, 0:T[g]], ALU.add).then_inc(S("ss_p"), 1)

            def add_block(ready, done, count, n, g):
                dve.wait_ge(S(ready), count + n + 1)
                if n:
                    dve.wait_ge(S(done), count + n)
                    dve.tensor_tensor(SS[:, 0:T[g]], SS[:, 0:T[g]], SQ[:, n % 2, 0:T[g]], ALU.add).then_inc(S(done), 1)
                else:
                    dve.tensor_copy(SS[:, 0:T[g]], SQ[:, 0, 0:T[g]]).then_inc(S(done), 1)

            def diagonals(r, g):
                dve.wait_ge(S("n_rt"), r + 1)
                dve.reciprocal(RT[:, 1, 0:NT[g]], RT[:, 0, 0:NT[g]]).then_inc(S("n_rc"), 1)
                dve.wait_ge(S("n_rc"), r + 1)
                n = NT[g]
                dve.tensor_tensor(DG[:, 0:n, :], IDENT.unsqueeze(1).to_broadcast([P, n, P]),
                                  RT[:, 1, 0:n].unsqueeze(2).to_broadcast([P, n, P]), ALU.mult).then_inc(S("n_dg"), 1)

            def spread(g):
                return PSF[:, 2048:2048 + T[g]]

            def split(a, g, src, base, layer):
                for n in range(NB):
                    wait(dve, S("a_lo"), 8 * a + n - 1)
                    dve.scalar_tensor_tensor(out=TT[:, n % 2, 0:T[g]], in0=src[:, n, 0:T[g]], scalar=gain(base, layer, n),
                                             in1=spread(g), op0=ALU.mult, op1=ALU.mult).then_inc(S("a_t"), 1)

            def load_x(g):
                sum_zero(g)
                for n in range(NB):
                    add_square(g, n, n % 2, g, g)
                diagonals(g, g)
                dve.wait_ge(S("n_b"), g + 1)
                dve.wait_ge(S("xt_cp"), 8 * g + 8)
                split(g, g, Y if g else X, G_MIX_PRE, 0)

            rounds = [0]

            def top_max(spans, r):
                wait(dve, S("top"), 2 * r)
                for m, s in spans:
                    ins_ = dve.max(M8[0:s.shape[0], m, :], s)
                ins_.then_inc(S("top"), 1)

            def top_mark(spans, r):
                wait(dve, S("top"), 2 * r + 1)
                for m, s in spans:
                    ins_ = dve.match_replace(out=s, in_to_replace=M8[0:s.shape[0], m, :], in_values=s, imm_value=CHOSEN)
                ins_.then_inc(S("top"), 1)

            def top_round(spans, r):
                top_max(spans, r)
                top_mark(spans, r)

            def in_stage(g):
                ph = phase("in", g)
                if g:
                    dve.tensor_copy(XPE[:, :, 0:BUF], XPE[:, :, 512:512 + BUF]).then_inc(S("halo"), 1)

                def pool_windows(pg):
                    w = POOLW[pg]
                    n = EXT if g else BUF + 512
                    p = pg % 2
                    dve.wait_ge(S(f"free_a{p}"), ph.base["a", p] + 7 + pg // 2)
                    dve.wait_ge(S("nat"), 4 * g + 4)
                    src = XPE[:, pg, 0:n]
                    base = sum((q + 2 + (1 if g == 0 else 0)) for q in range(pg)) + (0 if g == 0 else 18)
                    step = 1
                    count = base
                    wait(dve, S("win"), base)
                    wait(dve, S("pool_d"), 4 * g + pg)
                    for q in range(pg + 1):
                        dst = (PA, PB)[q % 2]
                        n -= step
                        if q:
                            dve.wait_ge(S("win"), count)
                        dve.tensor_tensor(dst[:, 0:n], src[:, 0:n], src[:, step:step + n], ALU.add).then_inc(S("win"), 1)
                        count += 1
                        src = dst
                        step *= 2
                    dve.wait_ge(S("win"), count)
                    if pg >= 2:
                        dve.wait_ge(S("pool_mm"), 4 * g + pg - 1)
                    else:
                        dve.wait_ge(S(f"q_out{pg}"), 16 * (2 * g + 2))
                    first = 16 - w
                    ins_ = dve.scalar_tensor_tensor(out=PD[:, p, 0:512], in0=src[:, first:first + 512], scalar=1.0 / w,
                                                    in1=XPE[:, pg, BUF:BUF + 512], op0=ALU.mult, op1=ALU.subtract)
                    if g == 0:
                        a = CN["inv"][0] + 16 * pg
                        ins_.then_inc(S("win"), 1)
                        dve.tensor_tensor(T16[:], src[:, first:first + 16], CT[:, a:a + 16], ALU.mult).then_inc(S("win"), 1)
                        dve.wait_ge(S("win"), count + 2)
                        ins_ = dve.tensor_tensor(PD[:, p, 0:16], T16[:], XPE[:, pg, BUF:BUF + 16], ALU.subtract)
                    else:
                        ins_.then_inc(S("win"), 1)
                        ins_ = dve.scalar_tensor_tensor(out=PD[:, p, 512:T[1]].rearrange("p (b t) -> p b t", b=DB), in0=sample_windows(src, first),
                                                        scalar=1.0 / w,
                                                        in1=XPE[:, pg, BUF + 512:EXT].rearrange("p (b r) -> p b r", b=DB)[:, :, BUF:],
                                                        op0=ALU.mult, op1=ALU.subtract)
                    ins_.then_inc(S("pool_d"), 1)

                def sample_windows(src, first):
                    a = BUF + 512
                    return src[:, a:a + DB * (BUF + DT)].rearrange("p (b r) -> p b r", b=DB)[:, :, first:first + DT]

                def pool_lo(pg):
                    dve.wait_ge(S("pool_hi"), 4 * g + pg + 1)
                    dve.scalar_tensor_tensor(out=hv(PHL[pg % 2][:, 1, 0:T[g]], g), in0=aux(pg % 2, g), scalar=GC[:, G_POOL + pg:G_POOL + pg + 1],
                                             in1=hv(PHL[pg % 2][:, 0, 0:T[g]], g).bitcast(F32), op0=ALU.mult, op1=ALU.subtract).then_inc(S("pool_lo"), 1)

                def rotate(local):
                    r, p = 10 * g + local, local % 2
                    dve.wait_ge(S("rope_sw"), r + 1)
                    if local == 0:
                        dve.wait_ge(S("rope_in"), 16 * (g + 1))
                    wait(dve, S("rope_out"), r)
                    dve.tensor_tensor(hv(TT[:, 0, 0:T[g]], g), aux(p, g), hv(RP[:, 1, 0:T[g]], g), ALU.mult).then_inc(S("rope_t1"), 1)
                    dve.wait_ge(S("rope_t1"), r + 1)
                    dve.wait_ge(S("rope_t2"), r + 1)
                    if local < 8:
                        j = local // 2
                        if p == 0:
                            wait(dve, S(f"q_out{j % 2}"), 16 * (2 * g + j // 2))
                            dst = QT[:, j % 2, 0:T[g]]
                        else:
                            dst = IQ[:, j, 0:T[g]]
                    else:
                        dst = (KT, IKT)[p][:, 512 * g:512 * g + T[g]]
                    dve.tensor_tensor(dst, TT[:, 0, 0:T[g]], TT[:, 1, 0:T[g]], ALU.add).then_inc(S("rope_out"), 1)

                spans = [(2, score(2)), (3, score(3))]
                for local in range(16):
                    if local < 10:
                        rotate(local)
                    if local == 13:
                        dve.wait_ge(S("nat"), 4 * g + 4)
                        for lo, hi, w in ((0, 4, P), (4, 5, NS)):
                            if lo < NT[g]:
                                ins_ = dve.tensor_scalar(IW[0:w, 4 * g + lo:4 * g + hi, :],
                                                         PSF[0:w, 3072 + P * lo:3072 + P * hi].rearrange("p (k d) -> p k d", d=P)[:, :, 0:8],
                                                         8 ** -0.5, None, ALU.mult)
                        if g:
                            ins_ = dve.tensor_copy(IWT[:], SQ[0:8, 1, 512:T[1]])
                        ins_.then_inc(S("iw_rows"), 1)
                        pool_windows(0)
                    if local >= 14:
                        pool_windows(local - 13)
                    if local == 15:
                        pool_lo(0)
                    if g and local % 2 and local < 12:
                        for q in range(4):
                            top_round(spans, 4 * (local // 2) + q)
                pool_lo(1)
                pool_windows(3)
                if g:
                    dve.tensor_copy(GXS[:].rearrange("p g (b t) -> p g b t", b=DB),
                                    XPE[:, :, BUF + 512:EXT].rearrange("p g (b r) -> p g b r", b=DB)[:, :, :, BUF:]).then_inc(S("xs_cp"), 1)
                n = 512 * (g + 1)
                dve.wait_ge(S("ik_hi"), g + 1)
                dve.tensor_tensor(IKS[:, 1, 0:n], IKT[:, 0:n], IKS[:, 0, 0:n].bitcast(F32), ALU.subtract).then_inc(S("ik_lo"), 1)
                pool_lo(2)
                pool_lo(3)

            def index(g):
                if g:
                    for b in range(2):
                        dve.wait_ge(S(f"pool_out{b}"), 64)
                    dve.wait_ge(S("xp_rows"), 1)
                for u, t in zip(IDX_U[g], IDX_T[g]):
                    s = score(t)
                    for h in range(8):
                        hh = 8 * u + h
                        dve.wait_ge(S("idx_r"), hh + 1)
                        w = IW[:, t, h:h + 1]
                        r = R[:, h % 2, 0:P * (t + 1)]
                        if h == 0:
                            if u == 0 or u == 2:
                                dve.wait_ge(S("iw_rows"), g + 1)
                            ins_ = dve.tensor_scalar(s, r, w, None, ALU.mult)
                        else:
                            dve.wait_ge(S("s_acc"), hh)
                            ins_ = dve.scalar_tensor_tensor(out=s, in0=r, scalar=w, in1=s, op0=ALU.mult, op1=ALU.add)
                        ins_.then_inc(S("s_acc"), 1)
                    diag = s[:, P * t:P * t + P]
                    dve.wait_ge(S("s_acc"), 8 * u + 8)
                    dve.tensor_tensor(diag, diag, TRIL, ALU.mult).then_inc(S("s_fix"), 1)
                    dve.wait_ge(S("s_fix"), 2 * u + 1)
                    dve.tensor_tensor(diag, diag, const("neg"), ALU.add).then_inc(S("s_fix"), 1)
                dve.wait_ge(S("s_fix"), 2 * IDX_U[g][-1] + 2)

            def index_sample():
                dve.wait_ge(S("spread_mm"), 1)
                g_b = PS[0:NS, 6:7, 0:NS].to_broadcast([NS, DB, NS])
                dve.scalar_tensor_tensor(out=MS[:], in0=const("dm", NS).rearrange("p (b c) -> p b c", b=DB), scalar=8 ** -0.5,
                                         in1=g_b, op0=ALU.mult, op1=ALU.mult).then_inc(S("ms"), 1)
                dve.memset(SCS[:, KCOL:KCOL + 8], DUMMY).then_inc(S("scs"), 1)
                for q in range(24, 32):
                    top_round([(2, score(2)), (3, score(3))], q)
                dve.wait_ge(S("mix_mm"), DB)
                dve.tensor_copy(SCS[:, 0:PAST], PS[0:NS, 4, :]).then_inc(S("scs"), 1)
                dve.tensor_tensor(SCS[:, PAST:KCOL], PS[0:NS, 5, 0:NS], const("m01s", NS), ALU.mult).then_inc(S("scs"), 1)
                dve.wait_ge(S("scs"), 3)
                dve.tensor_tensor(SCS[:, PAST:KCOL], SCS[:, PAST:KCOL], const("negs", NS), ALU.add).then_inc(S("scs"), 1)
                dve.wait_ge(S("scs"), 4)

            def attend(g):
                def mask(t):
                    if t >= 2:
                        if t == 2:
                            dve.wait_ge(S("top"), 64)
                        if t == 4:
                            dve.wait_ge(S("top"), 2 * (32 + 17 + 32))
                        if t >= 4:
                            dve.wait_ge(S("qk_mm"), 8 * (t - 1))
                        dve.tensor_scalar(MK[:, t % 2, 0:P * (t + 1)], score(t), SPLITTER, MASK, ALU.is_gt, ALU.mult).then_inc(S("mk"), 1)

                def invert(hh):
                    dve.wait_ge(S("exp"), hh + 1)
                    c = slice(hh % 16, hh % 16 + 1)
                    dve.reciprocal(MX[:, 3, c], MX[:, 2, c]).then_inc(S("inv"), 1)

                pending, step = [], 0
                LAG = 2
                mask(4 * g)
                for kind, t, z, kk in items(g):
                    if kind == "tr" and kk == 0:
                        for q, _ in pending:
                            invert(q)
                        pending = []
                    if kind == "qk":
                        hh = 8 * t + z
                        dve.wait_ge(S("qk_mm"), hh + 1)
                        c = slice(hh % 16, hh % 16 + 1)
                        axes = AX.X if t < 4 else AX.XY
                        src = logits(z % 2, t)
                        if t < 4:
                            src = src.rearrange("p c n -> p (c n)")
                        dve.tensor_reduce(MX[:, 0, c], src, axes, ALU.max).then_inc(S("mx"), 1)
                        dve.wait_ge(S("mx"), hh + 1)
                        dve.tensor_scalar(MX[:, 1, c], MX[:, 0, c], -(HD ** -0.5), None, ALU.mult).then_inc(S("nm"), 1)
                        if z == 4 and t % 4 < 3:
                            mask(t + 1)
                        pending.append((hh, step))
                    elif kind == "tr":
                        kc = kbase(t, z) + kk
                        dve.wait_ge(S("pt_hi"), kc + 1)
                        dve.tensor_tensor(PT[:, kc % 2, 1, :], PS[:, 4 + kc % 2, :], PT[:, kc % 2, 0, :].bitcast(F32), ALU.subtract).then_inc(S("pt_lo"), 1)
                    elif kind == "o":
                        dve.wait_ge(S("o_hi"), 2 * t + z + 1)
                        r = slice(64 * z, 64 * z + 64)
                        at = slice(P * (t - 4 * g), P * (t - 4 * g) + P)
                        dve.tensor_tensor(AR[r, 1, 0:4, at], PS[r, 6 + z, :].rearrange("p (j q) -> p j q", j=4),
                                          AR[r, 0, 0:4, at].bitcast(F32), ALU.subtract).then_inc(S("o_lo"), 1)
                    if kind != "pv":
                        step += 1
                        while pending and pending[0][1] + LAG < step:
                            invert(pending.pop(0)[0])

            def attend_sample():
                dve.wait_ge(S("qk_mm"), 64)
                dve.memset(QZ[:], 0.0).then_inc(S("qz0"), 1)
                dve.tensor_scalar(MKS[:], SCS[:, 0:KCOL], SPLITTER, MASK, ALU.is_gt, ALU.mult).then_inc(S("mks"), 1)
                for b in range(DB):
                    dve.wait_ge(S("qks_mm"), b + 1)
                    dve.tensor_reduce(MX[0:NS, 0, b:b + 1], PSF[0:NS, 1024 * (b % 2):1024 * (b % 2) + KCOL], AX.X, ALU.max).then_inc(S("mxs"), 1)
                    dve.wait_ge(S("mxs"), b + 1)
                    dve.tensor_scalar(MX[0:NS, 1, b:b + 1], MX[0:NS, 0, b:b + 1], -(HD ** -0.5), None, ALU.mult).then_inc(S("nms"), 1)
                    dve.wait_ge(S("exps"), b + 1)
                    dve.reciprocal(MX[0:NS, 3, b:b + 1], MX[0:NS, 2, b:b + 1]).then_inc(S("invs"), 1)
                    dve.wait_ge(S("invs"), b + 1)
                    pr = PRS[:, b % 2, :]
                    dve.tensor_scalar(pr, pr, MX[0:NS, 3, b:b + 1], None, ALU.mult).then_inc(S("ps_norm"), 1)
                dve.wait_ge(S("osc_hi"), 1)
                for half in range(2):
                    r = slice(64 * half, 64 * half + 64)
                    for j in range(4):
                        at = AR[r, 0, j, 512:T[1]].rearrange("p (b t) -> p b t", b=DB)
                        lo = AR[r, 1, j, 512:T[1]].rearrange("p (b t) -> p b t", b=DB)
                        ins_ = dve.tensor_tensor(lo, PS[r, 7, :].rearrange("p (b h t) -> p h b t", b=DB, h=8)[:, 4 * half + j],
                                                 at.bitcast(F32), ALU.subtract)
                ins_.then_inc(S("osc"), 1)

            def out_like(ph, g, s, extra=None):
                mp = norm_at("post", g, s)
                z = z_at(g, SZ[s])
                sum_zero(z)
                with dve.Fori(0, ph.iters) as i:
                    for p in (0, 1):
                        add_square(mp, 2 * i + p, p, g, z)
                        if extra:
                            extra(i, p)

            big = [(m, score(m + 4)) for m in range(4)]
            BIG0 = 32 + 17

            def gate_up(ph, first=None):
                g = ph.g
                dve.wait_ge(S("rb"), 3 * g + 2 * ph.layer + 1)
                with dve.Fori(0, ph.iters) as i:
                    wait(dve, S("w_used"), ph.c0 + 2 * i + 1)
                    wait(dve, S("free_d1"), ph.base["d", 1] + i)
                    dve.tensor_tensor(hv(TT[:, 0, 0:T[g]], g), lin(0, g), hv(RB[:, 0:T[g]], g), ALU.mult).then_inc(S("free_d0"), 1)
                    if first is not None:
                        top_max(big, first + i)
                    wait(dve, S("w_used"), ph.c0 + 2 * i + 2)
                    wait(dve, S("gated"), ph.hb + i)
                    wait(dve, S("h_lo"), ph.hb + i)
                    dve.tensor_tensor(hv(TT[:, 1, 0:T[g]], g), lin(1, g), hv(TT[:, 0, 0:T[g]], g), ALU.mult).then_inc(S("free_d1"), 1)
                    wait(dve, S("h_hi"), ph.hb + i)
                    dve.tensor_tensor(flat(HR[:, 1, ds(i, 1), 0:T[g]]), TT[:, 1, 0:T[g]], flat(HR[:, 0, ds(i, 1), 0:T[g]].bitcast(F32)),
                                      ALU.subtract).then_inc(S("h_lo"), 1)
                    if first is not None:
                        top_mark(big, first + i)

            def down(ph, s, first=None):
                g = ph.g
                if ph.half == 0:
                    if first is not None:
                        with dve.Fori(0, ph.iters) as i:
                            top_round(big, first + i)
                    return
                mp, z = norm_at("post", g, s), z_at(g, SZ[s])
                sum_zero(z)
                with dve.Fori(0, ph.iters) as i:
                    for p in (0, 1):
                        n = 2 * i + p
                        wait(dve, S("w_used"), ph.c0 + n + 1)
                        y = hv(flat(Y[:, ds(n, 1), 0:T[g]]), g)
                        dve.tensor_tensor(y, lin(p, g), y, ALU.add).then_inc(S(f"free_d{p}"), 1)
                        add_square(mp, n, p, g, z)
                    if first is not None:
                        top_round(big, first + i)

            def post(g, s):
                ph = (phase("out", g), phase("dn", g, 0, 1), phase("oo", g), phase("dn", g, 1, 1))[s]
                r = r_at(g, SPOST[s])
                diagonals(r, g)
                dve.wait_ge(S("n_b"), r + 1)
                for p in (0, 1):
                    dve.wait_ge(S(f"free_{ph.free[p]}{p}"), ph.end[ph.free[p], p])
                base, layer = ((G_MIX_POST, 0), (G_FFN_POST, 0), (G_MIX_POST, 1), (G_FFN_POST, 1))[s]
                q = 8 * (4 * g + s)
                if g and s == 0:
                    dve.wait_ge(S("xb_in"), 16)

                def scale(n):
                    if n >= 2:
                        dve.wait_ge(S("x_new"), q + n - 1)
                    dve.tensor_tensor(TT[:, n % 2, 0:T[g]], Y[:, n, 0:T[g]], spread(g), ALU.mult).then_inc(S("x_t"), 1)

                scale(0)
                for n in range(NB):
                    dve.wait_ge(S("x_t"), q + n + 1)
                    dve.scalar_tensor_tensor(out=X[:, n, 0:T[g]], in0=TT[:, n % 2, 0:T[g]], scalar=gain(base, layer, n),
                                             in1=X[:, n, 0:T[g]], op0=ALU.mult, op1=ALU.add).then_inc(S("x_new"), 1)
                    if n + 1 < NB:
                        scale(n + 1)
                    if s < 3:
                        if n:
                            add_block("sq_m", "ss_m", 8 * (3 * g + s), n - 1, g)
                if s == 3:
                    return
                add_block("sq_m", "ss_m", 8 * (3 * g + s), NB - 1, g)
                diagonals(r_at(g, SPRE[s]), g)

            def gate(g):
                ph = phase("v", g)
                z = z_at(g, 2)
                sum_zero(z)
                dve.wait_ge(S("rb"), 3 * g + 2)

                def body(i):
                    for p in (0, 1):
                        wait(dve, S("w_used"), ph.c0 + 2 * i + p + 1)
                        v = flat(Y[:, ds(2 * i + p, 1), 0:T[g]])
                        dve.tensor_tensor(hv(v, g), lin(p, g), hv(RB[:, 0:T[g]], g), ALU.mult).then_inc(S(f"free_d{p}"), 1)
                    for p in (0, 1):
                        n = 2 * i + p
                        wait(dve, S("v_gelu"), 8 * g + n + 1)
                        wait(dve, S("lv"), 8 * g + n + 1)
                        dve.wait_ge(S("ss_zero"), z + 1)
                        dve.tensor_tensor(SS[:, 0:T[g]], SS[:, 0:T[g]], flat(Y[:, ds(n, 1), 0:T[g]]), ALU.add).then_inc(S("lv"), 1)

                with dve.Fori(0, 2) as i:
                    body(i)
                    if g == 0:
                        top_round(big, BIG0 + 30 + i)
                dve.wait_ge(S("ws_in"), 16 * 10 * (g + 1))
                tril = TRIL.unsqueeze(1).to_broadcast([P, 8, P])
                dve.tensor_tensor(WS[:], WS[:], tril, ALU.mult).then_inc(S("ws_m"), 1)
                tril8 = TRIL[0:NS, 0:NS].unsqueeze(1).to_broadcast([NS, 8, NS])
                dve.tensor_tensor(WS8[:], WS8[:], tril8, ALU.mult).then_inc(S("ws_m"), 1)
                with dve.Fori(2, 4) as i:
                    body(i)
                ph = phase("u", g)
                for local in range(8):
                    p = local % 2
                    dve.wait_ge(S("w_used"), ph.c0 + local + 1)
                    dve.tensor_tensor(hv(U[:, local, 0:T[g]], g), lin(p, g), hv(RB[:, 0:T[g]], g), ALU.mult).then_inc(S(f"free_d{p}"), 1)
                    if local == 1:
                        dve.wait_ge(S("mean"), g + 1)
                    if 1 <= local <= 3:
                        for n in range(3 * local - 3, min(3 * local, NB)):
                            dve.scalar_tensor_tensor(out=hv(Y[:, n, 0:T[g]], g), in0=aux(0, g), scalar=-1.0 / D, in1=hv(Y[:, n, 0:T[g]], g),
                                                     op0=ALU.mult, op1=ALU.add).then_inc(S("ln_c"), 1)
                    if 2 <= local <= 3:
                        for n in range(5 * local - 10, 3 * local - 1 if local < 3 else NB):
                            add_block("ln_sq", "ln_ss", 8 * g, n, g)
                    if local == 4:
                        diagonals(r_at(g, 4), g)
                    if local == 6:
                        dve.wait_ge(S("n_b"), r_at(g, 4) + 1)
                    if local >= 6:
                        for n in range(4 * local - 24, 4 * local - 20):
                            wait(dve, S("ln_z"), 8 * g + n - 1)
                            dve.wait_ge(S("ln_c"), 8 * g + n + 1)
                            dve.tensor_tensor(TT[:, n % 2, 0:T[g]], Y[:, n, 0:T[g]], spread(g), ALU.mult).then_inc(S("ln_t"), 1)
                a = a_at_(g, 2)

                def rows(n):
                    if n % 2:
                        return
                    dve.wait_ge(S("z_ps"), 8 * g + n + 1)
                    base = (4 + 2 * (1 - n % 2)) * 512
                    ins_ = dve.tensor_copy(ZN[:, 0:4, P * n:P * n + P], PSF[:, base:base + 512].rearrange("p (k d) -> p k d", d=P))
                    if g:
                        ins_ = dve.tensor_copy(ZN[0:NS, 4, P * n:P * n + P], PSF[0:NS, base + 512:base + 512 + P])
                    ins_.then_inc(S("zc_d"), 1)

                dve.wait_ge(S("ln_z"), 8 * g + 8)
                dve.wait_ge(S("u_gelu"), 8 * g + 8)
                rows(0)
                for n in range(NB):
                    if n + 2 < NB:
                        rows(n + 2)
                    dve.wait_ge(S("s_mm"), 8 * g + n + 1)
                    bias = BS[:, n:n + 1, :].to_broadcast([P, 4, P])
                    ins_ = dve.tensor_tensor(SQ[:, n % 2, 0:512].rearrange("p (k t) -> p k t", t=P),
                                             PS[:, 2 * (n % 2), :].rearrange("p (k t) -> p k t", t=P), bias, ALU.add)
                    if g:
                        bias8 = BS[:, n:n + 1, 0:DT].to_broadcast([P, DB, DT])
                        ins_ = dve.tensor_tensor(SQ[:, n % 2, 512:T[1]].rearrange("p (b t) -> p b t", b=DB),
                                                 PS[:, 2 * (n % 2) + 1, 0:NS].rearrange("p (b t) -> p b t", b=DB), bias8, ALU.add)
                    ins_.then_inc(S("s_b"), 1)
                    dve.wait_ge(S("s_b"), 8 * g + n + 1)
                    wait(dve, S("a_lo"), 8 * a + n - 1)
                    dve.tensor_tensor(TT[:, n % 2, 0:T[g]], SQ[:, n % 2, 0:T[g]], U[:, n, 0:T[g]], ALU.mult).then_inc(S("a_t"), 1)

            for k, name in enumerate(("free_d0", "free_d1", "h_lo", "lv")):
                dve.memset(T16[:, k:k + 1], 0.0).then_inc(S(name), 1)
            dve.wait_ge(S("c_in"), 16)
            dve.tensor_copy(IDB[:], IDENT).then_inc(S("setup_d"), 1)
            dve.tensor_scalar(MCB[:], TRIL, 1.0, -MASK, ALU.subtract, ALU.mult).then_inc(S("setup_d"), 1)
            dve.memset(RT[:], 1.0).then_inc(S("setup_d"), 1)
            dve.memset(XPE[:, :, 0:BUF], 0.0).then_inc(S("halo"), 1)
            dve.wait_ge(S("setup_d"), 3)
            dve.wait_ge(S("setup_a"), 1)
            load_x(0)
            dve.wait_ge(S("s_in"), 32)
            dve.tensor_copy(EB[:].rearrange("p b c -> p (b c)"), EM[0:NS, :]).then_inc(S("setup_d"), 1)
            dve.wait_ge(S("setup_d"), 4)
            dve.wait_ge(S("setup_pe"), 5)
            in_stage(0)
            index(0)
            load_x(1)
            in_stage(1)
            index(1)
            dve.memset(IQZ[:], 0.0).then_inc(S("iqz0"), 1)
            index_sample()
            for g in range(2):
                attend(g)
                if g:
                    attend_sample()
                if g == 0:
                    def sample_rounds(i, p):
                        for q in range(2):
                            top_round([(4, SCS)], 32 + 4 * i + 2 * p + q)
                    out_like(phase("out", 0), 0, 0, sample_rounds)
                    dve.wait_ge(S("top"), 2 * 48)
                    dve.max(M8[0:NS, 4, :], SCS).then_inc(S("top"), 1)
                    dve.wait_ge(S("top"), 2 * 48 + 1)
                    dve.memset(M8[0:NS, 4, TOPK_S % 8:8], DUMMY).then_inc(S("m8_cut"), 1)
                    dve.wait_ge(S("m8_cut"), 1)
                    dve.match_replace(out=SCS, in_to_replace=M8[0:NS, 4, :], in_values=SCS, imm_value=CHOSEN).then_inc(S("top"), 1)
                else:
                    out_like(phase("out", 1), 1, 0)
                post(g, 0)
                at = BIG0
                for layer in range(2):
                    for half in range(2):
                        run = g == 0 and layer == 0
                        gate_up(phase("gu", g, layer, half), at if run else None)
                        at += FH
                        down(phase("dn", g, layer, half), 1 + 2 * layer, at if run else None)
                        at += 4
                    if layer == 0:
                        post(g, 1)
                        gate(g)
                        out_like(phase("oo", g), g, 2)
                        post(g, 2)
                    else:
                        post(g, 3)


_INS = ["x_prompt", "x_sample", "cache_k", "cache_v", "cache_idx_k", "state_pool", "page_table",
        "norm_mix_pre", "norm_mix_post", "norm_ffn_pre", "norm_ffn_post", "w_in_even", "w_out_even",
        "w_pool_group", "pool_scale", "w_in_odd", "sgu_norm_g", "sgu_norm_b", "w_spatial", "b_spatial",
        "w_out_odd", "w_ffn_gate_up", "w_ffn_down"]
_OUTS = [("y_prompt", (1, SEQ, D)), ("y_sample", (DB, DT, D)),
         ("new_k_prompt", (1, 1, SEQ, 2, HD)), ("new_v_prompt", (1, 1, SEQ, 2, HD)),
         ("new_idx_k_prompt", (1, 1, SEQ, HD)), ("new_pool_prompt", (1, 1, BUF, 512)),
         ("new_k_sample", (1, DB, DT, 2, HD)), ("new_v_sample", (1, DB, DT, 2, HD)),
         ("new_idx_k_sample", (1, DB, DT, HD)), ("new_pool_sample", (1, DB, BUF, 512)),
         ("new_sgu_v_sample", (1, DB, DT, D))]


def kernel(**inputs):
    import concourse.bacc as _bacc
    from concourse.bass_utils import run_bass_kernel_spmd as _run

    nc = _bacc.Bacc("TRN2", target_bir_lowering=False, num_devices=1)
    arrays, ins, outs = {}, {}, {}
    table, rope = constants()
    given = {name: np.ascontiguousarray(inputs[name]) for name in _INS}
    given["constants"], given["rope"] = table, rope
    for name, a in given.items():
        arrays[f"in_{name}"] = a
        ins[name] = nc.dram_tensor(f"in_{name}", a.shape, mybir.dt.from_np(a.dtype), kind="ExternalInput").ap()
    for name, shape in _OUTS:
        outs[name] = nc.dram_tensor(f"out_{name}", shape, F32, kind="ExternalOutput").ap()
    build_kernel(nc, ins, outs)
    r = _run(nc, [arrays], core_ids=[0])
    return tuple(r.results[0][f"out_{name}"] for name, _ in _OUTS)
```
